# Optimizing a Trainium2 kernel written in Bass

```python
import math
import jax, jax.numpy as jnp
from jax import lax
import numpy as np

D_MODEL = 1024
BATCH = 1
SEQ = 256
DEPTH = 2

GRID_W = 64
CTX_LEN = 256
N_MIXERS = 2
MIXER_ATTN = 0
MIXER_POOL = 1
N_HEADS = 8
HEAD_DIM = 64
V_DIM = 2 * HEAD_DIM
QK_WIDTH = N_HEADS * 2 * HEAD_DIM
V_WIDTH = N_HEADS * V_DIM
ROPE_BASE = 10000.0
ROPE_PAIRS_PER_AXIS = HEAD_DIM // 4
POOL_WINDOWS = (2, 4, 8, 16)
N_POOL_GROUPS = len(POOL_WINDOWS)
POOL_GROUP = D_MODEL // N_POOL_GROUPS
D_FF = -(-8 * D_MODEL // (3 * 256)) * 256
Q_BLOCK = 128
ALPHA = (2.0 * DEPTH) ** 0.25
BETA = (8.0 * DEPTH) ** -0.25
LN_EPS = 1e-5
N_MOD = 6
N_ATTN_LAYERS = (DEPTH + 1) // 2
N_POOL_LAYERS = DEPTH // 2


def layer_norm(x, g, b):
    xf = x.astype(jnp.float32)
    mu = jnp.mean(xf, axis=-1, keepdims=True)
    var = jnp.mean(jnp.square(xf - mu), axis=-1, keepdims=True)
    return ((xf - mu) * lax.rsqrt(var + LN_EPS) * g + b).astype(x.dtype)

def adaln_params(cond, w_mod, b_mod):
    m = jax.nn.silu(cond) @ w_mod + b_mod
    return jnp.split(m, N_MOD, axis=-1)

def modulate(h, shift, scale):
    return h * (1 + scale) + shift

def axial_rope_tables(rows, dtype):
    row = jnp.repeat(jnp.arange(rows, dtype=jnp.float32), GRID_W)
    col = jnp.tile(jnp.arange(GRID_W, dtype=jnp.float32), rows)
    inv = jnp.power(ROPE_BASE, -jnp.arange(ROPE_PAIRS_PER_AXIS, dtype=jnp.float32) / ROPE_PAIRS_PER_AXIS)
    ang = jnp.concatenate([row[:, None] * inv, col[:, None] * inv], axis=-1)
    cos = jnp.cos(ang)[:, None, None, :].astype(dtype)
    sin = jnp.sin(ang)[:, None, None, :].astype(dtype)
    return cos, sin

def apply_rope(x, cos, sin):
    half = HEAD_DIM // 2
    x1, x2 = x[..., :half], x[..., half:]
    return jnp.concatenate([x1 * cos - x2 * sin, x1 * sin + x2 * cos], axis=-1)

def project_q(h, w_qkv):
    B, S = h.shape[:2]
    return (h @ w_qkv[:, :QK_WIDTH]).reshape(B, S, N_HEADS, 2, HEAD_DIM)

def project_kv(h, w_qkv):
    B, S = h.shape[:2]
    kv = h @ w_qkv[:, QK_WIDTH:]
    k = kv[..., :QK_WIDTH].reshape(B, S, N_HEADS, 2, HEAD_DIM)
    v = kv[..., QK_WIDTH:].reshape(B, S, N_HEADS, V_DIM)
    return k, v

def diff_softmax_mix(q, k, v, lam):
    s = jnp.einsum('bqhmd,bkhmd->bhmqk', q * (HEAD_DIM ** -0.5), k).astype(jnp.float32)
    p = jax.nn.softmax(s, axis=-1)
    a = p[:, :, 0] - lam * p[:, :, 1]
    return jnp.einsum('bhqk,bkhe->bqhe', a.astype(v.dtype), v)

def diff_head_out(o, subln_g, lam_init, w_o):
    B, Q = o.shape[:2]
    of = o.astype(jnp.float32)
    of = of * lax.rsqrt(jnp.mean(of * of, axis=-1, keepdims=True) + LN_EPS) * subln_g * (1.0 - lam_init)
    return of.astype(o.dtype).reshape(B, Q, V_WIDTH) @ w_o

def latent_diff_attention(q_l, k_all, v_all, lam):
    B, S = q_l.shape[:2]
    n_blk = S // Q_BLOCK
    qb = jnp.moveaxis(q_l.reshape(B, n_blk, Q_BLOCK, N_HEADS, 2, HEAD_DIM), 1, 0)
    ob = lax.map(lambda q: diff_softmax_mix(q, k_all, v_all, lam), qb)
    return jnp.moveaxis(ob, 0, 1).reshape(B, S, N_HEADS, V_DIM)

def multiscale_pool(h, w_pool, pool_scale):
    B, S, D = h.shape
    hf = h.astype(jnp.float32)
    cs = jnp.concatenate([jnp.zeros((B, 1, D), jnp.float32), lax.cumsum(hf, axis=1)], axis=1)
    t = jnp.arange(S)
    outs = []
    for g, w in enumerate(POOL_WINDOWS):
        lo = jnp.clip(t - w // 2, 0, S)
        hi = jnp.clip(t + w - w // 2, 0, S)
        cg = cs[..., g * POOL_GROUP:(g + 1) * POOL_GROUP]
        mean = (cg[:, hi] - cg[:, lo]) / (hi - lo).astype(jnp.float32)[None, :, None]
        outs.append(mean - hf[..., g * POOL_GROUP:(g + 1) * POOL_GROUP])
    pooled = jnp.stack(outs, axis=2).astype(h.dtype)
    y = jnp.einsum('bsgi,gio->bsgo', pooled, w_pool).reshape(B, S, D)
    return y * pool_scale

def swiglu(h, w_in, w_out):
    g, u = jnp.split(h @ w_in, 2, axis=-1)
    return (jax.nn.silu(g) * u) @ w_out

def reads_context(layer):
    return (layer % N_MIXERS) == MIXER_ATTN

def first_inputs(seed: int = 0) -> dict:
    key = jax.random.key(seed)
    ks = jax.random.split(key, 16)
    D = D_MODEL
    f32 = jnp.float32
    return {
        "x": jax.random.normal(ks[0], (BATCH, SEQ, D), f32),
        "c": jax.random.normal(ks[1], (BATCH, D), f32),
        "ctx": jax.random.normal(ks[2], (BATCH, CTX_LEN, D), f32),
        "c_ctx": jax.random.normal(ks[3], (D,), f32),
        "w_mod": jax.random.normal(ks[4], (DEPTH, D, N_MOD * D), f32) * (0.5 * D ** -0.5),
        "b_mod": jax.random.normal(ks[5], (DEPTH, N_MOD * D), f32) * 0.01,
        "ln_g": 1.0 + 0.02 * jax.random.normal(ks[6], (DEPTH, 2, D), f32),
        "ln_b": 0.02 * jax.random.normal(ks[7], (DEPTH, 2, D), f32),
        "attn_w_qkv": jax.random.normal(ks[8], (N_ATTN_LAYERS, D, QK_WIDTH + QK_WIDTH + V_WIDTH), f32) * D ** -0.5,
        "attn_lambda": 0.1 * jax.random.normal(ks[9], (N_ATTN_LAYERS, 4, HEAD_DIM), f32),
        "attn_subln_g": 1.0 + 0.02 * jax.random.normal(ks[10], (N_ATTN_LAYERS, V_DIM), f32),
        "attn_w_o": jax.random.normal(ks[11], (N_ATTN_LAYERS, V_WIDTH, D), f32) * (V_WIDTH ** -0.5 * BETA),
        "pool_w": jax.random.normal(ks[12], (N_POOL_LAYERS, N_POOL_GROUPS, POOL_GROUP, POOL_GROUP), f32) * (POOL_GROUP ** -0.5 * BETA),
        "pool_scale": 0.5 + 0.05 * jax.random.normal(ks[13], (N_POOL_LAYERS, D), f32),
        "ffn_w_in": jax.random.normal(ks[14], (DEPTH, D, 2 * D_FF), f32) * D ** -0.5,
        "ffn_w_out": jax.random.normal(ks[15], (DEPTH, D_FF, D), f32) * (D_FF ** -0.5 * BETA),
    }

def first_block(x, c, ctx, c_ctx, w_mod, b_mod, ln_g, ln_b, attn_w_qkv, attn_lambda, attn_subln_g,
              attn_w_o, pool_w, pool_scale, ffn_w_in, ffn_w_out):
    n_lat = x.shape[1]
    rows = n_lat // GRID_W
    cos, sin = axial_rope_tables(rows, x.dtype)
    h_ctx = ctx
    for i in range(DEPTH):
        mixer = i % N_MIXERS
        ctx_later = any(reads_context(j) for j in range(i + 1, DEPTH))
        sh1, sc1, g1, sh2, sc2, g2 = adaln_params(c[:, None, :], w_mod[i], b_mod[i])
        csh1, csc1, cg1, csh2, csc2, cg2 = adaln_params(c_ctx, w_mod[i], b_mod[i])
        hx = modulate(x, sh1, sc1)
        hc = modulate(h_ctx, csh1, csc1)
        if mixer == MIXER_ATTN:
            a = i // N_MIXERS
            lam_init = 0.8 - 0.6 * math.exp(-0.3 * i)
            lp = attn_lambda[a].astype(jnp.float32)
            lam = jnp.exp(jnp.sum(lp[0] * lp[1])) - jnp.exp(jnp.sum(lp[2] * lp[3])) + lam_init
            w_qkv = attn_w_qkv[a]
            k_c, v_c = project_kv(hc, w_qkv)
            q_l = apply_rope(project_q(hx, w_qkv), cos, sin)
            k_l, v_l = project_kv(hx, w_qkv)
            k_l = apply_rope(k_l, cos, sin)
            k_all = jnp.concatenate([k_c, k_l], axis=1)
            v_all = jnp.concatenate([v_c, v_l], axis=1)
            y_lat = diff_head_out(latent_diff_attention(q_l, k_all, v_all, lam),
                                  attn_subln_g[a], lam_init, attn_w_o[a])
            if ctx_later:
                q_c = project_q(hc, w_qkv)
                y_ctx = diff_head_out(diff_softmax_mix(q_c, k_c, v_c, lam),
                                      attn_subln_g[a], lam_init, attn_w_o[a])
        else:
            p = i // N_MIXERS
            y_lat = multiscale_pool(hx, pool_w[p], pool_scale[p])
            if ctx_later:
                y_ctx = multiscale_pool(hc, pool_w[p], pool_scale[p])
        x = layer_norm(ALPHA * x + g1 * y_lat, ln_g[i, 0], ln_b[i, 0])
        x = layer_norm(ALPHA * x + g2 * swiglu(modulate(x, sh2, sc2), ffn_w_in[i], ffn_w_out[i]),
                       ln_g[i, 1], ln_b[i, 1])
        if ctx_later:
            h_ctx = layer_norm(ALPHA * h_ctx + cg1 * y_ctx, ln_g[i, 0], ln_b[i, 0])
            h_ctx = layer_norm(ALPHA * h_ctx + cg2 * swiglu(modulate(h_ctx, csh2, csc2), ffn_w_in[i], ffn_w_out[i]),
                               ln_g[i, 1], ln_b[i, 1])
    return x


DEPTH_2 = 1

PLE_DIM = 256
GLA_HEADS = 4
GLA_DK = D_MODEL // 8
GLA_DV = D_MODEL // 4
GLA_GATE_RANK = 16
GLA_GATE_TAU = 16.0
GLA_CHUNK = 64
MOBA_HEADS = 8
MOBA_DH = D_MODEL // 8
MOBA_BLOCK = 256
MOBA_TOPK = 3
MOBA_QCHUNK = 32
D_FF_2 = 4 * D_MODEL
EPS = 1e-6

IN_SPLITS = (
    GLA_HEADS * GLA_DK,
    GLA_HEADS * GLA_DK,
    GLA_HEADS * GLA_DV,
    GLA_GATE_RANK,
    GLA_HEADS * GLA_DV,
    MOBA_HEADS * MOBA_DH,
    MOBA_HEADS * MOBA_DH,
    MOBA_HEADS * MOBA_DH,
    D_MODEL,
    D_MODEL,
)
N_IN = sum(IN_SPLITS)


def rms_norm(x, g):
    xf = x.astype(jnp.float32)
    y = xf * lax.rsqrt(jnp.mean(xf * xf, axis=-1, keepdims=True) + EPS)
    return (y * g.astype(jnp.float32)).astype(x.dtype)

def gla_chunked(q, k, v, log_a):
    B, S, H, dk = q.shape
    dv = v.shape[-1]
    n = S // GLA_CHUNK

    def chunk(t):
        return t.astype(jnp.float32).reshape(B, n, GLA_CHUNK, H, t.shape[-1]).transpose(0, 3, 1, 2, 4)

    q, k, v, log_a = chunk(q), chunk(k), chunk(v), chunk(log_a)
    b = jnp.cumsum(log_a, axis=3)
    b_last = b[:, :, :, -1:, :]
    qd = q * jnp.exp(b) * (dk ** -0.5)
    kd = k * jnp.exp(-b)
    kl = k * jnp.exp(b_last - b)
    kv = jnp.einsum('bhncd,bhnce->bhnde', kl, v)
    decay = jnp.exp(b_last[:, :, :, 0, :])

    def step(state, inp):
        dec, kv_n = inp
        return dec[..., None] * state + kv_n, state

    s0 = jnp.zeros((B, H, dk, dv), jnp.float32)
    _, s_prev = lax.scan(step, s0, (jnp.moveaxis(decay, 2, 0), jnp.moveaxis(kv, 2, 0)))
    s_prev = jnp.moveaxis(s_prev, 0, 2)
    o_inter = jnp.einsum('bhncd,bhnde->bhnce', qd, s_prev)
    causal = jnp.tril(jnp.ones((GLA_CHUNK, GLA_CHUNK), bool))
    a = jnp.where(causal, jnp.einsum('bhncd,bhnsd->bhncs', qd, kd), 0.0)
    o = o_inter + jnp.einsum('bhncs,bhnse->bhnce', a, v)
    return o.transpose(0, 2, 3, 1, 4).reshape(B, S, H, dv)

def moba_attention(q, k, v):
    B, S, H, dh = q.shape
    s_pad = -(-S // MOBA_BLOCK) * MOBA_BLOCK
    nb = s_pad // MOBA_BLOCK
    n_sel = min(MOBA_TOPK, max(nb - 1, 1))
    nq = s_pad // MOBA_QCHUNK
    pad = ((0, 0), (0, s_pad - S), (0, 0), (0, 0))
    q, k, v = [jnp.pad(t, pad).transpose(0, 2, 1, 3) for t in (q, k, v)]
    kb = k.reshape(B, H, nb, MOBA_BLOCK, dh)
    vb = v.reshape(B, H, nb, MOBA_BLOCK, dh)
    scale = dh ** -0.5
    slopes = 2.0 ** (-8.0 * jnp.arange(1, H + 1, dtype=jnp.float32) / H)

    k_mean = jnp.mean(kb.astype(jnp.float32), axis=3)
    gate = jnp.einsum('bhsd,bhnd->bhsn', q.astype(jnp.float32), k_mean)
    pos = jnp.arange(s_pad)
    fully_past = jnp.arange(nb)[None, :] < (pos // MOBA_BLOCK)[:, None]
    gate = jnp.where(fully_past, gate, -jnp.inf)
    top_val, top_idx = lax.top_k(gate, n_sel)
    valid = jnp.isfinite(top_val)

    def to_chunks(t):
        return jnp.moveaxis(t.reshape(B, H, nq, MOBA_QCHUNK, *t.shape[3:]), 2, 0)

    b_ix = jnp.arange(B)[:, None, None, None]
    h_ix = jnp.arange(H)[None, :, None, None]

    def attend(args):
        q_c, idx_c, valid_c, c = args
        t = c * MOBA_QCHUNK + jnp.arange(MOBA_QCHUNK)
        blk = (c * MOBA_QCHUNK) // MOBA_BLOCK
        k_own = lax.dynamic_index_in_dim(kb, blk, axis=2, keepdims=False)
        v_own = lax.dynamic_index_in_dim(vb, blk, axis=2, keepdims=False)
        own_pos = blk * MOBA_BLOCK + jnp.arange(MOBA_BLOCK)
        d_own = (t[:, None] - own_pos[None, :]).astype(jnp.float32)
        sc_own = (jnp.einsum('bhqd,bhkd->bhqk', q_c, k_own).astype(jnp.float32) * scale
                  - slopes[:, None, None] * jnp.abs(d_own))
        sc_own = jnp.where(d_own >= 0, sc_own, -jnp.inf)
        k_sel = kb[b_ix, h_ix, idx_c]
        v_sel = vb[b_ix, h_ix, idx_c]
        sel_pos = idx_c[..., None] * MOBA_BLOCK + jnp.arange(MOBA_BLOCK)
        d_sel = (t[:, None, None] - sel_pos).astype(jnp.float32)
        sc_sel = (jnp.einsum('bhqd,bhqnkd->bhqnk', q_c, k_sel).astype(jnp.float32) * scale
                  - slopes[:, None, None, None] * jnp.abs(d_sel))
        sc_sel = jnp.where(valid_c[..., None], sc_sel, -jnp.inf)
        scores = jnp.concatenate(
            [sc_own, sc_sel.reshape(B, H, MOBA_QCHUNK, n_sel * MOBA_BLOCK)], axis=-1)
        prob = jax.nn.softmax(scores, axis=-1).astype(v.dtype)
        p_own = prob[..., :MOBA_BLOCK]
        p_sel = prob[..., MOBA_BLOCK:].reshape(B, H, MOBA_QCHUNK, n_sel, MOBA_BLOCK)
        return (jnp.einsum('bhqk,bhkd->bhqd', p_own, v_own)
                + jnp.einsum('bhqnk,bhqnkd->bhqd', p_sel, v_sel))

    out = lax.map(attend, (to_chunks(q), to_chunks(top_idx), to_chunks(valid), jnp.arange(nq)))
    out = jnp.moveaxis(out, 0, 2).reshape(B, H, s_pad, dh)[:, :, :S]
    return out.transpose(0, 2, 1, 3).reshape(B, S, H * dh)

def second_inputs(seed: int = 0) -> dict:
    key = jax.random.key(seed)
    ks = jax.random.split(key, 20)

    def nrm(k, shape, fan_in, scale=1.0):
        return jax.random.normal(k, shape, jnp.float32) * (scale * fan_in ** -0.5)

    def gain(k, shape):
        return 1.0 + 0.05 * jax.random.normal(k, shape, jnp.float32)

    return {
        'x': jax.random.normal(ks[0], (BATCH, SEQ, D_MODEL), jnp.float32),
        'p': jax.random.normal(ks[1], (DEPTH_2, BATCH, SEQ, PLE_DIM), jnp.float32),
        'norm_mix': gain(ks[2], (DEPTH_2, D_MODEL)),
        'w_in': nrm(ks[3], (DEPTH_2, D_MODEL, N_IN), D_MODEL),
        'gla_gate_w2': nrm(ks[4], (DEPTH_2, GLA_GATE_RANK, GLA_HEADS * GLA_DK), GLA_GATE_RANK),
        'gla_gate_b': 0.1 * jax.random.normal(ks[5], (DEPTH_2, GLA_HEADS * GLA_DK), jnp.float32),
        'gla_out_norm': gain(ks[6], (DEPTH_2, GLA_HEADS, GLA_DV)),
        'moba_q_norm': gain(ks[7], (DEPTH_2, MOBA_DH)),
        'moba_k_norm': gain(ks[8], (DEPTH_2, MOBA_DH)),
        'w_branch_a': nrm(ks[9], (DEPTH_2, GLA_HEADS * GLA_DV, D_MODEL), GLA_HEADS * GLA_DV),
        'w_branch_b': nrm(ks[10], (DEPTH_2, MOBA_HEADS * MOBA_DH, D_MODEL), MOBA_HEADS * MOBA_DH),
        'w_out': nrm(ks[11], (DEPTH_2, D_MODEL, D_MODEL), D_MODEL, 0.5),
        'norm_mlp': gain(ks[12], (DEPTH_2, D_MODEL)),
        'w_up': nrm(ks[13], (DEPTH_2, D_MODEL, D_FF_2), D_MODEL),
        'w_down': nrm(ks[14], (DEPTH_2, D_FF_2, D_MODEL), D_FF_2, 0.5),
        'norm_ple': gain(ks[15], (DEPTH_2, D_MODEL)),
        'w_ple_gate': nrm(ks[16], (DEPTH_2, D_MODEL, D_MODEL), D_MODEL),
        'w_ple': nrm(ks[17], (DEPTH_2, PLE_DIM, D_MODEL), PLE_DIM, 0.5),
    }

def second_block(x, p, norm_mix, w_in, gla_gate_w2, gla_gate_b, gla_out_norm, moba_q_norm,
              moba_k_norm, w_branch_a, w_branch_b, w_out, norm_mlp, w_up, w_down,
              norm_ple, w_ple_gate, w_ple):
    B, S, _ = x.shape
    points = []
    acc = 0
    for sz in IN_SPLITS[:-1]:
        acc += sz
        points.append(acc)

    for i in range(DEPTH_2):
        h = rms_norm(x, norm_mix[i])
        u = h @ w_in[i]
        (gq, gk, gv, g_lr, g_r, mq, mk, mv, gate_a, gate_b) = jnp.split(u, points, axis=-1)

        z = (g_lr @ gla_gate_w2[i] + gla_gate_b[i]).astype(jnp.float32)
        log_a = jax.nn.log_sigmoid(z) / GLA_GATE_TAU
        o_a = gla_chunked(gq.reshape(B, S, GLA_HEADS, GLA_DK),
                          gk.reshape(B, S, GLA_HEADS, GLA_DK),
                          gv.reshape(B, S, GLA_HEADS, GLA_DV),
                          log_a.reshape(B, S, GLA_HEADS, GLA_DK)).astype(x.dtype)
        o_a = rms_norm(o_a, gla_out_norm[i]).reshape(B, S, GLA_HEADS * GLA_DV) * jax.nn.silu(g_r)
        y_a = o_a @ w_branch_a[i]

        qh = rms_norm(mq.reshape(B, S, MOBA_HEADS, MOBA_DH), moba_q_norm[i])
        kh = rms_norm(mk.reshape(B, S, MOBA_HEADS, MOBA_DH), moba_k_norm[i])
        vh = mv.reshape(B, S, MOBA_HEADS, MOBA_DH)
        y_b = moba_attention(qh, kh, vh) @ w_branch_b[i]

        y = jax.nn.sigmoid(gate_a) * y_a + jax.nn.sigmoid(gate_b) * y_b
        x = x + y @ w_out[i]

        h2 = rms_norm(x, norm_mlp[i])
        x = x + jnp.square(jax.nn.relu(h2 @ w_up[i])) @ w_down[i]

        ple_gate = jax.nn.sigmoid(rms_norm(x, norm_ple[i]) @ w_ple_gate[i])
        x = x + ple_gate * (p[i] @ w_ple[i])
    return x


def setup_inputs(seed=0):
    out = dict(first_inputs(seed))
    for name, value in second_inputs(seed + 1).items():
        if name != "x":
            out[name + "_2"] = value
    return out


def reference(
    x, c, ctx, c_ctx, w_mod, b_mod, ln_g, ln_b, attn_w_qkv, attn_lambda, attn_subln_g, attn_w_o,
    pool_w, pool_scale, ffn_w_in, ffn_w_out, p_2, norm_mix_2, w_in_2, gla_gate_w2_2,
    gla_gate_b_2, gla_out_norm_2, moba_q_norm_2, moba_k_norm_2, w_branch_a_2, w_branch_b_2,
    w_out_2, norm_mlp_2, w_up_2, w_down_2, norm_ple_2, w_ple_gate_2, w_ple_2,
):
    x = first_block(
        x, c, ctx, c_ctx, w_mod, b_mod, ln_g, ln_b, attn_w_qkv, attn_lambda, attn_subln_g,
        attn_w_o, pool_w, pool_scale, ffn_w_in, ffn_w_out,
    )
    return second_block(
        x, p_2, norm_mix_2, w_in_2, gla_gate_w2_2, gla_gate_b_2, gla_out_norm_2, moba_q_norm_2,
        moba_k_norm_2, w_branch_a_2, w_branch_b_2, w_out_2, norm_mlp_2, w_up_2, w_down_2,
        norm_ple_2, w_ple_gate_2, w_ple_2,
    )


_drawn_inputs = setup_inputs


def setup_inputs(seed=0):
    import zlib

    import numpy as np

    out = dict(_drawn_inputs(seed))
    spreads = {}
    factors = {'b_mod': 7.852,
     'attn_lambda': 8.0,
     'attn_subln_g': 8.0,
     'pool_scale': 8.0,
     'norm_mix_2': 3.105,
     'gla_gate_w2_2': 3.196,
     'gla_gate_b_2': 8.0,
     'gla_out_norm_2': 7.36,
     'moba_q_norm_2': 8.0,
     'moba_k_norm_2': 8.0,
     'norm_ple_2': 200.0,
     'norm_mlp_2': 8.0,
     'p_2': 6.368,
     'w_ple_gate_2': 8.0,
     'w_ple_2': 6.358}
    for name, (base, spread) in spreads.items():
        noise = np.random.default_rng([zlib.crc32(name.encode()), seed]).standard_normal(out[name].shape)
        drawn = base * np.exp(spread * noise) if base else spread * noise
        out[name] = __import__('jax').numpy.asarray(drawn.astype(out[name].dtype))
    for name, factor in factors.items():
        out[name] = (out[name] * factor).astype(out[name].dtype)
    return out
```

```python
import math
from contextlib import ExitStack

import numpy as np

import concourse.bass as bass
from concourse import mybir

fp32 = mybir.dt.float32
f32r = mybir.dt.float32r
ALU = mybir.AluOpType
ACT = mybir.ActivationFunctionType
AXX = mybir.AxisListType.X

P = 128
D = 1024
KT = D // P
S = 256
TT = S // P
F1 = 2816
F2 = 4096
H = 8
GH, GDK, GDV, GCH, GRANK = 4, 128, 256, 64, 16
ALPHA = 4.0 ** 0.25
LN_EPS, RMS_EPS = 1e-5, 1e-6
LAM_INIT = 0.8 - 0.6 * math.exp(0.0)
POOL_WINDOWS = (2, 4, 8, 16)
N_IN = 8208
LR0 = 2 * GH * GDK + GH * GDV
CW = 512

RAW, WS = 4, 4

SUBS = {}
_n = 0
for _name, _count in (("qkv", 24), ("wo", 8), ("in0", 44), ("out0", 22), ("pool", 2), ("in1", 44), ("out1", 22),
                      ("win", 64), ("bra", 8), ("brb", 8), ("wo2", 8), ("up", 32), ("down", 32), ("pg", 8),
                      ("ple", 2)):
    SUBS[_name] = _n
    _n += _count
NSUB = _n

UNITS = {}
_n = 0
for _name, _count in (("q", 2), ("k", 4), ("v", 4), ("att", 16), ("wo", 2), ("in0", 11), ("out0", 2), ("pool", 2),
                      ("in1", 11), ("out1", 2), ("win", 16), ("z", 1), ("cum", 2), ("gqT", 2), ("go", 2),
                      ("bra", 2), ("brb", 2), ("wo2", 2), ("up", 8), ("down", 2), ("pg", 2), ("ple", 2)):
    UNITS[_name] = _n
    _n += _count

GROUPS = {}
_n = 0
for _name, _count in (("ctx", 4), ("x", 4), ("q", 4), ("k", 8), ("att", 16), ("o", 4), ("x1", 4), ("in0", 11),
                      ("pool", 4), ("x3", 4), ("in1", 11), ("rms0", 4), ("glaA", 2), ("oa", 4), ("mqk", 8),
                      ("moba", 16), ("ob", 4), ("y", 4), ("rms1", 4), ("up", 16), ("rms2", 4), ("p", 1)):
    GROUPS[_name] = _n
    _n += _count

MODS = [(0, m) for m in range(12)] + [(1, m) for m in (6, 7, 8, 9)] + [(1, m) for m in (0, 1, 2, 3, 4, 5, 10, 11)]
MOD_WHICH = {0: 0, 1: 1, 3: 2, 4: 3}
NMOD0 = 4


def mod_is_column(layer, m):
    return m // 2 in (3, 4) or (layer == 0 and m // 2 < 2)


C_ID, C_SELC, C_SELB, C_COS, C_SIN, C_DIST, C_TRI, C_TRS, C_IND, C_END = np.cumsum(
    [0, 128, 2, 128, 64, 64, 512, 128, 128, 2]).tolist()


def shape_constants():
    c = np.zeros((P, C_END), np.float32)
    p = np.arange(P)
    c[:, C_ID:C_ID + P] = np.eye(P)
    for r in range(2):
        c[p % 32 == r, C_SELC + r] = 1.0
    c[p % 32 == 0, C_SELB:C_SELB + P] = 1.0
    row = np.repeat(np.arange(S // 64, dtype=np.float32), 64)
    col = np.tile(np.arange(64, dtype=np.float32), S // 64)
    inv = np.power(np.float32(10000.0), -np.arange(16, dtype=np.float32) / np.float32(16))
    ang = np.concatenate([row[:, None] * inv, col[:, None] * inv], axis=-1).astype(np.float32)
    c[:, C_COS:C_SIN] = np.cos(ang).reshape(TT, P, 32).transpose(1, 0, 2).reshape(P, 64)
    c[:, C_SIN:C_DIST] = np.sin(ang).reshape(TT, P, 32).transpose(1, 0, 2).reshape(P, 64)
    q = np.arange(S)[:, None]
    k = np.arange(S)[None, :]
    dist = np.where(k <= q, (k - q).astype(np.float32), np.float32(-1e30))
    c[:, C_DIST:C_TRI] = dist.reshape(TT, P, S).transpose(1, 0, 2).reshape(P, TT * S)
    same = (p[:, None] // GCH) == (p[None, :] // GCH)
    c[:, C_TRI:C_TRS] = np.where(same & (p[:, None] <= p[None, :]), 1.0 / 16.0, 0.0)
    c[:, C_TRS:C_IND] = np.where(same & (p[:, None] > p[None, :]), 1.0 / 16.0, 0.0)
    for j in range(2):
        c[p // GCH == j, C_IND + j] = 1.0 / 16.0
    w = np.zeros((TT, P, 4, S), np.float32)
    t = np.arange(S)
    for g, win in enumerate(POOL_WINDOWS):
        lo = np.clip(t - win // 2, 0, S)
        hi = np.clip(t + win - win // 2, 0, S)
        m = ((t[:, None] >= lo[None, :]) & (t[:, None] < hi[None, :])).astype(np.float32)
        m = m / (hi - lo).astype(np.float32)[None, :] - np.eye(S, dtype=np.float32)
        w[:, :, g, :] = m.reshape(TT, P, S)
    return c, w.transpose(1, 0, 2, 3).reshape(P, TT * 4 * S).copy()


SUB_OF = (("q", "qkv", 4, 0), ("k", "qkv", 4, 8), ("v", "qkv", 4, 16), ("wo", "wo", 0, 4), ("in0", "in0", 4, 0),
          ("out0", "out0", 0, 18), ("pool", "pool", 0, -2), ("in1", "in1", 4, 0), ("out1", "out1", 0, 18),
          ("win", "win", 4, 0), ("bra", "bra", 0, 4), ("brb", "brb", 0, 4), ("wo2", "wo2", 0, 4), ("up", "up", 4, 0),
          ("down", "down", 0, 28), ("pg", "pg", 0, 4), ("ple", "ple", 0, -2))


def summed(stage, j=0):
    _, subs, per, off = next(e for e in SUB_OF if e[0] == stage)
    if stage in ("k", "v"):
        j //= 2
    return SUBS[subs] + off + 4 + per * j


def at_least(eng, sem, value):
    if isinstance(value, int) and value <= 0:
        return
    eng.wait_ge(sem, value)


def build(nc, a, cst_d, pool_d, out):
    ctx = ExitStack()
    with ctx:
        def sem(name):
            return ctx.enter_context(nc.semaphore(name))

        def sb(stack, name, shape, dt=fp32):
            return stack.enter_context(nc.sbuf_tensor(name, shape, dt))

        raw = sb(ctx, "raw", [P, RAW, 2048])
        wH = sb(ctx, "wH", [P, WS, 1024], f32r)
        wL = sb(ctx, "wL", [P, WS, 1024], f32r)
        aH = sb(ctx, "aH", [P, KT, S], f32r)
        aL = sb(ctx, "aL", [P, KT, S], f32r)
        x = sb(ctx, "x", [P, TT, D])
        cst = sb(ctx, "cst", [P, C_END])
        stat = sb(ctx, "stat", [P, 64])
        bn = sb(ctx, "bn", [P, TT, 12])
        mv = sb(ctx, "mv", [P, TT, 2])
        ps = ctx.enter_context(nc.psum_tensor("ps", [P, 8, 512], fp32))
        ident = cst[:, C_ID:C_ID + P]

        sA = ExitStack()
        lnp = sb(sA, "lnp", [P, 2, D])
        tf = sb(sA, "tf", [P, 2, 512])
        ro = tf
        te = tf[:, 0, :]
        modraw = sb(sA, "modraw", [P, 2, 2048])
        modrow = sb(sA, "modrow", [P, 512])
        modcol = sb(sA, "modcol", [P, 2, 4, KT, 2])
        bcol = sb(sA, "bcol", [P, 96])
        rows = sb(sA, "rows", [112, P])
        cT = sb(sA, "cT", [P, KT, 32])
        lamt = sb(sA, "lamt", [P, 256])
        lam2 = sb(sA, "lam2", [P, 8])
        subg = sb(sA, "subg", [P, P])
        g1b = sb(sA, "g1b", [P, D])
        g2b0 = sb(sA, "g2b0", [P, D])
        sAtt = ExitStack()
        v = sb(sAtt, "v", [P, 4, D])
        qz = sb(sAtt, "qz", [P, H, 2, S])
        kT = sb(sAtt, "kT", [P, H, 512])
        sPrj = ExitStack()
        cH = sb(sPrj, "cH", [P, KT, S], f32r)
        cL = sb(sPrj, "cL", [P, KT, S], f32r)
        rt = sb(sPrj, "rt", [P, 2, TT, 512])
        sPrj.close()
        sCore = ExitStack()
        ex = sb(sCore, "ex", [P, 2, 2, 512])
        am = sb(sCore, "am", [P, 2, 512])
        at = sb(sCore, "at", [P, 2, 4, P])
        ot = sb(sCore, "ot", [P, TT, D])
        sCore.close()
        sAtt.close()
        sIni = ExitStack()
        mod0 = sb(sIni, "mod0", [P, 2 * NMOD0, 2048])
        sIni.close()
        sL1 = ExitStack()
        g2b1 = sb(sL1, "g2b1", [P, D])
        sh1b = sb(sL1, "sh1b", [P, D])
        sc1b = sb(sL1, "sc1b", [P, D])
        psb = sb(sL1, "psb", [P, D])
        sF = ExitStack()
        hH = sb(sF, "hH", [P, F1 // P, S], f32r)
        hL = sb(sF, "hL", [P, F1 // P, S], f32r)
        sil = sb(sF, "sil", [P, 2, TT, 256])
        hid = sb(sF, "hid", [P, 2, TT, 256])
        sF.close()
        sP = ExitStack()
        poolm = sb(sP, "poolm", [P, TT, 4, S])
        hm = sb(sP, "hm", [P, TT, D])
        sP.close()
        sL1.close()
        sA.close()

        sB = ExitStack()
        xn = sb(sB, "xn", [P, TT, D])
        rows2 = sb(sB, "rows2", [24, P])
        gcol = sb(sB, "gcol", [P, 24])
        sM = ExitStack()
        u = sb(sM, "u", [P, TT, 8192])
        lrw = sb(sM, "lrw", [P, KT, GRANK])
        lrH = sb(sM, "lrH", [P, KT, GRANK], f32r)
        lrL = sb(sM, "lrL", [P, KT, GRANK], f32r)
        lrt = sb(sM, "lrt", [P, TT, GRANK])
        lrT = sb(sM, "lrT", [GRANK, S])
        w2 = sb(sM, "w2", [GRANK, 512])
        gbb = sb(sM, "gbb", [P, 512])
        onb = sb(sM, "onb", [P, D])
        qkg = sb(sM, "qkg", [P, 2, P])
        sG = ExitStack()
        la, lt = xn[:, :, 0:512], xn[:, :, 512:D]
        ekd = sb(sG, "ekd", [P, TT, 512])
        ekl = sb(sG, "ekl", [P, TT, 512])
        qkT = sb(sG, "qkT", [P, 2, GH, S])
        aT = ekd[:, :, :].rearrange("p t (h c) -> p t h c", h=GH)
        st = sb(sG, "st", [P, 3, GH, GDV])
        dec = sb(sG, "dec", [P, GH, TT, 2])
        sG.close()
        sQ = ExitStack()
        mT = sb(sQ, "mT", [P, 16, S])
        sc = sb(sQ, "sc", [P, 2, TT, S])
        pe_ = sb(sQ, "pe_", [P, 2, TT, S])
        pT = sb(sQ, "pT", [P, 2, 2, S])
        sQ.close()
        sM.close()
        sU = ExitStack()
        uH = sb(sU, "uH", [P, F2 // P, S], f32r)
        uL = sb(sU, "uL", [P, F2 // P, S], f32r)
        hu = sb(sU, "hu", [P, 2, TT, 512])
        sU.close()
        sE = ExitStack()
        pt = sb(sE, "pt", [P, TT, 256])
        pH = sb(sE, "pH", [P, 2, S], f32r)
        pL = sb(sE, "pL", [P, 2, S], f32r)
        gate = sb(sE, "gate", [P, TT, D])
        sE.close()
        sB.close()

        w_raw = [sem(f"w_raw{i}") for i in range(RAW)]
        w_hi, w_lo, w_used = sem("w_hi"), sem("w_lo"), sem("w_used")
        acc_done, acc_out = sem("acc_done"), sem("acc_out")
        t_done, t_f, t_hi, t_lo = sem("t_done"), sem("t_f"), sem("t_hi"), sem("t_lo")
        x_in, ctx_in, rows_in, cst_in = sem("x_in"), sem("ctx_in"), sem("rows_in"), sem("cst_in")
        small_in = sem("small_in")
        mod0_in = [sem(f"mod0_in{i}") for i in range(NMOD0)]
        mod_in = [sem(f"mod_in{i}") for i in range(2)]
        mod_used, mod_acc, mod_row, mod_sel, mod_out = (sem(n) for n in
                                                        ("mod_used", "mod_acc", "mod_row", "mod_sel", "mod_out"))
        bias0_in, bias1_in, pscale_in = sem("bias0_in"), sem("bias1_in"), sem("pscale_in")
        rows_T, cT_zero, cT_ready, qz_zero = sem("rows_T"), sem("cT_zero"), sem("cT_ready"), sem("qz_zero")
        lam_sum, lam_exp = sem("lam_sum"), sem("lam_exp")
        rot = sem("rot")
        s_max, s_exp, o_done, o_out = (sem(n) for n in ("s_max", "s_exp", "o_done", "o_out"))
        o_sq, o_sd, o_norm = sem("o_sq"), sem("o_sd"), sem("o_norm")
        ln_in, ln_var, ln_sd, ln_x = sem("ln_in"), sem("ln_var"), sem("ln_sd"), sem("ln_x")
        silu_done = sem("silu_done")
        pool_in, pool_h = sem("pool_in"), sem("pool_h")
        act_self, dve_self, pool_self = sem("act_self"), sem("dve_self"), sem("pool_self")
        rms_sq, rms_ms, rms_sd, xn_ready = sem("rms_sq"), sem("rms_ms"), sem("rms_sd"), sem("xn_ready")
        rows2_in, rows2_T, gcol_ready = sem("rows2_in"), sem("rows2_T"), sem("gcol_ready")
        lrw_in, lr_hi, lr_lo, lr_done, lr_t, lr_T, lr_Tc = (sem(n) for n in
                                                           ("lrw_in", "lr_hi", "lr_lo", "lr_done", "lr_t", "lr_T", "lr_Tc"))
        vec_in = sem("vec_in")
        z_abs, z_ln, la_ready, dec_sum, dec_exp, e_ready, g_mul = (sem(n) for n in
                                                                  ("z_abs", "z_ln", "la_ready", "dec_sum", "dec_exp", "e_ready", "g_mul"))
        a_evac, kv_done, kv_out = sem("a_evac"), sem("kv_done"), sem("kv_out")
        go_evac, go_sq, go_sd, oa_ready = sem("go_evac"), sem("go_sq"), sem("go_sd"), sem("oa_ready")
        m_sq, m_sd, m_norm = sem("m_sq"), sem("m_sd"), sem("m_norm")
        m_max, m_exp, m_o, m_oout = sem("m_max"), sem("m_exp"), sem("m_o"), sem("m_oout")
        p_in, gate_done, x_done, out_done = sem("p_in"), sem("gate_done"), sem("x_done"), sem("out_done")

        def pair(un):
            b = 2 * (un % 2)
            return ps[:, b:b + 2, :]

        def tbank(g):
            return ps[:, 4 + g % 2, :]

        block = ctx.enter_context(nc.Block())

        @block.sync
        def _(sp):
            def piece(n, i, parts):
                slot = (n // 2) % RAW
                at_least(sp, w_lo, n - 2 * RAW + 2 + 8 * i if n >= 2 * RAW or not isinstance(i, int) else 0)
                for (lo, hi), src in parts:
                    shape = src.shape
                    dst = raw[:, slot, :].rearrange("p (k c) -> p k c", k=shape[1])[:, :, lo:hi]
                    sp.dma_start(dst, src).then_inc(w_raw[slot], 32 // len(parts))

            def by_k(w):
                return w.rearrange("(k p) n -> p k n", p=P)

            def chunk(n, i, w, c0):
                for h in range(2):
                    piece(n + 4 * 0 + 2 * h, i, [((0, CW), by_k(w)[:, 4 * h:4 * h + 4, bass.ds(c0, CW)])])

            def rows_of(n, w, k0, kn):
                for k in range(k0, k0 + kn, 2):
                    piece(n + k - k0, 0, [((0, D), by_k(w)[:, k:k + 2, :])])

            sp.dma_start(x[:, :, :], a["x"].rearrange("b (t p) d -> p (b t) d", p=P)).then_inc(x_in, 16)
            for m in range(NMOD0):
                sp.dma_start(mod0[:, 2 * m:2 * m + 2, :].rearrange("p h (k c) -> p (h k) c", k=4),
                             by_k(a["w_mod"][0])[:, :, m * CW:(m + 1) * CW]).then_inc(mod0_in[m], 16)
            for c in range(6):
                chunk(SUBS["qkv"] + 4 * c, 0, a["attn_w_qkv"][0], c * CW)
            rows_of(SUBS["wo"], a["attn_w_o"][0], 0, KT)

            def swiglu_chunk(n, i, w, c0):
                for h in range(2):
                    wk = by_k(w)[:, 4 * h:4 * h + 4, :]
                    piece(n + 2 * h, i, [((256 * s, 256 * s + 256), wk[:, :, bass.ds(c0 + s * F1, 256)])
                                         for s in range(2)])

            def swiglu(layer):
                n = SUBS[f"in{layer}"]
                swiglu_chunk(n, 0, a["ffn_w_in"][layer], 0)
                with sp.Fori(0, 5) as i:
                    for j in range(2):
                        swiglu_chunk(n + 4 + 4 * j, i, a["ffn_w_in"][layer], i * 512 + (256 + 256 * j))
                rows_of(SUBS[f"out{layer}"], a["ffn_w_out"][layer], 0, F1 // P)

            swiglu(0)
            slot = (SUBS["pool"] // 2) % RAW
            sp.wait_ge(w_lo, SUBS["pool"] - 2 * RAW + 2)
            sp.dma_start(raw[:, slot, :].rearrange("p (g c) -> p g c", g=8),
                         a["pool_w"][0].rearrange("g (k p) o -> p (g k) o", p=P)).then_inc(w_raw[slot], 32)
            swiglu(1)
            n = SUBS["win"]
            with sp.Fori(0, 2) as i:
                for j in range(2):
                    chunk(n + 4 * j, i, a["w_in_2"][0], i * (2 * CW) + j * CW)
            with sp.Fori(0, 6) as i:
                for j in range(2):
                    chunk(n + 16 + 4 * j, i, a["w_in_2"][0], i * (2 * CW) + (LR0 + GRANK + j * CW))
            rows_of(SUBS["bra"], a["w_branch_a_2"][0], 0, KT)
            rows_of(SUBS["brb"], a["w_branch_b_2"][0], 0, KT)
            rows_of(SUBS["wo2"], a["w_out_2"][0], 0, KT)
            n = SUBS["up"]
            with sp.Fori(0, 4) as i:
                for j in range(2):
                    chunk(n + 4 * j, i, a["w_up_2"][0], i * (2 * CW) + j * CW)
            rows_of(SUBS["down"], a["w_down_2"][0], 0, F2 // P)
            rows_of(SUBS["pg"], a["w_ple_gate_2"][0], 0, KT)
            rows_of(SUBS["ple"], a["w_ple_2"][0], 0, 2)
            for t in range(TT):
                sp.wait_ge(x_done, t + 1)
                sp.dma_start(out[0, t * P:(t + 1) * P, :], x[:, t, :]).then_inc(out_done, 16)
            sp.wait_ge(out_done, 16 * TT)

        @block.gpsimd
        def _(pool):
            pool.dma_start(rows[0:96, :], a["b_mod"].rearrange("l (r p) -> (l r) p", p=P)).then_inc(rows_in, 16)
            pool.dma_start(rows[96:104, :], a["c"].rearrange("b (r p) -> (b r) p", p=P)).then_inc(rows_in, 16)
            pool.dma_start(rows[104:112, :], a["c_ctx"].rearrange("(r p) -> r p", p=P)).then_inc(rows_in, 16)
            pool.dma_start(cst[:, :], cst_d).then_inc(cst_in, 16)
            nc.gpsimd.memset(cT[:, :, :], 0.0).then_inc(cT_zero, 1)
            pool.dma_start(lnp[:, :, :], a["ctx"].rearrange("b (t p) d -> p (b t) d", p=P)).then_inc(ctx_in, 16)
            pool.dma_start(lamt[:, :], a["attn_lambda"].rearrange("a l d -> a (l d)").to_broadcast([P, 256]))\
                .then_inc(small_in, 16)
            pool.dma_start(subg[:, :], a["attn_subln_g"].to_broadcast([P, P])).then_inc(small_in, 16)
            pool.dma_start(g1b[:, :], a["b_mod"][0:1, 2 * D:3 * D].to_broadcast([P, D])).then_inc(bias0_in, 16)
            pool.dma_start(g2b0[:, :], a["b_mod"][0:1, 5 * D:6 * D].to_broadcast([P, D])).then_inc(bias0_in, 16)

            def mod_load(c):
                layer, m = MODS[c]
                wk = a["w_mod"][layer].rearrange("(k p) n -> p k n", p=P)
                for h in range(2):
                    if c > NMOD0:
                        pool.wait_ge(mod_used, 2 * (c - NMOD0 - 1) + h + 1)
                    pool.dma_start(modraw[:, h, :].rearrange("p (k c) -> p k c", k=4),
                                   wk[:, 4 * h:4 * h + 4, m * CW:(m + 1) * CW]).then_inc(mod_in[h], 16)

            def ln_load(k):
                if k == 0:
                    pool.wait_ge(t_done, GROUPS["ctx"] + 4)
                else:
                    pool.wait_ge(ln_x, TT * k)
                for j, w in enumerate((a["ln_g"], a["ln_b"])):
                    pool.dma_start(lnp[:, j, :], w[k // 2, k % 2:k % 2 + 1, :].to_broadcast([P, D])).then_inc(ln_in, 16)

            mod_load(NMOD0)
            pool.wait_ge(mod_acc, NMOD0)
            nc.gpsimd.memset(qz[:, :, :, :], 0.0).then_inc(qz_zero, 1)
            ln_load(0)
            for c in range(NMOD0 + 1, 16):
                mod_load(c)
            ln_load(1)
            for dst, j in ((sh1b, 0), (sc1b, 1), (g1b, 2), (g2b1, 5)):
                pool.dma_start(dst[:, :], a["b_mod"][1:2, j * D:(j + 1) * D].to_broadcast([P, D])).then_inc(bias1_in, 16)
            pool.dma_start(psb[:, :], a["pool_scale"].to_broadcast([P, D])).then_inc(pscale_in, 16)
            for c in range(16, 24):
                mod_load(c)
            ln_load(2)
            pool.dma_start(poolm[:, :, :, :].rearrange("p t g s -> p (t g s)"), pool_d).then_inc(pool_in, 16)
            ln_load(3)
            pool.wait_ge(ln_x, TT * 4)
            for j, nm in enumerate(("norm_mix_2", "norm_mlp_2", "norm_ple_2")):
                pool.dma_start(rows2[8 * j:8 * j + 8, :], a[nm].rearrange("l (r p) -> (l r) p", p=P))\
                    .then_inc(rows2_in, 16)
            with nc.allow_non_contiguous_dma(reason="16 columns of w_in"):
                pool.dma_start(lrw[:, :, :], a["w_in_2"][0].rearrange("(k p) n -> p k n", p=P)[:, :, LR0:LR0 + GRANK])\
                    .then_inc(lrw_in, 16)
            pool.dma_start(w2[:, :], a["gla_gate_w2_2"][0]).then_inc(vec_in, 16)
            pool.dma_start(gbb[:, :], a["gla_gate_b_2"].to_broadcast([P, 512])).then_inc(vec_in, 16)
            pool.dma_start(onb[:, :], a["gla_out_norm_2"].rearrange("l h e -> l (h e)").to_broadcast([P, D]))\
                .then_inc(vec_in, 16)
            pool.dma_start(qkg[:, 0, :], a["moba_q_norm_2"].to_broadcast([P, P])).then_inc(vec_in, 16)
            pool.dma_start(qkg[:, 1, :], a["moba_k_norm_2"].to_broadcast([P, P])).then_inc(vec_in, 16)
            for t in range(TT):
                pool.wait_ge(a_evac, t + 1)
                nc.gpsimd.affine_select(out=aT[:, t, :, :], in_=aT[:, t, :, :], compare_op=ALU.is_ge, fill=0.0,
                                        base=0, pattern=[[0, GH], [1, P]], channel_multiplier=-1).then_inc(pool_self, 1)
                pool.wait_ge(pool_self, t + 1)
                nc.gpsimd.memset(aT[0:GCH, t, :, GCH:P], 0.0).then_inc(t_lo, 1)
            pool.wait_ge(w_used, summed("down"))
            pool.dma_start(pt[:, :, :], a["p_2"][0, 0].rearrange("(t p) d -> p t d", p=P)).then_inc(p_in, 16)

        @block.scalar
        def _(act):
            links = [0]

            def link(ins):
                links[0] += 1
                ins.then_inc(act_self, 1)
                act.wait_ge(act_self, links[0])

            def adv(n, i=0):
                if n >= NSUB:
                    return
                if n % 2 == 0:
                    act.wait_ge(w_raw[(n // 2) % RAW], 32 * (n // 8 + 1) + 32 * i)
                at_least(act, w_used, n - WS + 1 + 8 * i)
                nc.scalar.activation(wH[:, n % WS, :], raw[:, (n // 2) % RAW, (n % 2) * 1024:(n % 2) * 1024 + 1024],
                                     ACT.Copy).then_inc(w_hi, 1)

            def hi(g, dst, i=0, gain=None, mod=None, step=2):
                act.wait_ge(t_done, g + 1 + step * i)
                src = tbank(g).rearrange("p (k s) -> p k s", k=2)
                if gain is not None:
                    for k in range(2):
                        ins = nc.scalar.activation(dst[:, k, :], src[:, k, :], ACT.Copy, scale=gain[:, k:k + 1])
                elif mod is not None:
                    shift, scale = mod
                    tmp = tf[:, g % 2, :].rearrange("p (k s) -> p k s", k=2)
                    for k in range(2):
                        ins = nc.scalar.activation(tmp[:, k, :], src[:, k, :], ACT.Identity,
                                                   bias=shift[:, k:k + 1], scale=scale[:, k:k + 1])
                    link(ins)
                    ins = nc.scalar.activation(dst, tmp, ACT.Copy)
                else:
                    ins = nc.scalar.activation(dst, src, ACT.Copy)
                ins.then_inc(t_hi, 1)

            def modulated(layer, which, stream):
                c = modcol[:, layer, :, :, :]
                return lambda j: (c[:, which, 2 * j:2 * j + 2, stream], c[:, which + 1, 2 * j:2 * j + 2, stream])

            def mod_copy(c):
                if c < NMOD0:
                    act.wait_ge(mod_acc, c + 1)
                else:
                    act.wait_ge(mod_used, 2 * (c - NMOD0) + 2)
                nc.scalar.activation(modrow[:, :], ps[:, c if c < NMOD0 else 7, :], ACT.Copy).then_inc(mod_row, 1)

            def root(dst, src, done, cond, value):
                act.wait_ge(cond, value)
                nc.scalar.activation(dst, src, ACT.Sqrt).then_inc(done, 1)

            for n in range(WS):
                adv(n)
            act.wait_ge(rows_T, 1)
            act.wait_ge(cT_zero, 1)
            nc.scalar.activation(cT[:, :, 0:2].rearrange("p k r -> p r k"),
                                 ps[:, 6, 96:112].rearrange("p (r k) -> p r k", r=2), ACT.Silu).then_inc(cT_ready, 1)
            nc.scalar.activation(bcol[:, :], ps[:, 6, 0:96], ACT.Copy).then_inc(cT_ready, 1)
            act.wait_ge(lam_sum, 1)
            nc.scalar.activation(lam2[:, 2:4], lam2[:, 0:2], ACT.Exp).then_inc(lam_exp, 1)
            for c in range(NMOD0):
                if c:
                    act.wait_ge(mod_sel, c)
                mod_copy(c)
            act.wait_ge(mod_out, NMOD0)
            mc = modulated(0, 0, 1)
            for j in range(4):
                hi(GROUPS["ctx"] + j, cH[:, 2 * j:2 * j + 2, :], mod=mc(j))
            mc = modulated(0, 0, 0)
            for j in range(4):
                hi(GROUPS["x"] + j, aH[:, 2 * j:2 * j + 2, :], mod=mc(j))

            n = SUBS["qkv"]
            modc = [NMOD0]

            def next_mod():
                act.wait_ge(mod_sel, modc[0])
                mod_copy(modc[0])
                modc[0] += 1

            for c in range(6):
                for j in range(3):
                    adv(n + 4 * c + 4 + j)
                if c >= 2:
                    un = UNITS["k"] + 2 * (c - 2)
                    if c >= 4:
                        for j in range(2):
                            act.wait_ge(w_used, summed("v", 2 * (c - 4)))
                            nc.scalar.activation(v[:, 2 * j:2 * j + 2, (c - 4) * CW:(c - 3) * CW], pair(un + j),
                                                 ACT.Copy).then_inc(acc_out, 1)
                adv(n + 4 * c + 7)
                if c < 2:
                    for j in range(2):
                        g = GROUPS["q"] + 2 * c + j
                        act.wait_ge(t_done, g + 1)
                        if c == 0 and j == 0:
                            act.wait_ge(qz_zero, 1)
                        src = tbank(g).rearrange("p (h s) -> p h s", h=2)
                        for m in range(2):
                            ins = nc.scalar.activation(qz[64 * m:64 * m + 64, 4 * c + 2 * j:4 * c + 2 * j + 2, m, :],
                                                       src[64 * m:64 * m + 64, :, :], ACT.Copy)
                        ins.then_inc(t_lo, 1)
                elif c < 4:
                    for j in range(4):
                        g = GROUPS["k"] + 4 * (c - 2) + j
                        act.wait_ge(t_done, g + 1)
                        h0 = 4 * (c - 2) + 2 * (j % 2)
                        nc.scalar.activation(kT[:, h0:h0 + 2, (j // 2) * 256:(j // 2) * 256 + 256],
                                             tbank(g).rearrange("p (h s) -> p h s", h=2), ACT.Copy).then_inc(t_lo, 1)
                if c >= 1:
                    next_mod()
                    if c >= 3:
                        next_mod()

            for r in range(16):
                un = UNITS["att"] + r
                act.wait_ge(s_max, r + 1)
                if r >= 2:
                    act.wait_ge(acc_out, UNITS["att"] + r - 1)
                for m in range(2):
                    ins = nc.scalar.activation(ex[:, r % 2, m, :], pair(un)[:, m, :], ACT.Exp,
                                               bias=stat[:, 8 * (r % 2) + m:8 * (r % 2) + m + 1], scale=0.125,
                                               accum_out=stat[:, 8 * (r % 2) + 2 + m:8 * (r % 2) + 3 + m])
                ins.then_inc(s_exp, 1)
                if r >= 1:
                    g = GROUPS["att"] + r - 1
                    act.wait_ge(t_done, g + 1)
                    if r >= 3:
                        act.wait_ge(o_done, r - 2)
                    nc.scalar.activation(at[:, (r - 1) % 2, :, :], tbank(g).rearrange("p (k q) -> p k q", k=4),
                                         ACT.Copy).then_inc(t_lo, 1)
                if r % 4 == 2:
                    next_mod()
            g = GROUPS["att"] + 15
            act.wait_ge(t_done, g + 1)
            act.wait_ge(o_done, 14)
            nc.scalar.activation(at[:, 1, :, :], tbank(g).rearrange("p (k q) -> p k q", k=4), ACT.Copy).then_inc(t_lo, 1)
            root(stat[:, 32:48], stat[:, 16:32], o_sd, o_sq, 1)
            for j in range(4):
                hi(GROUPS["o"] + j, aH[:, 2 * j:2 * j + 2, :])
            for j in range(8):
                adv(SUBS["wo"] + 4 + j)

            def ln(k):
                for t in range(TT):
                    root(stat[:, 52 + t:53 + t], stat[:, 50 + t:51 + t], ln_sd, ln_var, TT * k + t + 1)

            def swiglu(layer):
                n, un, g = SUBS[f"in{layer}"], UNITS[f"in{layer}"], GROUPS[f"in{layer}"]

                def one(c, i=0, first=False):
                    for j in range(3):
                        adv(n + 4 * c + 4 + j, i)
                    act.wait_ge(w_used, summed(f"in{layer}", c) + 8 * i)
                    nc.scalar.activation(sil[:, c % 2, :, :], pair(un + c)[:, :, 0:256], ACT.Silu).then_inc(silu_done, 1)
                    adv(n + 4 * c + 7, i)
                    if not first:
                        k0 = 2 * (c - 1) + 4 * i
                        hi(g + c - 1, hH[:, bass.ds(k0, 2), :] if not isinstance(i, int) else hH[:, k0:k0 + 2, :], i)

                one(0, first=True)
                with act.Fori(0, 5) as i:
                    one(1, i)
                    one(2, i)
                hi(g + 10, hH[:, 20:22, :])
                for k in range(F1 // P):
                    adv(SUBS[f"out{layer}"] + 4 + k)
                    if layer == 0 and k % 2 == 0 and k < 16:
                        next_mod()

            ln(0)
            mc = modulated(0, 2, 0)
            for j in range(4):
                hi(GROUPS["x1"] + j, aH[:, 2 * j:2 * j + 2, :], mod=mc(j))
            swiglu(0)
            ln(1)
            for j in range(4):
                hi(GROUPS["pool"] + j, aH[:, 2 * j:2 * j + 2, :])
            for j in range(2):
                adv(SUBS["pool"] + 4 + j)
            ln(2)
            mc = modulated(1, 2, 0)
            for j in range(4):
                hi(GROUPS["x3"] + j, aH[:, 2 * j:2 * j + 2, :], mod=mc(j))
            swiglu(1)
            ln(3)

            def rms(k, after, value):
                act.wait_ge(after, value)
                for t in range(TT):
                    nc.scalar.activation(xn[:, t, :], x[:, t, :], ACT.Square,
                                         accum_out=stat[:, 56 + t:57 + t]).then_inc(rms_sq, 1)
                root(stat[:, 60:62], stat[:, 58:60], rms_sd, rms_ms, k + 1)

            def gained(k, dst, name):
                for j in range(4):
                    hi(GROUPS[name] + j, dst[:, 2 * j:2 * j + 2, :], gain=gcol[:, 8 * k + 2 * j:8 * k + 2 * j + 2])

            rms(0, ln_x, 8)
            act.wait_ge(rows2_T, 1)
            link(nc.scalar.activation(gcol[:, :], ps[:, 6, 0:24], ACT.Copy))
            act.wait_ge(lrw_in, 16)
            nc.scalar.activation(lrH[:, :, :], lrw[:, :, :], ACT.Copy).then_inc(lr_hi, 1)
            gained(0, aH, "rms0")
            n, un = SUBS["win"], UNITS["win"]

            def win(c, func, i=0):
                for j in range(3):
                    adv(n + 4 * c + 4 + j, i)
                act.wait_ge(w_used, summed("win", c) + 8 * i)
                dst = u[:, :, c * CW:(c + 1) * CW] if isinstance(i, int) else u[:, :, bass.ds(c * CW + i * (2 * CW), CW)]
                nc.scalar.activation(dst, pair(un + c), func).then_inc(acc_out, 1)
                adv(n + 4 * c + 7, i)

            with act.Fori(0, 2) as i:
                win(0, ACT.Copy, i)
                win(1, ACT.Copy, i)
            win(4, ACT.Silu)
            win(5, ACT.Silu)
            with act.Fori(0, 3) as i:
                win(6, ACT.Copy, i)
                win(7, ACT.Copy, i)
            with act.Fori(0, 2) as i:
                win(12, ACT.Sigmoid, i)
                win(13, ACT.Sigmoid, i)
            act.wait_ge(lr_done, 1)
            nc.scalar.activation(lrt[:, :, :], ps[:, 6, 0:TT * GRANK].rearrange("p (t r) -> p t r", t=TT), ACT.Copy)\
                .then_inc(lr_t, 1)
            act.wait_ge(lr_T, 1)
            nc.scalar.activation(lrT[:, :], ps[0:GRANK, 6, 0:S], ACT.Copy).then_inc(lr_Tc, 1)
            act.wait_ge(z_abs, 1)
            link(nc.scalar.activation(lt, lt, ACT.Exp, scale=-1.0))
            nc.scalar.activation(lt, lt, ACT.Ln, bias=1.0).then_inc(z_ln, 1)
            act.wait_ge(dec_sum, 1)
            nc.scalar.activation(dec[:, :, :, :].rearrange("p h t j -> p (h t j)"), ps[:, 6, 0:16], ACT.Exp)\
                .then_inc(dec_exp, 1)
            un = UNITS["cum"]
            act.wait_ge(acc_done, 18)
            nc.scalar.activation(lt, pair(un), ACT.Exp).then_inc(e_ready, 1)
            nc.scalar.activation(ekd[:, :, :], pair(un), ACT.Exp, scale=-1.0).then_inc(e_ready, 1)
            act.wait_ge(acc_done, 19)
            nc.scalar.activation(ekl[:, :, :], pair(un + 1), ACT.Exp).then_inc(e_ready, 1)
            for j in range(2):
                un = UNITS["gqT"] + j
                act.wait_ge(acc_done, 20 + j)
                nc.scalar.activation(qkT[:, j, :, :].rearrange("p (a h) s -> p a (h s)", a=2), pair(un), ACT.Copy)\
                    .then_inc(acc_out, 1)
            for t in range(TT):
                g = GROUPS["glaA"] + t
                act.wait_ge(t_done, g + 1)
                nc.scalar.activation(ekd[:, t, :], tbank(g), ACT.Copy).then_inc(a_evac, 1)
            for t in range(TT):
                un = UNITS["go"] + t
                act.wait_ge(acc_done, 22 + t)
                nc.scalar.activation(xn[:, t, :].rearrange("p (b c) -> p b c", b=2), pair(un), ACT.Copy)\
                    .then_inc(acc_out, 1)
            root(stat[:, 8:16], stat[:, 0:8], go_sd, go_sq, 1)
            root(stat[:, 32:48], stat[:, 16:32], m_sd, m_sq, 1)
            root(stat[:, 16:32], stat[:, 0:16], m_sd, m_sq, 2)
            for j in range(4):
                hi(GROUPS["oa"] + j, aH[:, 2 * j:2 * j + 2, :])
            for j in range(8):
                adv(SUBS["bra"] + 4 + j)
            for j in range(8):
                g = GROUPS["mqk"] + j
                act.wait_ge(t_done, g + 1)
                nc.scalar.activation(mT[:, 2 * j:2 * j + 2, :], tbank(g).rearrange("p (h s) -> p h s", h=2), ACT.Copy)\
                    .then_inc(t_lo, 1)
            for h in range(H):
                act.wait_ge(m_max, h + 1)
                if h >= 2:
                    act.wait_ge(t_done, GROUPS["moba"] + 2 * (h - 1))
                for t in range(TT):
                    ins = nc.scalar.activation(pe_[:, h % 2, t, :], sc[:, h % 2, t, :], ACT.Exp,
                                               bias=stat[:, 8 * (h % 2) + t:8 * (h % 2) + t + 1],
                                               accum_out=stat[:, 8 * (h % 2) + 2 + t:8 * (h % 2) + 3 + t])
                ins.then_inc(m_exp, 1)
                g = GROUPS["moba"] + 2 * h
                act.wait_ge(t_done, g + 2)
                if h >= 2:
                    act.wait_ge(m_o, h - 1)
                nc.scalar.activation(pT[:, h % 2, 0, :], tbank(g)[:, 0:S], ACT.Copy).then_inc(t_lo, 1)
                nc.scalar.activation(pT[:, h % 2, 1, P:S], tbank(g + 1)[:, 0:P], ACT.Copy).then_inc(t_lo, 1)
            for j in range(4):
                hi(GROUPS["ob"] + j, aH[:, 2 * j:2 * j + 2, :])
            for j in range(8):
                adv(SUBS["brb"] + 4 + j)
            for j in range(4):
                hi(GROUPS["y"] + j, aH[:, 2 * j:2 * j + 2, :])
            for j in range(8):
                adv(SUBS["wo2"] + 4 + j)
            rms(1, acc_out, UNITS["wo2"] + 2)
            gained(1, aH, "rms1")
            n, un, g = SUBS["up"], UNITS["up"], GROUPS["up"]

            def up(c, i=0, first=False):
                for j in range(4):
                    adv(n + 4 * c + 4 + j, i)
                if not first:
                    for j in range(2):
                        k0 = 4 * (c - 1) + 2 * j
                        hi(g + 2 * (c - 1) + j, uH[:, k0:k0 + 2, :] if isinstance(i, int)
                           else uH[:, bass.ds(k0 + 8 * i, 2), :], i, step=4)

            up(0, first=True)
            with act.Fori(0, 3) as i:
                up(1, i)
                up(2, i)
            up(7)
            for j in range(2):
                hi(g + 14 + j, uH[:, 28 + 2 * j:30 + 2 * j, :])
            for k in range(F2 // P):
                adv(SUBS["down"] + 4 + k)
            rms(2, acc_out, UNITS["down"] + 2)
            gained(2, aH, "rms2")
            for j in range(8):
                adv(SUBS["pg"] + 4 + j)
            for t in range(TT):
                un = UNITS["pg"] + t
                act.wait_ge(w_used, summed("pg"))
                nc.scalar.activation(gate[:, t, :].rearrange("p (b c) -> p b c", b=2), pair(un), ACT.Sigmoid)\
                    .then_inc(acc_out, 1)
            hi(GROUPS["p"], pH[:, :, :])

        @block.vector
        def _(dve):
            links = [0]

            def link(ins):
                links[0] += 1
                ins.then_inc(dve_self, 1)
                dve.wait_ge(dve_self, links[0])

            V = nc.vector

            def adv(n, i=0):
                if n >= NSUB:
                    return
                dve.wait_ge(w_hi, n + 1 + 8 * i)
                V.tensor_tensor(wL[:, n % WS, :], raw[:, (n // 2) % RAW, (n % 2) * 1024:(n % 2) * 1024 + 1024],
                                wH[:, n % WS, :].bitcast(fp32), ALU.subtract).then_inc(w_lo, 1)

            def lo(g, dst, high, i=0, gain=None, mod=False, step=2, k_hi=None):
                dve.wait_ge(t_hi, k_hi + 1 + step * i)
                src = tbank(g).rearrange("p (k s) -> p k s", k=2)
                if gain is not None:
                    for k in range(2):
                        ins = V.scalar_tensor_tensor(out=dst[:, k, :], in0=src[:, k, :], scalar=gain[:, k:k + 1],
                                                     in1=high[:, k, :].bitcast(fp32), op0=ALU.mult, op1=ALU.subtract)
                elif mod:
                    ins = V.tensor_tensor(dst, tf[:, g % 2, :].rearrange("p (k s) -> p k s", k=2),
                                          high.bitcast(fp32), ALU.subtract)
                else:
                    ins = V.tensor_tensor(dst, src, high.bitcast(fp32), ALU.subtract)
                ins.then_inc(t_lo, 1)

            hcount = [0]

            def lo4(name, L_, H_, **kw):
                gain = kw.pop("gain", None)
                for j in range(4):
                    lo(GROUPS[name] + j, L_[:, 2 * j:2 * j + 2, :], H_[:, 2 * j:2 * j + 2, :],
                       gain=None if gain is None else gain[:, 2 * j:2 * j + 2], k_hi=hcount[0], **kw)
                    hcount[0] += 1

            def mod_put(c):
                layer, m = MODS[c]
                one = 1.0 if m // 2 in (1, 4) else 0.0
                dve.wait_ge(mod_sel, c + 1)
                if mod_is_column(layer, m):
                    b0 = 48 * layer + 4 * m
                    V.scalar_tensor_tensor(
                        out=modcol[:, layer, MOD_WHICH[m // 2], 4 * (m % 2):4 * (m % 2) + 4, :],
                        in0=ps[:, 7, 0:8].rearrange("p (k r) -> p k r", r=2), scalar=one,
                        in1=bcol[:, b0:b0 + 4].unsqueeze(2).to_broadcast([P, 4, 2]),
                        op0=ALU.add, op1=ALU.add).then_inc(mod_out, 1)
                else:
                    dst = {(0, 2): g1b, (0, 5): g2b0, (1, 0): sh1b, (1, 1): sc1b, (1, 2): g1b, (1, 5): g2b1}[layer, m // 2]
                    dst = dst[:, (m % 2) * CW:(m % 2) * CW + CW]
                    if layer == 0:
                        dve.wait_ge(bias0_in, 32)
                    else:
                        dve.wait_ge(bias1_in, 64)
                    V.scalar_tensor_tensor(out=dst, in0=ps[:, 7, :], scalar=one, in1=dst,
                                           op0=ALU.add, op1=ALU.add).then_inc(mod_out, 1)

            for n in range(WS):
                adv(n)
            dve.wait_ge(small_in, 32)
            lv = lamt[:, :].rearrange("p (a b d) -> p a b d", a=2, b=2)
            link(V.tensor_tensor(lv[:, :, 0, :], lv[:, :, 0, :], lv[:, :, 1, :], ALU.mult))
            V.tensor_reduce(lam2[:, 0:2], lv[:, :, 0, :], AXX, ALU.add).then_inc(lam_sum, 1)
            dve.wait_ge(lam_exp, 1)
            link(V.tensor_tensor(lam2[:, 4:5], lam2[:, 2:3], lam2[:, 3:4], ALU.subtract))
            link(V.tensor_scalar(lam2[:, 5:6], lam2[:, 4:5], LAM_INIT, None, ALU.add))
            link(V.tensor_scalar(subg[:, :], subg[:, :], 1.0 - LAM_INIT, None, ALU.mult))
            dve.wait_ge(cT_ready, 2)
            for c in range(NMOD0):
                mod_put(c)
            lo4("ctx", cL, cH, mod=True)
            lo4("x", aL, aH, mod=True)

            modc = [NMOD0]

            def next_mod():
                mod_put(modc[0])
                modc[0] += 1

            rots = [0]

            def rotate(un, done, plain):
                dve.wait_ge(w_used, done)
                if rots[0]:
                    dve.wait_ge(t_done, GROUPS["q"] + 2 * rots[0])
                if plain:
                    V.tensor_copy(ro[:, :, :], pair(un)).then_inc(acc_out, 1)
                else:
                    for t in range(TT):
                        src = pair(un)[:, t, :].rearrange("p (m h d) -> p m h d", h=2, d=32)
                        for j, tab in enumerate((C_COS, C_SIN)):
                            cs = cst[:, tab + 32 * t:tab + 32 * t + 32].unsqueeze(1).unsqueeze(1).to_broadcast([P, 8, 2, 32])
                            ins = V.tensor_tensor(rt[:, j, t, :].rearrange("p (m h d) -> p m h d", h=2, d=32), src, cs,
                                                  ALU.mult)
                    link(ins)
                    for t in range(TT):
                        c_, s_ = (rt[:, j, t, :].rearrange("p (m h d) -> p m h d", h=2, d=32) for j in range(2))
                        o_ = ro[:, t, :].rearrange("p (m h d) -> p m h d", h=2, d=32)
                        V.tensor_tensor(o_[:, :, 0, :], c_[:, :, 0, :], s_[:, :, 1, :], ALU.subtract)
                        ins = V.tensor_tensor(o_[:, :, 1, :], s_[:, :, 0, :], c_[:, :, 1, :], ALU.add)
                    ins.then_inc(acc_out, 1)
                rots[0] += 1

            n = SUBS["qkv"]
            for c in range(6):
                for j in range(3):
                    adv(n + 4 * c + 4 + j)
                if c < 2:
                    rotate(UNITS["q"] + c, summed("q", c), False)
                elif c < 4:
                    rotate(UNITS["k"] + 2 * (c - 2), summed("k", 2 * (c - 2)), True)
                    rotate(UNITS["k"] + 2 * (c - 2) + 1, summed("k", 2 * (c - 2)), False)
                adv(n + 4 * c + 7)
                if c >= 1:
                    next_mod()
                    if c >= 3:
                        next_mod()

            def mix(r):
                b = 8 * (r % 2)
                dve.wait_ge(s_exp, r + 1)
                link(V.reciprocal(stat[:, b + 4:b + 6], stat[:, b + 2:b + 4]))
                link(V.tensor_tensor(stat[:, b + 6:b + 7], stat[:, b + 5:b + 6], lam2[:, 5:6], ALU.mult))
                link(V.tensor_scalar(te, ex[:, r % 2, 1, :], stat[:, b + 6:b + 7], None, ALU.mult))
                if r >= 2:
                    dve.wait_ge(t_done, GROUPS["att"] + r - 1)
                V.scalar_tensor_tensor(out=am[:, r % 2, :], in0=ex[:, r % 2, 0, :], scalar=stat[:, b + 4:b + 5],
                                       in1=te, op0=ALU.mult, op1=ALU.subtract).then_inc(acc_out, 1)

            def put_o(r):
                h, t = r // 2, r % 2
                dve.wait_ge(o_done, r + 1)
                V.tensor_copy(ot[:, t, h * P:(h + 1) * P], ps[:, 6, 0:P]).then_inc(o_out, 1)

            for r in range(16):
                b = 8 * (r % 2)
                dve.wait_ge(acc_done, r + 1)
                link(V.tensor_reduce(stat[:, b + 6:b + 8], pair(UNITS["att"] + r), AXX, ALU.max))
                V.tensor_scalar(stat[:, b:b + 2], stat[:, b + 6:b + 8], -0.125, None, ALU.mult).then_inc(s_max, 1)
                if r >= 1:
                    mix(r - 1)
                if r >= 2:
                    put_o(r - 2)
                if r % 4 == 2:
                    next_mod()
            mix(15)
            put_o(14)
            put_o(15)
            sq = ex[:, :, :, :].rearrange("p a b (h d) -> p a (b h) d", d=P)
            o4 = ot[:, :, :].rearrange("p t (h d) -> p t h d", d=P)
            dve.wait_ge(acc_out, UNITS["att"] + 16)
            dve.wait_ge(o_out, 16)
            link(V.tensor_tensor(sq, o4, o4, ALU.mult))
            link(V.tensor_reduce(stat[:, 32:48].rearrange("p (t h) -> p t h", t=TT), sq, AXX, ALU.add))
            V.tensor_scalar(stat[:, 16:32], stat[:, 32:48], 1.0 / P, LN_EPS, ALU.mult, ALU.add).then_inc(o_sq, 1)
            dve.wait_ge(o_sd, 1)
            link(V.reciprocal(stat[:, 16:32], stat[:, 32:48]))
            link(V.tensor_tensor(o4, o4, stat[:, 16:32].rearrange("p (t h) -> p t h", t=TT).unsqueeze(3)
                                 .to_broadcast([P, TT, H, P]), ALU.mult))
            for t in range(TT):
                V.tensor_tensor(o4[:, t, :, :], o4[:, t, :, :], subg[:, :].unsqueeze(1).to_broadcast([P, H, P]), ALU.mult)\
                    .then_inc(o_norm, 1)
            lo4("o", aL, aH)
            for j in range(8):
                adv(SUBS["wo"] + 4 + j)

            def ln(k, stage, gate_):
                tmp = tf[:, :, :].rearrange("p b c -> p (b c)")
                un = UNITS[stage]
                for t in range(TT):
                    dve.wait_ge(w_used, summed(stage))
                    V.tensor_tensor(tf[:, :, :], pair(un + t), gate_[:, :].rearrange("p (b c) -> p b c", b=2), ALU.mult)\
                        .then_inc(acc_out, 1)
                    dve.wait_ge(acc_out, un + t + 1)
                    link(V.scalar_tensor_tensor(out=x[:, t, :], in0=x[:, t, :], scalar=ALPHA, in1=tmp,
                                                op0=ALU.mult, op1=ALU.add))
                    V.bn_stats(bn[:, t, 0:6], x[:, t, 0:512])
                    link(V.bn_stats(bn[:, t, 6:12], x[:, t, 512:1024]))
                    link(V.bn_aggr(mv[:, t, :], bn[:, t, :]))
                    V.tensor_scalar(stat[:, 50 + t:51 + t], mv[:, t, 1:2], LN_EPS, None, ALU.add).then_inc(ln_var, 1)
                for t in range(TT):
                    dve.wait_ge(ln_sd, TT * k + t + 1)
                    link(V.reciprocal(stat[:, 54 + t:55 + t], stat[:, 52 + t:53 + t]))
                    link(V.tensor_scalar(x[:, t, :], x[:, t, :], mv[:, t, 0:1], stat[:, 54 + t:55 + t],
                                         ALU.subtract, ALU.mult))
                    dve.wait_ge(ln_in, 32 * (k + 1))
                    link(V.tensor_tensor(x[:, t, :], x[:, t, :], lnp[:, 0, :], ALU.mult))
                    V.tensor_tensor(x[:, t, :], x[:, t, :], lnp[:, 1, :], ALU.add).then_inc(ln_x, 1)

            def swiglu(layer):
                n, un, g = SUBS[f"in{layer}"], UNITS[f"in{layer}"], GROUPS[f"in{layer}"]
                k_hi = hcount[0]
                sbase = 11 * layer

                def low(c, i):
                    k0 = 2 * c + 4 * i
                    d, s = (hL[:, k0:k0 + 2, :], hH[:, k0:k0 + 2, :]) if isinstance(i, int) else \
                           (hL[:, bass.ds(k0, 2), :], hH[:, bass.ds(k0, 2), :])
                    lo(g + c, d, s, i, k_hi=k_hi + c)

                def one(c, i=0, first=False):
                    for j in range(3):
                        adv(n + 4 * c + 4 + j, i)
                    dve.wait_ge(silu_done, sbase + c + 1 + 2 * i)
                    V.tensor_tensor(hid[:, c % 2, :, :], sil[:, c % 2, :, :], pair(un + c)[:, :, 256:512], ALU.mult)\
                        .then_inc(acc_out, 1)
                    adv(n + 4 * c + 7, i)
                    if not first:
                        low(c - 1, i)

                one(0, first=True)
                with dve.Fori(0, 5) as i:
                    one(1, i)
                    one(2, i)
                low(10, 0)
                hcount[0] += 11
                for k in range(F1 // P):
                    adv(SUBS[f"out{layer}"] + 4 + k)
                    if layer == 0 and k % 2 == 1 and k < 16:
                        next_mod()

            ln(0, "wo", g1b)
            lo4("x1", aL, aH, mod=True)
            swiglu(0)
            ln(1, "out0", g2b0)
            dve.wait_ge(ln_x, 2 * TT)
            for t in range(TT):
                V.tensor_tensor(hm[:, t, :], x[:, t, :], sc1b[:, :], ALU.mult)
            dve.wait_ge(pscale_in, 16)
            link(V.tensor_tensor(g1b[:, :], g1b[:, :], psb[:, :], ALU.mult))
            for t in range(TT):
                V.tensor_tensor(hm[:, t, :], hm[:, t, :], sh1b[:, :], ALU.add).then_inc(pool_h, 1)
            lo4("pool", aL, aH)
            for j in range(2):
                adv(SUBS["pool"] + 4 + j)
            ln(2, "pool", g1b)
            lo4("x3", aL, aH, mod=True)
            swiglu(1)
            ln(3, "out1", g2b1)

            def rms(k):
                dve.wait_ge(rms_sq, TT * (k + 1))
                V.tensor_scalar(stat[:, 58:60], stat[:, 56:58], 1.0 / D, RMS_EPS, ALU.mult, ALU.add).then_inc(rms_ms, 1)
                dve.wait_ge(rms_sd, k + 1)
                link(V.reciprocal(stat[:, 62:64], stat[:, 60:62]))
                for t in range(TT):
                    V.tensor_scalar(xn[:, t, :], x[:, t, :], stat[:, 62 + t:63 + t], None, ALU.mult).then_inc(xn_ready, 1)

            rms(0)
            dve.wait_ge(lr_hi, 1)
            V.tensor_tensor(lrL[:, :, :], lrw[:, :, :], lrH[:, :, :].bitcast(fp32), ALU.subtract).then_inc(lr_lo, 1)
            lo4("rms0", aL, aH, gain=gcol[:, 0:8])
            n = SUBS["win"]
            with dve.Fori(0, 8) as i:
                for j in range(8):
                    adv(n + 4 + j, i)
            dve.wait_ge(acc_done, 17)
            dve.wait_ge(vec_in, 80)
            link(V.tensor_tensor(la, pair(UNITS["z"]), gbb[:, :].unsqueeze(1).to_broadcast([P, TT, 512]), ALU.add))
            V.scalar_tensor_tensor(out=lt, in0=la, scalar=-1.0, in1=la,
                                   op0=ALU.mult, op1=ALU.max).then_inc(z_abs, 1)
            dve.wait_ge(z_ln, 1)
            V.scalar_tensor_tensor(out=la, in0=la, scalar=0.0, in1=lt,
                                   op0=ALU.min, op1=ALU.subtract).then_inc(acc_out, 1)
            gq, gk = u[:, :, 0:512], u[:, :, 512:1024]
            dve.wait_ge(e_ready, 2)
            V.scalar_tensor_tensor(out=gq, in0=gq, scalar=GDK ** -0.5, in1=lt, op0=ALU.mult, op1=ALU.mult)\
                .then_inc(g_mul, 1)
            V.tensor_tensor(ekd[:, :, :], ekd[:, :, :], gk, ALU.mult).then_inc(acc_out, 1)
            dve.wait_ge(e_ready, 3)
            V.tensor_tensor(ekl[:, :, :], ekl[:, :, :], gk, ALU.mult).then_inc(acc_out, 1)
            dve.wait_ge(dec_exp, 1)
            for c in range(3):
                for h in range(GH):
                    dve.wait_ge(kv_done, GH * c + h + 1)
                    src = ps[:, 6 + h % 2, 0:GDV]
                    if c == 0:
                        ins = V.tensor_copy(st[:, 0, h, :], src)
                    else:
                        if h == 0:
                            dve.wait_ge(kv_out, GH * c)
                        ins = V.scalar_tensor_tensor(out=st[:, c, h, :], in0=st[:, c - 1, h, :],
                                                     scalar=dec[:, h, c // 2, c % 2:c % 2 + 1], in1=src,
                                                     op0=ALU.mult, op1=ALU.add)
                    ins.then_inc(kv_out, 1)
            dve.wait_ge(acc_out, UNITS["go"] + 2)
            o4g = xn[:, :, :].rearrange("p t (h e) -> p t h e", e=GDV)
            sq = qkT[:, :, :, :].rearrange("p t h e -> p t h e")
            link(V.tensor_tensor(sq, o4g, o4g, ALU.mult))
            link(V.tensor_reduce(stat[:, 8:16].rearrange("p (t h) -> p t h", t=TT), sq, AXX, ALU.add))
            V.tensor_scalar(stat[:, 0:8], stat[:, 8:16], 1.0 / GDV, RMS_EPS, ALU.mult, ALU.add).then_inc(go_sq, 1)
            dve.wait_ge(go_sd, 1)
            link(V.reciprocal(stat[:, 0:8], stat[:, 8:16]))
            link(V.tensor_tensor(o4g, o4g, stat[:, 0:8].rearrange("p (t h) -> p t h", t=TT).unsqueeze(3)
                                 .to_broadcast([P, TT, GH, GDV]), ALU.mult))
            link(V.tensor_tensor(xn[:, :, :], xn[:, :, :], onb[:, :].unsqueeze(1).to_broadcast([P, TT, D]), ALU.mult))
            V.tensor_tensor(xn[:, :, :], xn[:, :, :], u[:, :, 2048:3072], ALU.mult).then_inc(oa_ready, 1)
            mqk = u[:, :, 3072:5120].rearrange("p t (g d) -> p t g d", d=P)
            sqm = mT[:, :, :].rearrange("p g (x d) -> p (g x) d", d=P)
            for t in range(TT):
                link(V.tensor_tensor(sqm[:, 0:16, :], mqk[:, t, :, :], mqk[:, t, :, :], ALU.mult))
                link(V.tensor_reduce(stat[:, 32:48] if t == 0 else stat[:, 48:64], sqm[:, 0:16, :], AXX, ALU.add))
            V.tensor_scalar(stat[:, 16:32], stat[:, 32:48], 1.0 / P, RMS_EPS, ALU.mult, ALU.add).then_inc(m_sq, 1)
            dve.wait_ge(m_sd, 1)
            link(V.tensor_scalar(stat[:, 0:16], stat[:, 48:64], 1.0 / P, RMS_EPS, ALU.mult, ALU.add))
            link(V.reciprocal(stat[:, 48:64], stat[:, 32:48]))
            link(V.tensor_scalar(stat[:, 48:56], stat[:, 48:56], P ** -0.5, None, ALU.mult))
            for t in range(TT):
                if t == 1:
                    V.tensor_copy(stat[:, 0:1], stat[:, 0:1]).then_inc(m_sq, 1)
                    dve.wait_ge(m_sd, 2)
                    link(V.reciprocal(stat[:, 48:64], stat[:, 16:32]))
                    link(V.tensor_scalar(stat[:, 48:56], stat[:, 48:56], P ** -0.5, None, ALU.mult))
                link(V.tensor_tensor(mqk[:, t, :, :], mqk[:, t, :, :], stat[:, 48:64].unsqueeze(2)
                                     .to_broadcast([P, 16, P]), ALU.mult))
                for j in range(2):
                    ins = V.tensor_tensor(mqk[:, t, 8 * j:8 * j + 8, :], mqk[:, t, 8 * j:8 * j + 8, :],
                                          qkg[:, j, :].unsqueeze(1).to_broadcast([P, 8, P]), ALU.mult)
                link(ins)
            V.tensor_copy(stat[:, 48:49], stat[:, 48:49]).then_inc(m_norm, 1)
            lo4("oa", aL, aH)
            for j in range(8):
                adv(SUBS["bra"] + 4 + j)
            ga, gb = u[:, :, 6144:7168], u[:, :, 7168:8192]
            for t in range(TT):
                dve.wait_ge(w_used, summed("bra"))
                V.tensor_tensor(ga[:, t, :].rearrange("p (b c) -> p b c", b=2), pair(UNITS["bra"] + t),
                                ga[:, t, :].rearrange("p (b c) -> p b c", b=2), ALU.mult).then_inc(acc_out, 1)
            dist = cst[:, C_DIST:C_TRI].rearrange("p (t k) -> p t k", t=TT)
            ob = xn

            def moba_out(h):
                b = 8 * (h % 2)
                dve.wait_ge(m_o, h + 1)
                dve.wait_ge(m_exp, h + 1)
                link(V.reciprocal(stat[:, b + 4:b + 6], stat[:, b + 2:b + 4]))
                for t in range(TT):
                    ins = V.tensor_scalar(ob[:, t, h * P:(h + 1) * P], ps[:, 6 + h % 2, t * P:(t + 1) * P],
                                          stat[:, b + 4 + t:b + 5 + t], None, ALU.mult)
                ins.then_inc(m_oout, 1)

            for h in range(H):
                b = 8 * (h % 2)
                un = h % 2
                dve.wait_ge(s_max, 16 + h + 1)
                if h >= 2:
                    dve.wait_ge(m_exp, h - 1)
                link(V.scalar_tensor_tensor(out=sc[:, h % 2, :, :], in0=dist, scalar=2.0 ** -(h + 1),
                                            in1=ps[:, h % 4, :].rearrange("p (t k) -> p t k", t=TT),
                                            op0=ALU.mult, op1=ALU.add))
                V.tensor_reduce(stat[:, b:b + 2], sc[:, h % 2, :, :], AXX, ALU.max, negate=True).then_inc(m_max, 1)
                if h >= 1:
                    moba_out(h - 1)
            moba_out(H - 1)
            lo4("ob", aL, aH)
            for j in range(8):
                adv(SUBS["brb"] + 4 + j)
            for t in range(TT):
                dve.wait_ge(w_used, summed("brb"))
                gbt = gb[:, t, :].rearrange("p (b c) -> p b c", b=2)
                V.tensor_tensor(gbt, pair(UNITS["brb"] + t), gbt, ALU.mult).then_inc(acc_out, 1)
                dve.wait_ge(acc_out, UNITS["brb"] + t + 1)
                V.tensor_tensor(xn[:, t, :], ga[:, t, :], gb[:, t, :], ALU.add).then_inc(oa_ready, 1)
            lo4("y", aL, aH)
            for j in range(8):
                adv(SUBS["wo2"] + 4 + j)

            def residual(stage):
                un = UNITS[stage]
                for t in range(TT):
                    dve.wait_ge(w_used, summed(stage))
                    xt = x[:, t, :].rearrange("p (b c) -> p b c", b=2)
                    V.tensor_tensor(xt, pair(un + t), xt, ALU.add).then_inc(acc_out, 1)

            residual("wo2")
            rms(1)
            lo4("rms1", aL, aH, gain=gcol[:, 8:16])
            n, un, g = SUBS["up"], UNITS["up"], GROUPS["up"]
            k_hi = hcount[0]

            def ulow(c, i):
                for j in range(2):
                    k0 = 4 * c + 2 * j
                    d, s = (uL[:, k0:k0 + 2, :], uH[:, k0:k0 + 2, :]) if isinstance(i, int) else \
                           (uL[:, bass.ds(k0 + 8 * i, 2), :], uH[:, bass.ds(k0 + 8 * i, 2), :])
                    lo(g + 2 * c + j, d, s, i, k_hi=k_hi + 2 * c + j, step=4)

            def up(c, i=0, first=False):
                for j in range(3):
                    adv(n + 4 * c + 4 + j, i)
                dve.wait_ge(w_used, summed("up", c) + 8 * i)
                V.tensor_scalar(hu[:, c % 2, :, :], pair(un + c), 0.0, None, ALU.max).then_inc(acc_out, 1)
                dve.wait_ge(acc_out, un + c + 1 + 2 * i)
                V.tensor_tensor(hu[:, c % 2, :, :], hu[:, c % 2, :, :], hu[:, c % 2, :, :], ALU.mult).then_inc(silu_done, 1)
                adv(n + 4 * c + 7, i)
                if not first:
                    ulow(c - 1, i)

            up(0, first=True)
            with dve.Fori(0, 3) as i:
                up(1, i)
                up(2, i)
            up(7)
            ulow(7, 0)
            hcount[0] += 16
            for k in range(F2 // P):
                adv(SUBS["down"] + 4 + k)
            residual("down")
            rms(2)
            lo4("rms2", aL, aH, gain=gcol[:, 16:24])
            for j in range(8):
                adv(SUBS["pg"] + 4 + j)
            lo(GROUPS["p"], pL[:, :, :], pH[:, :, :], k_hi=hcount[0])
            for t in range(TT):
                dve.wait_ge(w_used, summed("ple"))
                dve.wait_ge(acc_out, UNITS["pg"] + t + 1)
                gt = gate[:, t, :].rearrange("p (b c) -> p b c", b=2)
                link(V.tensor_tensor(gt, pair(UNITS["ple"] + t), gt, ALU.mult))
                V.tensor_tensor(x[:, t, :], x[:, t, :], gate[:, t, :], ALU.add).then_inc(x_done, 1)

        @block.tensor
        def _(pe):
            T = nc.tensor

            def sub_ready(n, i=0):
                pe.wait_ge(w_lo, n + 1 + 8 * i)

            def three(outp, xh, xl, h, l, first, last_):
                T.matmul(outp, xh, h, start=first, stop=False)
                T.matmul(outp, xh, l, start=False, stop=False)
                return T.matmul(outp, xl, h, start=False, stop=last_)

            def chunk_mm(n, i, units, acts, t_need=None):
                for s in range(4):
                    sub_ready(n + s, i)
                    if t_need is not None:
                        pe.wait_ge(t_lo, t_need + s + 1)
                    if s == 0:
                        for un in units:
                            at_least(pe, acc_out, un - 1 + 2 * i)
                    for kk in range(2):
                        k = 2 * s + kk
                        h = wH[:, (n + s) % WS, kk * CW:(kk + 1) * CW]
                        l = wL[:, (n + s) % WS, kk * CW:(kk + 1) * CW]
                        for un, (xh, xl) in zip(units, acts):
                            for t in range(TT):
                                ins = three(pair(un)[:, t, :], xh[:, k, t * P:(t + 1) * P], xl[:, k, t * P:(t + 1) * P],
                                            h, l, k == 0, k == KT - 1)
                    ins.then_inc(w_used, 1)

            def rows_mm(n, un, xh, xl, kn, t_need=None, after_sub=None):
                for k in range(kn):
                    sub_ready(n + k)
                    if t_need is not None and k % 2 == 0:
                        pe.wait_ge(t_lo, t_need + k // 2 + 1)
                    for t in range(TT):
                        if k == 0:
                            at_least(pe, acc_out, un + t - 1)
                        for b in range(2):
                            ins = three(pair(un + t)[:, b, :], xh[:, k, t * P:(t + 1) * P], xl[:, k, t * P:(t + 1) * P],
                                        wH[:, (n + k) % WS, b * CW:(b + 1) * CW], wL[:, (n + k) % WS, b * CW:(b + 1) * CW],
                                        k == 0, k == kn - 1)
                    ins.then_inc(w_used, 1)
                    if after_sub is not None:
                        after_sub(k)

            def group(g, blocks, i=0, step=2):
                at_least(pe, t_lo, g - 1 + step * i if g >= 2 or not isinstance(i, int) else 0)
                for j, b in enumerate(blocks):
                    ins = T.transpose(tbank(g)[:, j * P:(j + 1) * P], b, ident)
                ins.then_inc(t_done, 1)

            def groups(name, src):
                for j in range(4):
                    group(GROUPS[name] + j, [src[:, t, (2 * j + k) * P:(2 * j + k + 1) * P] for k in range(2) for t in range(TT)])

            def mod_mm(c):
                bank = c if c < NMOD0 else 7
                if c > NMOD0:
                    pe.wait_ge(mod_out, c)
                for h in range(2):
                    if c < NMOD0:
                        if h == 0:
                            pe.wait_ge(mod0_in[c], 16)
                        src = mod0[:, 2 * c + h, :]
                    else:
                        pe.wait_ge(mod_in[h], 16 * (c - NMOD0 + 1))
                        src = modraw[:, h, :]
                    for j in range(4):
                        ins = T.matmul(ps[32 * j:32 * j + 32, bank, :], cT[:, 4 * h + j, :], src[:, j * CW:(j + 1) * CW],
                                       start=h == 0, stop=h == 1)
                    if c >= NMOD0:
                        ins.then_inc(mod_used, 1)
                if c < NMOD0:
                    ins.then_inc(mod_acc, 1)

            def mod_select(c):
                layer, m = MODS[c]
                pe.wait_ge(mod_row, c + 1)
                if c and c <= NMOD0:
                    pe.wait_ge(mod_out, c)
                if mod_is_column(layer, m):
                    for k in range(4):
                        ins = T.matmul(ps[:, 7, 2 * k:2 * k + 2], modrow[:, k * P:(k + 1) * P],
                                       cst[:, C_SELC:C_SELC + 2], start=True, stop=True)
                else:
                    ins = T.matmul(ps[:, 7, :], cst[:, C_SELB:C_SELB + P], modrow[:, :], start=True, stop=True)
                ins.then_inc(mod_sel, 1)

            pe.wait_ge(cst_in, 16)
            pe.wait_ge(rows_in, 48)
            T.transpose(ps[:, 6, 0:112], rows[:, :], ident[0:112, 0:112]).then_inc(rows_T, 1)
            pe.wait_ge(cT_ready, 2)
            for c in range(NMOD0):
                mod_mm(c)
            for c in range(NMOD0):
                mod_select(c)
            pe.wait_ge(ctx_in, 16)
            groups("ctx", lnp)
            pe.wait_ge(x_in, 16)
            groups("x", x)

            modc = [NMOD0]

            def mods(count=1):
                for _ in range(count):
                    mod_mm(modc[0])
                    mod_select(modc[0])
                    modc[0] += 1

            n = SUBS["qkv"]
            X, C = (aH, aL), (cH, cL)

            def heads(g, un):
                pe.wait_ge(acc_out, un + 1)
                for j in range(2):
                    group(g + j, [ro[:, t, (2 * j + k) * P:(2 * j + k + 1) * P] for k in range(2) for t in range(TT)])

            for c in range(6):
                if c < 2:
                    chunk_mm(n + 4 * c, 0, [UNITS["q"] + c], [X], GROUPS["x"] if c == 0 else None)
                    heads(GROUPS["q"] + 2 * c, UNITS["q"] + c)
                else:
                    un = UNITS["k"] + 2 * (c - 2)
                    chunk_mm(n + 4 * c, 0, [un, un + 1], [C, X])
                    if c < 4:
                        heads(GROUPS["k"] + 4 * (c - 2), un)
                        heads(GROUPS["k"] + 4 * (c - 2) + 2, un + 1)
                if c >= 1:
                    mods(2 if c >= 3 else 1)

            def scores(r):
                h, t = r // 2, r % 2
                un = UNITS["att"] + r
                if r >= 2:
                    pe.wait_ge(s_exp, r - 1)
                else:
                    pe.wait_ge(acc_out, un - 1)
                for m in range(2):
                    ins = T.matmul(pair(un)[:, m, :], qz[:, h, m, t * P:(t + 1) * P], kT[:, h, :], start=True, stop=True)
                ins.then_inc(acc_done, 1)

            def values(r):
                h = r // 2
                pe.wait_ge(t_lo, GROUPS["att"] + r + 1)
                if r >= 1:
                    pe.wait_ge(o_out, r)
                for k in range(4):
                    ins = T.matmul(ps[:, 6, 0:P], at[:, r % 2, k, :],
                                   v[:, k, h * P:(h + 1) * P], start=k == 0, stop=k == 3)
                ins.then_inc(o_done, 1)

            pe.wait_ge(t_lo, GROUPS["k"] + 8)
            scores(0)
            for r in range(16):
                if r < 15:
                    scores(r + 1)
                pe.wait_ge(acc_out, UNITS["att"] + r + 1)
                group(GROUPS["att"] + r, [am[:, r % 2, k * P:(k + 1) * P] for k in range(4)])
                if r >= 1:
                    values(r - 1)
                if r % 4 == 1:
                    mods()
            values(15)
            pe.wait_ge(o_norm, 2)
            groups("o", ot)
            rows_mm(SUBS["wo"], UNITS["wo"], aH, aL, KT, GROUPS["o"])
            pe.wait_ge(ln_x, TT)
            groups("x1", x)

            def swiglu(layer, name):
                n, un, g = SUBS[f"in{layer}"], UNITS[f"in{layer}"], GROUPS[f"in{layer}"]

                def mm(c, i=0, need=None):
                    chunk_mm(n + 4 * c, i, [un + c], [X], need)

                def tr(c, i=0):
                    pe.wait_ge(acc_out, un + c + 1 + 2 * i)
                    group(g + c, [hid[:, c % 2, t, k * P:(k + 1) * P] for k in range(2) for t in range(TT)], i)

                mm(0, need=GROUPS[name])
                with pe.Fori(0, 5) as i:
                    mm(1, i)
                    tr(0, i)
                    mm(2, i)
                    tr(1, i)
                tr(10)

                def beside(k):
                    if layer == 0 and k < 16:
                        if k % 2 == 0:
                            mod_mm(modc[0])
                        else:
                            mod_select(modc[0])
                            modc[0] += 1

                rows_mm(SUBS[f"out{layer}"], UNITS[f"out{layer}"], hH, hL, F1 // P, g, beside)

            swiglu(0, "x1")
            pe.wait_ge(pool_in, 16)
            pe.wait_ge(pool_h, 2)
            for j in range(4):
                g = GROUPS["pool"] + j
                at_least(pe, t_lo, g - 1)
                for k in range(2):
                    for t in range(TT):
                        ins = T.matmul(tbank(g)[:, k * S:(k + 1) * S], hm[:, t, (2 * j + k) * P:(2 * j + k + 1) * P],
                                       poolm[:, t, j, :], start=t == 0, stop=t == TT - 1)
                ins.then_inc(t_done, 1)
            n, un = SUBS["pool"], UNITS["pool"]
            for s in range(2):
                sub_ready(n + s)
                for gg in range(2):
                    gr = 2 * s + gg
                    pe.wait_ge(t_lo, GROUPS["pool"] + gr + 1)
                    for t in range(TT):
                        if gr == 0:
                            pe.wait_ge(acc_out, un + t - 1)
                        for k in range(2):
                            w0 = (2 * gg + k) * 256
                            ins = three(pair(un + t)[:, gr // 2, (gr % 2) * 256:(gr % 2) * 256 + 256],
                                        aH[:, 2 * gr + k, t * P:(t + 1) * P], aL[:, 2 * gr + k, t * P:(t + 1) * P],
                                        wH[:, (n + s) % WS, w0:w0 + 256], wL[:, (n + s) % WS, w0:w0 + 256],
                                        k == 0, k == 1)
                ins.then_inc(w_used, 1)
            pe.wait_ge(ln_x, 3 * TT)
            groups("x3", x)
            swiglu(1, "x3")

            pe.wait_ge(rows2_in, 48)
            pe.wait_ge(acc_out, UNITS["out1"] + 2)
            T.transpose(ps[:, 6, 0:24], rows2[:, :], ident[0:24, 0:24]).then_inc(rows2_T, 1)
            pe.wait_ge(xn_ready, TT)
            groups("rms0", xn)
            n, un = SUBS["win"], UNITS["win"]
            pe.wait_ge(t_lo, GROUPS["rms0"] + 4)
            with pe.Fori(0, 8) as i:
                for j in range(2):
                    chunk_mm(n + 4 * j, i, [un + j], [X])
            pe.wait_ge(lr_lo, 1)
            for t in range(TT):
                for k in range(KT):
                    ins = three(ps[:, 6, t * GRANK:(t + 1) * GRANK], aH[:, k, t * P:(t + 1) * P],
                                aL[:, k, t * P:(t + 1) * P], lrH[:, k, :], lrL[:, k, :], k == 0, k == KT - 1)
            ins.then_inc(lr_done, 1)
            pe.wait_ge(lr_t, 1)
            for t in range(TT):
                ins = T.transpose(ps[0:GRANK, 6, t * P:(t + 1) * P], lrt[:, t, :], ident)
            ins.then_inc(lr_T, 1)
            pe.wait_ge(lr_Tc, 1)
            pe.wait_ge(vec_in, 80)
            un = UNITS["z"]
            pe.wait_ge(acc_out, un - 1)
            for t in range(TT):
                ins = T.matmul(pair(un)[:, t, :], lrT[:, t * P:(t + 1) * P], w2[:, :], start=True, stop=True)
            ins.then_inc(acc_done, 1)
            pe.wait_ge(acc_out, un + 1)
            for j, tab in enumerate((C_TRI, C_TRS)):
                for t in range(TT):
                    ins = T.matmul(pair(UNITS["cum"] + j)[:, t, :], cst[:, tab:tab + P], la[:, t, :], start=True, stop=True)
                ins.then_inc(acc_done, 1)
            for h in range(GH):
                for t in range(TT):
                    ins = T.matmul(ps[:, 6, 4 * h + 2 * t:4 * h + 2 * t + 2], la[:, t, h * GDK:(h + 1) * GDK],
                                   cst[:, C_IND:C_IND + 2], start=True, stop=True)
            ins.then_inc(dec_sum, 1)
            for j, src in enumerate((u[:, :, 0:512], ekd[:, :, :])):
                un = UNITS["gqT"] + j
                if j == 0:
                    pe.wait_ge(g_mul, 1)
                    pe.wait_ge(acc_out, un)
                for h in range(GH):
                    for t in range(TT):
                        ins = T.transpose(pair(un)[:, h // 2, (h % 2) * S + t * P:(h % 2) * S + (t + 1) * P],
                                          src[:, t, h * GDK:(h + 1) * GDK], ident)
                ins.then_inc(acc_done, 1)
            pe.wait_ge(acc_out, UNITS["gqT"] + 2)
            for t in range(TT):
                g = GROUPS["glaA"] + t
                pe.wait_ge(t_lo, GROUPS["glaA"])
                for h in range(GH):
                    ins = T.matmul(tbank(g)[:, h * P:(h + 1) * P], qkT[:, 1, h, t * P:(t + 1) * P],
                                   qkT[:, 0, h, t * P:(t + 1) * P], start=True, stop=True)
                ins.then_inc(t_done, 1)
            pe.wait_ge(dec_exp, 1)
            for c in range(3):
                t, r0 = c // 2, GCH * (c % 2)
                for h in range(GH):
                    if GH * c + h >= 2:
                        pe.wait_ge(kv_out, GH * c + h - 1)
                    T.matmul(ps[:, 6 + h % 2, 0:GDV], ekl[r0:r0 + GCH, t, h * GDK:(h + 1) * GDK],
                             u[r0:r0 + GCH, t, 1024 + h * GDV:1024 + (h + 1) * GDV], start=True, stop=True)\
                        .then_inc(kv_done, 1)
            pe.wait_ge(kv_out, 3 * GH)
            for t in range(TT):
                un = UNITS["go"] + t
                pe.wait_ge(acc_out, un - 1)
                pe.wait_ge(t_lo, GROUPS["glaA"] + t + 1)
                for h in range(GH):
                    dst = pair(un)[:, h // 2, (h % 2) * GDV:(h % 2) * GDV + GDV]
                    ins = T.matmul(dst, aT[:, t, h, :], u[:, t, 1024 + h * GDV:1024 + (h + 1) * GDV],
                                   start=True, stop=True, skip_group_check=True)
                    for half in range(2):
                        c = 2 * t + half
                        if c == 0:
                            continue
                        ins = T.matmul(dst[GCH * half:GCH * half + GCH, :], qkT[:, 0, h, c * GCH:(c + 1) * GCH],
                                       st[:, c - 1, h, :], start=False, stop=True, skip_group_check=True)
                ins.then_inc(acc_done, 1)
            pe.wait_ge(oa_ready, 1)
            groups("oa", xn)
            rows_mm(SUBS["bra"], UNITS["bra"], aH, aL, KT, GROUPS["oa"])
            pe.wait_ge(m_norm, 1)
            for j in range(8):
                group(GROUPS["mqk"] + j, [u[:, t, 3072 + (2 * j + k) * P:3072 + (2 * j + k + 1) * P]
                                          for k in range(2) for t in range(TT)])
            pe.wait_ge(t_lo, GROUPS["mqk"] + 8)
            pe.wait_ge(acc_out, UNITS["bra"] + 2)

            def mscores(h):
                if h >= 4:
                    pe.wait_ge(m_max, h - 3)
                for t in range(TT):
                    ins = T.matmul(ps[:, h % 4, t * S:(t + 1) * S], mT[:, h, t * P:(t + 1) * P], mT[:, 8 + h, :],
                                   start=True, stop=True)
                ins.then_inc(s_max, 1)

            def mvalues(h):
                pe.wait_ge(t_lo, GROUPS["moba"] + 2 * h + 2)
                if h >= 2:
                    pe.wait_ge(m_oout, h - 1)
                vh = [u[:, k, 5120 + h * P:5120 + (h + 1) * P] for k in range(2)]
                b = 6 + h % 2
                T.matmul(ps[:, b, 0:P], pT[:, h % 2, 0, 0:P], vh[0], start=True, stop=True)
                T.matmul(ps[:, b, P:S], pT[:, h % 2, 0, P:S], vh[0], start=True, stop=False)
                T.matmul(ps[:, b, P:S], pT[:, h % 2, 1, P:S], vh[1], start=False, stop=True).then_inc(m_o, 1)

            mscores(0)
            for h in range(H):
                if h + 1 < H:
                    mscores(h + 1)
                g = GROUPS["moba"] + 2 * h
                pe.wait_ge(m_exp, h + 1)
                pe.wait_ge(t_lo, g)
                for t in range(TT):
                    ins = T.transpose(tbank(g)[:, t * P:(t + 1) * P], pe_[:, h % 2, t, 0:P], ident)
                ins.then_inc(t_done, 1)
                T.transpose(tbank(g + 1)[:, 0:P], pe_[:, h % 2, 1, P:S], ident).then_inc(t_done, 1)
                if h >= 1:
                    mvalues(h - 1)
            mvalues(H - 1)
            pe.wait_ge(m_oout, H)
            groups("ob", xn)
            rows_mm(SUBS["brb"], UNITS["brb"], aH, aL, KT, GROUPS["ob"])
            pe.wait_ge(oa_ready, 3)
            groups("y", xn)
            rows_mm(SUBS["wo2"], UNITS["wo2"], aH, aL, KT, GROUPS["y"])
            pe.wait_ge(xn_ready, 2 * TT)
            groups("rms1", xn)
            n, un, g = SUBS["up"], UNITS["up"], GROUPS["up"]

            def um(c, i=0, need=None):
                chunk_mm(n + 4 * c, i, [un + c], [X], need)

            def ut(c, i=0):
                pe.wait_ge(silu_done, 22 + c + 1 + 2 * i)
                for j in range(2):
                    group(g + 2 * c + j, [hu[:, c % 2, t, (2 * j + k) * P:(2 * j + k + 1) * P]
                                          for k in range(2) for t in range(TT)], i, step=4)

            um(0, need=GROUPS["rms1"])
            with pe.Fori(0, 3) as i:
                um(1, i)
                ut(0, i)
                um(2, i)
                ut(1, i)
            um(7)
            ut(6)
            ut(7)
            rows_mm(SUBS["down"], UNITS["down"], uH, uL, F2 // P, g)
            pe.wait_ge(xn_ready, 3 * TT)
            groups("rms2", xn)
            rows_mm(SUBS["pg"], UNITS["pg"], aH, aL, KT, GROUPS["rms2"])
            pe.wait_ge(p_in, 16)
            group(GROUPS["p"], [pt[:, t, k * P:(k + 1) * P] for k in range(2) for t in range(TT)])
            rows_mm(SUBS["ple"], UNITS["ple"], pH, pL, 2, GROUPS["p"])


_INS = ["x", "c", "ctx", "c_ctx", "w_mod", "b_mod", "ln_g", "ln_b", "attn_w_qkv", "attn_lambda", "attn_subln_g",
        "attn_w_o", "pool_w", "pool_scale", "ffn_w_in", "ffn_w_out", "p_2", "norm_mix_2", "w_in_2", "gla_gate_w2_2",
        "gla_gate_b_2", "gla_out_norm_2", "moba_q_norm_2", "moba_k_norm_2", "w_branch_a_2", "w_branch_b_2",
        "w_out_2", "norm_mlp_2", "w_up_2", "w_down_2", "norm_ple_2", "w_ple_gate_2", "w_ple_2"]


def kernel(**inputs):
    import concourse.bacc as bacc
    from concourse.bass_utils import run_bass_kernel_spmd

    nc = bacc.Bacc("TRN2", target_bir_lowering=False, num_devices=1)
    arrays, aps = {}, {}
    for name in _INS:
        arr = np.ascontiguousarray(inputs[name])
        arrays[f"in_{name}"] = arr
        aps[name] = nc.dram_tensor(f"in_{name}", arr.shape, mybir.dt.from_np(arr.dtype), kind="ExternalInput").ap()
    consts = []
    for name, arr in zip(("const_tables", "const_windows"), shape_constants()):
        arrays[name] = arr
        consts.append(nc.dram_tensor(name, arr.shape, fp32, kind="ExternalInput").ap())
    out = nc.dram_tensor("out", (1, S, D), fp32, kind="ExternalOutput").ap()
    build(nc, aps, consts[0], consts[1], out)
    r = run_bass_kernel_spmd(nc, [arrays], core_ids=[0])
    return r.results[0]["out"]
```

```python
import math
from contextlib import ExitStack

import numpy as np

import concourse.bass as bass
from concourse import mybir

fp32 = mybir.dt.float32
f32r = mybir.dt.float32r
ALU = mybir.AluOpType
ACT = mybir.ActivationFunctionType
AXX = mybir.AxisListType.X

P = 128
D = 1024
KT = D // P
S = 256
TT = S // P
F1 = 2816
F2 = 4096
H = 8
GH, GDK, GDV, GCH, GRANK = 4, 128, 256, 64, 16
ALPHA = 4.0 ** 0.25
LN_EPS, RMS_EPS = 1e-5, 1e-6
LAM_INIT = 0.8 - 0.6 * math.exp(0.0)
POOL_WINDOWS = (2, 4, 8, 16)
N_IN = 8208
LR0 = 2 * GH * GDK + GH * GDV
CW = 512

RAW, WS = 4, 4

SUBS = {}
_n = 0
for _name, _count in (("qkv", 24), ("wo", 8), ("in0", 44), ("out0", 22), ("pool", 2), ("in1", 44), ("out1", 22),
                      ("win", 64), ("bra", 8), ("brb", 8), ("wo2", 8), ("up", 32), ("down", 32), ("pg", 8),
                      ("ple", 2)):
    SUBS[_name] = _n
    _n += _count
NSUB = _n

UNITS = {}
_n = 0
for _name, _count in (("q", 2), ("k", 4), ("v", 4), ("att", 16), ("wo", 2), ("in0", 11), ("out0", 2), ("pool", 2),
                      ("in1", 11), ("out1", 2), ("win", 16),
                      ("bra", 2), ("brb", 2), ("wo2", 2), ("up", 8), ("down", 2), ("pg", 2), ("ple", 2)):
    UNITS[_name] = _n
    _n += _count

GROUPS = {}
_n = 0
for _name, _count in (("x", 4), ("ctx", 4), ("q", 4), ("k", 8), ("att", 16), ("o", 4), ("x1", 4), ("in0", 11),
                      ("pool", 4), ("x3", 4), ("in1", 11), ("rms0", 4), ("glaA", 2), ("mqk", 8), ("oa", 4),
                      ("ob", 4), ("y", 4), ("rms1", 4), ("up", 16), ("rms2", 4), ("p", 1)):
    GROUPS[_name] = _n
    _n += _count

MODS = [(0, m) for m in range(12)] + [(1, m) for m in (6, 7, 8, 9)] + [(1, m) for m in (0, 1, 2, 3, 4, 5, 10, 11)]
MOD_WHICH = {0: 0, 1: 1, 3: 2, 4: 3}
NMOD0 = 4


MODPLAN = {}
for _m, _c, _s, _s2 in ((4, 1, 0, 2), (5, 2, 0, 1), (6, 3, 0, 1), (7, 4, 0, 1), (8, 5, 0, 1)):
    MODPLAN.setdefault((_c, _s), []).append(("sum", _m))
    MODPLAN.setdefault((_c, _s2), []).append(("select", _m))


def mod_sum_in(r):
    return r % 2 == 1 and r <= 13


def mod_is_column(layer, m):
    return m // 2 in (3, 4) or (layer == 0 and m // 2 < 2)


C_ID, C_SELC, C_SELB, C_COS, C_SIN, C_DIST, C_TRI, C_TRS, C_IND, C_END = np.cumsum(
    [0, 128, 2, 128, 64, 64, 512, 128, 128, 2]).tolist()


def shape_constants():
    c = np.zeros((P, C_END), np.float32)
    p = np.arange(P)
    c[:, C_ID:C_ID + P] = np.eye(P)
    for r in range(2):
        c[p % 32 == r, C_SELC + r] = 1.0
    c[p % 32 == 0, C_SELB:C_SELB + P] = 1.0
    row = np.repeat(np.arange(S // 64, dtype=np.float32), 64)
    col = np.tile(np.arange(64, dtype=np.float32), S // 64)
    inv = np.power(np.float32(10000.0), -np.arange(16, dtype=np.float32) / np.float32(16))
    ang = np.concatenate([row[:, None] * inv, col[:, None] * inv], axis=-1).astype(np.float32)
    c[:, C_COS:C_SIN] = np.cos(ang).reshape(TT, P, 32).transpose(1, 0, 2).reshape(P, 64)
    c[:, C_SIN:C_DIST] = np.sin(ang).reshape(TT, P, 32).transpose(1, 0, 2).reshape(P, 64)
    q = np.arange(S)[:, None]
    k = np.arange(S)[None, :]
    dist = np.where(k <= q, (k - q).astype(np.float32), np.float32(-1e30))
    c[:, C_DIST:C_TRI] = dist.reshape(TT, P, S).transpose(1, 0, 2).reshape(P, TT * S)
    same = (p[:, None] // GCH) == (p[None, :] // GCH)
    c[:, C_TRI:C_TRS] = np.where(same & (p[:, None] <= p[None, :]), 1.0 / 16.0, 0.0)
    c[:, C_TRS:C_IND] = np.where(same & (p[:, None] > p[None, :]), 1.0 / 16.0, 0.0)
    for j in range(2):
        c[p // GCH == j, C_IND + j] = 1.0 / 16.0
    w = np.zeros((TT, P, 4, S), np.float32)
    t = np.arange(S)
    for g, win in enumerate(POOL_WINDOWS):
        lo = np.clip(t - win // 2, 0, S)
        hi = np.clip(t + win - win // 2, 0, S)
        m = ((t[:, None] >= lo[None, :]) & (t[:, None] < hi[None, :])).astype(np.float32)
        m = m / (hi - lo).astype(np.float32)[None, :] - np.eye(S, dtype=np.float32)
        w[:, :, g, :] = m.reshape(TT, P, S)
    return c, w.transpose(1, 0, 2, 3).reshape(P, TT * 4 * S).copy()


SUB_OF = (("q", "qkv", 4, 0), ("k", "qkv", 4, 8), ("v", "qkv", 4, 16), ("wo", "wo", 0, 4), ("in0", "in0", 4, 0),
          ("out0", "out0", 0, 18), ("pool", "pool", 0, -2), ("in1", "in1", 4, 0), ("out1", "out1", 0, 18),
          ("win", "win", 4, 0), ("bra", "bra", 0, 4), ("brb", "brb", 0, 4), ("wo2", "wo2", 0, 4), ("up", "up", 4, 0),
          ("down", "down", 0, 28), ("pg", "pg", 0, 4), ("ple", "ple", 0, -2))


def summed(stage, j=0):
    _, subs, per, off = next(e for e in SUB_OF if e[0] == stage)
    if stage in ("k", "v"):
        j //= 2
    return SUBS[subs] + off + 4 + per * j


def at_least(eng, sem, value):
    if isinstance(value, int) and value <= 0:
        return
    eng.wait_ge(sem, value)


def build(nc, a, cst_d, pool_d, out):
    ctx = ExitStack()
    with ctx:
        def sem(name):
            return ctx.enter_context(nc.semaphore(name))

        def sb(stack, name, shape, dt=fp32):
            return stack.enter_context(nc.sbuf_tensor(name, shape, dt))

        raw = sb(ctx, "raw", [P, RAW, 2048])
        wH = sb(ctx, "wH", [P, WS, 1024], f32r)
        wL = sb(ctx, "wL", [P, WS, 1024], f32r)
        aH = sb(ctx, "aH", [P, KT, S], f32r)
        aL = sb(ctx, "aL", [P, KT, S], f32r)
        x = sb(ctx, "x", [P, TT, D])
        cst = sb(ctx, "cst", [P, C_END])
        stat = sb(ctx, "stat", [P, 64])
        eps = sb(ctx, "eps", [P, 2])
        bn = sb(ctx, "bn", [P, TT, 12])
        mv = sb(ctx, "mv", [P, TT, 2])
        rows2 = sb(ctx, "rows2", [34, P])
        gcol = sb(ctx, "gcol", [P, 34])
        lrw = sb(ctx, "lrw", [P, KT, GRANK])
        ps = ctx.enter_context(nc.psum_tensor("ps", [P, 8, 512], fp32))
        ident = cst[:, C_ID:C_ID + P]

        sA = ExitStack()
        lnp = sb(sA, "lnp", [P, 2, D])
        tf = sb(sA, "tf", [P, 2, 512])
        ro = lnp[:, :, :].rearrange("p u (t c) -> p u t c", t=TT)
        te = tf[:, 0, :]
        modraw = sb(sA, "modraw", [P, 2, 2048])
        modrow = sb(sA, "modrow", [P, 512])
        modcol = sb(sA, "modcol", [P, 2, 4, KT, 2])
        bcol = sb(sA, "bcol", [P, 96])
        rows = sb(sA, "rows", [113, P])
        cT = sb(sA, "cT", [P, KT, 32])
        lamt = sb(sA, "lamt", [P, 256])
        lam2 = sb(sA, "lam2", [P, 8])
        subg = sb(sA, "subg", [P, 2])
        g1b = sb(sA, "g1b", [P, D])
        g2b0 = sb(sA, "g2b0", [P, D])
        sAtt = ExitStack()
        v = sb(sAtt, "v", [P, 4, D])
        qz = sb(sAtt, "qz", [P, H, 2, S])
        kT = sb(sAtt, "kT", [P, H, 512])
        sPrj = ExitStack()
        cH = sb(sPrj, "cH", [P, KT, S], f32r)
        cL = sb(sPrj, "cL", [P, KT, S], f32r)
        rt = sb(sPrj, "rt", [P, 2, TT, 512])
        sPrj.close()
        sCore = ExitStack()
        ex = sb(sCore, "ex", [P, 2, 2, 512])
        am = sb(sCore, "am", [P, 2, 512])
        at = sb(sCore, "at", [P, 2, 4, P])
        ot = sb(sCore, "ot", [P, TT, D])
        sCore.close()
        sAtt.close()
        sIni = ExitStack()
        mod0 = sb(sIni, "mod0", [P, 2 * NMOD0, 2048])
        sIni.close()
        sL1 = ExitStack()
        g2b1 = sb(sL1, "g2b1", [P, D])
        sh1b = sb(sL1, "sh1b", [P, D])
        sc1b = sb(sL1, "sc1b", [P, D])
        psb = sb(sL1, "psb", [P, D])
        sF = ExitStack()
        hH = sb(sF, "hH", [P, F1 // P, S], f32r)
        hL = sb(sF, "hL", [P, F1 // P, S], f32r)
        sil = sb(sF, "sil", [P, 2, TT, 256])
        hid = sb(sF, "hid", [P, 2, TT, 256])
        sF.close()
        sP = ExitStack()
        poolm = sb(sP, "poolm", [P, TT, 4, S])
        hm = sb(sP, "hm", [P, TT, D])
        sP.close()
        sL1.close()
        sA.close()

        sB = ExitStack()
        xn = sb(sB, "xn", [P, TT, D])
        sM = ExitStack()
        u = sb(sM, "u", [P, TT, 8192])
        lrH = sb(sM, "lrH", [P, KT, GRANK], f32r)
        lrL = sb(sM, "lrL", [P, KT, GRANK], f32r)
        lrt = sb(sM, "lrt", [P, TT, GRANK])
        lrT = sb(sM, "lrT", [GRANK, S])
        w2 = sb(sM, "w2", [GRANK, 512])
        gbb = sb(sM, "gbb", [P, 512])
        mst = sb(sM, "mst", [P, 2, TT, 16])
        sG = ExitStack()
        la, lt = xn[:, :, 0:512], xn[:, :, 512:D]
        ekd = sb(sG, "ekd", [P, TT, 512])
        ekl = sb(sG, "ekl", [P, TT, 512])
        qkT = sb(sG, "qkT", [P, 2, GH, S])
        aT = ekd[:, :, :].rearrange("p t (h c) -> p t h c", h=GH)
        st = sb(sG, "st", [P, 3, GH, GDV])
        dec = sb(sG, "dec", [P, GH, TT, 2])
        sG.close()
        sQ = ExitStack()
        mT = sb(sQ, "mT", [P, 16, S])
        sc = sb(sQ, "sc", [P, 2, TT, S])
        pe_ = sb(sQ, "pe_", [P, 2, TT, S])
        pT = sb(sQ, "pT", [P, 2, 3 * P])
        sQ.close()
        sM.close()
        sU = ExitStack()
        uH = sb(sU, "uH", [P, F2 // P, S], f32r)
        uL = sb(sU, "uL", [P, F2 // P, S], f32r)
        hu = sb(sU, "hu", [P, 2, TT, 512])
        sU.close()
        sE = ExitStack()
        pt = sb(sE, "pt", [P, TT, 256])
        pH = sb(sE, "pH", [P, 2, S], f32r)
        pL = sb(sE, "pL", [P, 2, S], f32r)
        gate = sb(sE, "gate", [P, TT, D])
        sE.close()
        sB.close()

        gsq = st[:, 0:2, :, :].rearrange("p t h e -> p (t h) e")
        w_raw = [sem(f"w_raw{i}") for i in range(RAW)]
        w_hi, w_lo, w_used = sem("w_hi"), sem("w_lo"), sem("w_used")
        acc_done, acc_out = sem("acc_done"), sem("acc_out")
        t_done, t_f, t_hi, t_lo = sem("t_done"), sem("t_f"), sem("t_hi"), sem("t_lo")
        x_in, ctx_in, rows_in, cst_in = sem("x_in"), sem("ctx_in"), sem("rows_in"), sem("cst_in")
        small_in = sem("small_in")
        mod0_in = [sem(f"mod0_in{i}") for i in range(NMOD0)]
        mod_in = [sem(f"mod_in{i}") for i in range(2)]
        mod_used, mod_acc, mod_row, mod_sel, mod_out = (sem(n) for n in
                                                        ("mod_used", "mod_acc", "mod_row", "mod_sel", "mod_out"))
        bias0_in, bias1_in, pscale_in = sem("bias0_in"), sem("bias1_in"), sem("pscale_in")
        rows_T, cT_zero, cT_ready, qz_zero = sem("rows_T"), sem("cT_zero"), sem("cT_ready"), sem("qz_zero")
        lam_sum, lam_exp = sem("lam_sum"), sem("lam_exp")
        s_max, s_exp, o_done, o_out = (sem(n) for n in ("s_max", "s_exp", "o_done", "o_out"))
        o_sq, o_sd, o_norm = sem("o_sq"), sem("o_sd"), sem("o_norm")
        ln_in, ln_var, ln_sd, ln_x = sem("ln_in"), sem("ln_var"), sem("ln_sd"), sem("ln_x")
        silu_done = sem("silu_done")
        pool_in, pool_h = sem("pool_in"), sem("pool_h")
        act_self, dve_self, pool_self = sem("act_self"), sem("dve_self"), sem("pool_self")
        rms_sq, rms_ms, rms_sd, xn_ready = sem("rms_sq"), sem("rms_ms"), sem("rms_sd"), sem("xn_ready")
        rows2_in, rows2_T, gcol_ready = sem("rows2_in"), sem("rows2_T"), sem("gcol_ready")
        lrw_in, lr_hi, lr_lo, lr_done, lr_t, lr_T, lr_Tc = (sem(n) for n in
                                                           ("lrw_in", "lr_hi", "lr_lo", "lr_done", "lr_t", "lr_T", "lr_Tc"))
        vec_in = sem("vec_in")
        z_abs, z_ln, la_ready, dec_sum, dec_exp, e_ready, g_mul = (sem(n) for n in
                                                                  ("z_abs", "z_ln", "la_ready", "dec_sum", "dec_exp", "e_ready", "g_mul"))
        z_done, cum_done, gT_done, gT_out = sem("z_done"), sem("cum_done"), sem("gT_done"), sem("gT_out")
        a_evac, kv_done, kv_out = sem("a_evac"), sem("kv_done"), sem("kv_out")
        go_done, go_evac, go_sq, go_sum, go_sd = (sem(n) for n in ("go_done", "go_evac", "go_sq", "go_sum", "go_sd"))
        oa_ready = sem("oa_ready")
        m_sq, m_sum, m_sd, m_norm = sem("m_sq"), sem("m_sum"), sem("m_sd"), sem("m_norm")
        m_scores, m_max, m_exp, m_T, m_Tc = (sem(n) for n in ("m_scores", "m_max", "m_exp", "m_T", "m_Tc"))
        m_o, m_oout = sem("m_o"), sem("m_oout")
        p_in, gate_done, x_done, out_done = sem("p_in"), sem("gate_done"), sem("x_done"), sem("out_done")

        def pair(un):
            b = 2 * (un % 2)
            return ps[:, b:b + 2, :]

        def side(j):
            return ps[:, 6:8, :] if j == 0 else ps[:, 4:6, :]

        def tbank(g):
            return ps[:, 4 + g % 2, :]

        block = ctx.enter_context(nc.Block())

        @block.sync
        def _(sp):
            def piece(n, i, parts):
                slot = (n // 2) % RAW
                at_least(sp, w_lo, n - 2 * RAW + 2 + 8 * i if n >= 2 * RAW or not isinstance(i, int) else 0)
                for (lo, hi), src in parts:
                    shape = src.shape
                    dst = raw[:, slot, :].rearrange("p (k c) -> p k c", k=shape[1])[:, :, lo:hi]
                    sp.dma_start(dst, src).then_inc(w_raw[slot], 32 // len(parts))

            def by_k(w):
                return w.rearrange("(k p) n -> p k n", p=P)

            def chunk(n, i, w, c0):
                for h in range(2):
                    piece(n + 4 * 0 + 2 * h, i, [((0, CW), by_k(w)[:, 4 * h:4 * h + 4, bass.ds(c0, CW)])])

            def rows_of(n, w, k0, kn):
                for k in range(k0, k0 + kn, 2):
                    piece(n + k - k0, 0, [((0, D), by_k(w)[:, k:k + 2, :])])

            sp.dma_start(rows[96:104, :], a["c"].rearrange("b (r p) -> (b r) p", p=P)).then_inc(rows_in, 16)
            sp.dma_start(rows[104:112, :], a["c_ctx"].rearrange("(r p) -> r p", p=P)).then_inc(rows_in, 16)
            sp.dma_start(rows[0:96, :], a["b_mod"].rearrange("l (r p) -> (l r) p", p=P)).then_inc(rows_in, 16)
            sp.dma_start(rows[112:113, :], a["attn_subln_g"]).then_inc(rows_in, 16)
            sp.dma_start(cst[:, :], cst_d).then_inc(cst_in, 16)
            for m in range(NMOD0):
                sp.dma_start(mod0[:, 2 * m:2 * m + 2, :].rearrange("p h (k c) -> p (h k) c", k=4),
                             by_k(a["w_mod"][0])[:, :, m * CW:(m + 1) * CW]).then_inc(mod0_in[m], 16)
            sp.dma_start(x[:, :, :], a["x"].rearrange("b (t p) d -> p (b t) d", p=P)).then_inc(x_in, 16)
            for c in range(6):
                chunk(SUBS["qkv"] + 4 * c, 0, a["attn_w_qkv"][0], c * CW)
                if c == 0:
                    sp.dma_start(lnp[:, :, :], a["ctx"].rearrange("b (t p) d -> p (b t) d", p=P)).then_inc(ctx_in, 16)
            rows_of(SUBS["wo"], a["attn_w_o"][0], 0, KT)

            def swiglu_chunk(n, i, w, c0):
                for h in range(2):
                    wk = by_k(w)[:, 4 * h:4 * h + 4, :]
                    piece(n + 2 * h, i, [((256 * s, 256 * s + 256), wk[:, :, bass.ds(c0 + s * F1, 256)])
                                         for s in range(2)])

            def swiglu(layer):
                n = SUBS[f"in{layer}"]
                swiglu_chunk(n, 0, a["ffn_w_in"][layer], 0)
                with sp.Fori(0, 5) as i:
                    for j in range(2):
                        swiglu_chunk(n + 4 + 4 * j, i, a["ffn_w_in"][layer], i * 512 + (256 + 256 * j))
                rows_of(SUBS[f"out{layer}"], a["ffn_w_out"][layer], 0, F1 // P)

            swiglu(0)
            slot = (SUBS["pool"] // 2) % RAW
            sp.wait_ge(w_lo, SUBS["pool"] - 2 * RAW + 2)
            sp.dma_start(raw[:, slot, :].rearrange("p (g c) -> p g c", g=8),
                         a["pool_w"][0].rearrange("g (k p) o -> p (g k) o", p=P)).then_inc(w_raw[slot], 32)
            swiglu(1)
            n = SUBS["win"]
            with sp.Fori(0, 2) as i:
                for j in range(2):
                    chunk(n + 4 * j, i, a["w_in_2"][0], i * (2 * CW) + j * CW)
            with sp.Fori(0, 6) as i:
                for j in range(2):
                    chunk(n + 16 + 4 * j, i, a["w_in_2"][0], i * (2 * CW) + (LR0 + GRANK + j * CW))
            rows_of(SUBS["bra"], a["w_branch_a_2"][0], 0, KT)
            rows_of(SUBS["brb"], a["w_branch_b_2"][0], 0, KT)
            rows_of(SUBS["wo2"], a["w_out_2"][0], 0, KT)
            n = SUBS["up"]
            with sp.Fori(0, 4) as i:
                for j in range(2):
                    chunk(n + 4 * j, i, a["w_up_2"][0], i * (2 * CW) + j * CW)
            rows_of(SUBS["down"], a["w_down_2"][0], 0, F2 // P)
            rows_of(SUBS["pg"], a["w_ple_gate_2"][0], 0, KT)
            rows_of(SUBS["ple"], a["w_ple_2"][0], 0, 2)
            for t in range(TT):
                sp.wait_ge(x_done, t + 1)
                sp.dma_start(out[0, t * P:(t + 1) * P, :], x[:, t, :]).then_inc(out_done, 16)
            sp.wait_ge(out_done, 16 * TT)

        @block.gpsimd
        def _(pool):
            nc.gpsimd.memset(cT[:, :, :], 0.0).then_inc(cT_zero, 1)
            pool.wait_ge(mod0_in[2], 16)
            pool.dma_start(lamt[:, :], a["attn_lambda"].rearrange("a l d -> a (l d)").to_broadcast([P, 256]))\
                .then_inc(small_in, 16)
            pool.dma_start(g1b[:, :], a["b_mod"][0:1, 2 * D:3 * D].to_broadcast([P, D])).then_inc(bias0_in, 16)
            pool.dma_start(g2b0[:, :], a["b_mod"][0:1, 5 * D:6 * D].to_broadcast([P, D])).then_inc(bias0_in, 16)

            for j, nm in enumerate(("norm_mix_2", "norm_mlp_2", "norm_ple_2")):
                pool.dma_start(rows2[8 * j:8 * j + 8, :], a[nm].rearrange("l (r p) -> (l r) p", p=P))\
                    .then_inc(rows2_in, 16)
            pool.dma_start(rows2[24:32, :], a["gla_out_norm_2"].rearrange("l h (r p) -> (l h r) p", p=P)).then_inc(rows2_in, 16)
            pool.dma_start(rows2[32:33, :], a["moba_k_norm_2"]).then_inc(rows2_in, 16)
            pool.dma_start(rows2[33:34, :], a["moba_q_norm_2"]).then_inc(rows2_in, 16)
            with nc.allow_non_contiguous_dma(reason="16 columns of w_in"):
                pool.dma_start(lrw[:, :, :], a["w_in_2"][0].rearrange("(k p) n -> p k n", p=P)[:, :, LR0:LR0 + GRANK])\
                    .then_inc(lrw_in, 16)

            def mod_load(c):
                layer, m = MODS[c]
                wk = a["w_mod"][layer].rearrange("(k p) n -> p k n", p=P)
                for h in range(2):
                    if c > NMOD0:
                        pool.wait_ge(mod_used, 2 * (c - NMOD0 - 1) + h + 1)
                    pool.dma_start(modraw[:, h, :].rearrange("p (k c) -> p k c", k=4),
                                   wk[:, 4 * h:4 * h + 4, m * CW:(m + 1) * CW]).then_inc(mod_in[h], 16)

            def ln_load(k):
                if k == 0:
                    pool.wait_ge(t_done, GROUPS["k"] + 8)
                else:
                    pool.wait_ge(ln_x, TT * k)
                for j, w in enumerate((a["ln_g"], a["ln_b"])):
                    pool.dma_start(lnp[:, j, :], w[k // 2, k % 2:k % 2 + 1, :].to_broadcast([P, D])).then_inc(ln_in, 16)

            mod_load(NMOD0)
            pool.wait_ge(mod_acc, NMOD0)
            nc.gpsimd.memset(qz[:, :, :, :], 0.0).then_inc(qz_zero, 1)
            for c in range(NMOD0 + 1, 16):
                mod_load(c)
                if c == 10:
                    ln_load(0)
            ln_load(1)
            for dst, j in ((sh1b, 0), (sc1b, 1), (g1b, 2), (g2b1, 5)):
                pool.dma_start(dst[:, :], a["b_mod"][1:2, j * D:(j + 1) * D].to_broadcast([P, D])).then_inc(bias1_in, 16)
            pool.dma_start(psb[:, :], a["pool_scale"].to_broadcast([P, D])).then_inc(pscale_in, 16)
            for c in range(16, 24):
                mod_load(c)
            ln_load(2)
            pool.dma_start(poolm[:, :, :, :].rearrange("p t g s -> p (t g s)"), pool_d).then_inc(pool_in, 16)
            ln_load(3)
            pool.wait_ge(ln_x, TT * 4)
            pool.dma_start(w2[:, :], a["gla_gate_w2_2"][0]).then_inc(vec_in, 16)
            pool.dma_start(gbb[:, :], a["gla_gate_b_2"].to_broadcast([P, 512])).then_inc(vec_in, 16)
            for t in range(TT):
                pool.wait_ge(a_evac, t + 1)
                nc.gpsimd.affine_select(out=aT[:, t, :, :], in_=aT[:, t, :, :], compare_op=ALU.is_ge, fill=0.0,
                                        base=0, pattern=[[0, GH], [1, P]], channel_multiplier=-1).then_inc(pool_self, 1)
                pool.wait_ge(pool_self, t + 1)
                nc.gpsimd.memset(aT[0:GCH, t, :, GCH:P], 0.0).then_inc(t_lo, 1)
            pool.wait_ge(w_used, summed("down"))
            pool.dma_start(pt[:, :, :], a["p_2"][0, 0].rearrange("(t p) d -> p t d", p=P)).then_inc(p_in, 16)

        @block.scalar
        def _(act):
            links = [0]

            def link(ins):
                links[0] += 1
                ins.then_inc(act_self, 1)
                act.wait_ge(act_self, links[0])

            def adv(n, i=0):
                if n >= NSUB:
                    return
                if n % 2 == 0:
                    act.wait_ge(w_raw[(n // 2) % RAW], 32 * (n // 8 + 1) + 32 * i)
                at_least(act, w_used, n - WS + 1 + 8 * i)
                nc.scalar.activation(wH[:, n % WS, :], raw[:, (n // 2) % RAW, (n % 2) * 1024:(n % 2) * 1024 + 1024],
                                     ACT.Copy).then_inc(w_hi, 1)

            def hi(g, dst, i=0, gain=None, mod=None, step=2):
                act.wait_ge(t_done, g + 1 + step * i)
                src = tbank(g).rearrange("p (k s) -> p k s", k=2)
                if gain is not None:
                    for k in range(2):
                        ins = nc.scalar.activation(dst[:, k, :], src[:, k, :], ACT.Copy, scale=gain[:, k:k + 1])
                elif mod is not None:
                    shift, scale = mod
                    tmp = tf[:, g % 2, :].rearrange("p (k s) -> p k s", k=2)
                    for k in range(2):
                        ins = nc.scalar.activation(tmp[:, k, :], src[:, k, :], ACT.Identity,
                                                   bias=shift[:, k:k + 1], scale=scale[:, k:k + 1])
                    link(ins)
                    ins = nc.scalar.activation(dst, tmp, ACT.Copy)
                else:
                    ins = nc.scalar.activation(dst, src, ACT.Copy)
                ins.then_inc(t_hi, 1)

            def modulated(layer, which, stream):
                c = modcol[:, layer, :, :, :]
                return lambda j: (c[:, which, 2 * j:2 * j + 2, stream], c[:, which + 1, 2 * j:2 * j + 2, stream])

            def mod_copy(c):
                if c < NMOD0:
                    act.wait_ge(mod_acc, c + 1)
                else:
                    act.wait_ge(mod_used, 2 * (c - NMOD0) + 2)
                nc.scalar.activation(modrow[:, :], ps[:, c if c < NMOD0 else 7, :], ACT.Copy).then_inc(mod_row, 1)

            def root(dst, src, done, cond, value):
                act.wait_ge(cond, value)
                nc.scalar.activation(dst, src, ACT.Sqrt).then_inc(done, 1)

            act.wait_ge(rows_T, 1)
            act.wait_ge(cT_zero, 1)
            nc.scalar.activation(cT[:, :, 0:2].rearrange("p k r -> p r k"),
                                 ps[:, 6, 96:112].rearrange("p (r k) -> p r k", r=2), ACT.Silu).then_inc(cT_ready, 1)
            nc.scalar.activation(subg[:, :], ps[:, 6, 112:113].to_broadcast([P, 2]), ACT.Copy, scale=1.0 - LAM_INIT)
            nc.scalar.activation(bcol[:, :], ps[:, 6, 0:96], ACT.Copy).then_inc(cT_ready, 1)
            for c in range(NMOD0):
                if c:
                    act.wait_ge(mod_sel, c)
                mod_copy(c)
            act.wait_ge(mod_out, NMOD0)
            mc = modulated(0, 0, 0)
            for j in range(4):
                hi(GROUPS["x"] + j, aH[:, 2 * j:2 * j + 2, :], mod=mc(j))
                adv(j)

            n = SUBS["qkv"]
            modc = [NMOD0]

            def next_mod():
                act.wait_ge(mod_sel, modc[0])
                mod_copy(modc[0])
                modc[0] += 1

            def mod_at(c, sub):
                for kind, m in MODPLAN.get((c, sub), ()):
                    if kind == "sum":
                        act.wait_ge(mod_sel, m)
                        mod_copy(m)
                        modc[0] = m + 1

            def heads_out(c):
                if c < 2:
                    for j in range(2):
                        g = GROUPS["q"] + 2 * c + j
                        act.wait_ge(t_done, g + 1)
                        if c == 0 and j == 0:
                            act.wait_ge(qz_zero, 1)
                        src = tbank(g).rearrange("p (h s) -> p h s", h=2)
                        for m in range(2):
                            ins = nc.scalar.activation(qz[64 * m:64 * m + 64, 4 * c + 2 * j:4 * c + 2 * j + 2, m, :],
                                                       src[64 * m:64 * m + 64, :, :], ACT.Copy)
                        ins.then_inc(t_lo, 1)
                else:
                    for j in range(4):
                        g = GROUPS["k"] + 4 * (c - 2) + j
                        act.wait_ge(t_done, g + 1)
                        h0 = 4 * (c - 2) + 2 * (j % 2)
                        nc.scalar.activation(kT[:, h0:h0 + 2, (j // 2) * 256:(j // 2) * 256 + 256],
                                             tbank(g).rearrange("p (h s) -> p h s", h=2), ACT.Copy).then_inc(t_lo, 1)

            for c in range(6):
                for j in range(3):
                    adv(n + 4 * c + 4 + j)
                    mod_at(c, j)
                if c == 0:
                    mc = modulated(0, 0, 1)
                    for j in range(4):
                        hi(GROUPS["ctx"] + j, cH[:, 2 * j:2 * j + 2, :], mod=mc(j))
                if c == 4:
                    act.wait_ge(lam_sum, 1)
                    nc.scalar.activation(lam2[:, 2:4], lam2[:, 0:2], ACT.Exp).then_inc(lam_exp, 1)
                if c >= 4:
                    un = UNITS["k"] + 2 * (c - 2)
                    for j in range(2):
                        act.wait_ge(w_used, summed("v", 2 * (c - 4)))
                        nc.scalar.activation(v[:, 2 * j:2 * j + 2, (c - 4) * CW:(c - 3) * CW], pair(un + j),
                                             ACT.Copy).then_inc(acc_out, 1)
                adv(n + 4 * c + 7)
                mod_at(c, 3)
                if 1 <= c <= 4:
                    heads_out(c - 1)

            def exps(r):
                un = UNITS["att"] + r
                act.wait_ge(s_max, r + 1)
                if r >= 2:
                    act.wait_ge(acc_out, UNITS["att"] + r - 1)
                for m in range(2):
                    ins = nc.scalar.activation(ex[:, r % 2, m, :], pair(un)[:, m, :], ACT.Exp,
                                               bias=stat[:, 8 * (r % 2) + m:8 * (r % 2) + m + 1], scale=0.125,
                                               accum_out=stat[:, 8 * (r % 2) + 2 + m:8 * (r % 2) + 3 + m])
                ins.then_inc(s_exp, 1)

            def square(r):
                h, t = r // 2, r % 2
                act.wait_ge(o_out, r + 1)
                at_least(act, o_sq, r)
                nc.scalar.activation(tf[:, 1, 0:P], ot[:, t, h * P:(h + 1) * P], ACT.Square,
                                     accum_out=stat[:, 16 + 8 * t + h:17 + 8 * t + h]).then_inc(o_sq, 1)

            exps(0)
            for r in range(16):
                if r < 15:
                    exps(r + 1)
                g = GROUPS["att"] + r
                act.wait_ge(t_done, g + 1)
                if r >= 2:
                    act.wait_ge(o_done, r - 1)
                nc.scalar.activation(at[:, r % 2, :, :], tbank(g).rearrange("p (k q) -> p k q", k=4),
                                     ACT.Copy).then_inc(t_lo, 1)
                if r >= 2:
                    square(r - 2)
                if mod_sum_in(r):
                    next_mod()
            for t in range(TT):
                square(14 + t)
                act.wait_ge(o_sq, 15 + t)
                nc.scalar.activation(stat[:, 32 + 8 * t:40 + 8 * t], stat[:, 16 + 8 * t:24 + 8 * t], ACT.Sqrt,
                                     bias=eps[:, 0:1], scale=1.0 / P).then_inc(o_sd, 1)
            for j in range(4):
                hi(GROUPS["o"] + j, aH[:, 2 * j:2 * j + 2, :], gain=subg)
            for j in range(8):
                adv(SUBS["wo"] + 4 + j)
            act.wait_ge(rows2_T, 1)
            nc.scalar.activation(gcol[:, 0:33], ps[:, 6, 0:33], ACT.Copy)
            nc.scalar.activation(gcol[:, 33:34], ps[:, 6, 33:34], ACT.Copy, scale=P ** -0.5).then_inc(gcol_ready, 1)

            def ln(k):
                for t in range(TT):
                    act.wait_ge(ln_var, TT * k + t + 1)
                    nc.scalar.activation(stat[:, 52 + t:53 + t], mv[:, t, 1:2], ACT.Sqrt, bias=eps[:, 0:1])\
                        .then_inc(ln_sd, 1)

            def swiglu(layer):
                n, un, g = SUBS[f"in{layer}"], UNITS[f"in{layer}"], GROUPS[f"in{layer}"]

                def one(c, i=0, first=False):
                    for j in range(3):
                        adv(n + 4 * c + 4 + j, i)
                    act.wait_ge(w_used, summed(f"in{layer}", c) + 8 * i)
                    nc.scalar.activation(sil[:, c % 2, :, :], pair(un + c)[:, :, 0:256], ACT.Silu).then_inc(silu_done, 1)
                    adv(n + 4 * c + 7, i)
                    if not first:
                        k0 = 2 * (c - 1) + 4 * i
                        hi(g + c - 1, hH[:, bass.ds(k0, 2), :] if not isinstance(i, int) else hH[:, k0:k0 + 2, :], i)

                one(0, first=True)
                with act.Fori(0, 5) as i:
                    one(1, i)
                    one(2, i)
                hi(g + 10, hH[:, 20:22, :])
                for k in range(F1 // P):
                    adv(SUBS[f"out{layer}"] + 4 + k)
                    if layer == 0 and k % 2 == 0 and k < 16:
                        next_mod()

            ln(0)
            mc = modulated(0, 2, 0)
            for j in range(4):
                hi(GROUPS["x1"] + j, aH[:, 2 * j:2 * j + 2, :], mod=mc(j))
            swiglu(0)
            ln(1)
            for j in range(4):
                hi(GROUPS["pool"] + j, aH[:, 2 * j:2 * j + 2, :])
            for j in range(2):
                adv(SUBS["pool"] + 4 + j)
            ln(2)
            mc = modulated(1, 2, 0)
            for j in range(4):
                hi(GROUPS["x3"] + j, aH[:, 2 * j:2 * j + 2, :], mod=mc(j))
            swiglu(1)
            ln(3)

            def rms(k, after, value):
                act.wait_ge(after, value)
                for t in range(TT):
                    nc.scalar.activation(xn[:, t, :], x[:, t, :], ACT.Square,
                                         accum_out=stat[:, 56 + t:57 + t]).then_inc(rms_sq, 1)
                root(stat[:, 60:62], stat[:, 58:60], rms_sd, rms_ms, k + 1)

            def gained(k, dst, name):
                for j in range(4):
                    hi(GROUPS[name] + j, dst[:, 2 * j:2 * j + 2, :], gain=gcol[:, 8 * k + 2 * j:8 * k + 2 * j + 2])

            rms(0, ln_x, 8)
            act.wait_ge(gcol_ready, 1)
            gained(0, aH, "rms0")
            act.wait_ge(lrw_in, 16)
            nc.scalar.activation(lrH[:, :, :], lrw[:, :, :], ACT.Copy).then_inc(lr_hi, 1)
            n, un = SUBS["win"], UNITS["win"]

            def beside(c, j):
                if (c, j) == (2, 0):
                    act.wait_ge(lr_done, 1)
                    nc.scalar.activation(lrt[:, :, :], ps[:, 6, 0:TT * GRANK].rearrange("p (t r) -> p t r", t=TT),
                                         ACT.Copy).then_inc(lr_t, 1)
                elif (c, j) == (3, 0):
                    act.wait_ge(lr_T, 1)
                    nc.scalar.activation(lrT[:, :], ps[0:GRANK, 6, 0:S], ACT.Copy).then_inc(lr_Tc, 1)
                elif (c, j) == (4, 1):
                    act.wait_ge(z_abs, 1)
                    link(nc.scalar.activation(lt, lt, ACT.Exp, scale=-1.0))
                    nc.scalar.activation(lt, lt, ACT.Ln, bias=1.0).then_inc(z_ln, 1)
                elif (c, j) == (5, 0):
                    act.wait_ge(cum_done, 1)
                    nc.scalar.activation(lt, side(1), ACT.Exp).then_inc(e_ready, 1)
                    nc.scalar.activation(ekd[:, :, :], side(1), ACT.Exp, scale=-1.0).then_inc(e_ready, 1)
                elif (c, j) == (5, 1):
                    act.wait_ge(cum_done, 2)
                    nc.scalar.activation(ekl[:, :, :], side(0), ACT.Exp).then_inc(e_ready, 1)
                elif (c, j) == (6, 0):
                    act.wait_ge(dec_sum, 1)
                    nc.scalar.activation(dec[:, :, :, :].rearrange("p h t j -> p (h t j)"), ps[:, 6, 0:16], ACT.Exp)\
                        .then_inc(dec_exp, 1)
                elif c == 7 and j < 2:
                    act.wait_ge(gT_done, j + 1)
                    nc.scalar.activation(qkT[:, j, :, :].rearrange("p (a h) s -> p a (h s)", a=2), side(1 - j), ACT.Copy)\
                        .then_inc(gT_out, 1)
                elif c == 8 and j < 2:
                    g = GROUPS["glaA"] + j
                    act.wait_ge(t_done, g + 1)
                    nc.scalar.activation(ekd[:, j, :], tbank(g), ACT.Copy).then_inc(a_evac, 1)
                elif c == 10 and j < 2:
                    act.wait_ge(acc_out, un + 10)
                    nc.scalar.activation(u[:, j, 6144:8192], u[:, j, 3072:5120], ACT.Square).then_inc(m_sq, 1)
                elif (c, j) == (11, 0):
                    act.wait_ge(m_sum, 1)
                    nc.scalar.activation(mst[:, 1, :, :], mst[:, 0, :, :], ACT.Sqrt, bias=eps[:, 1:2], scale=1.0 / P)\
                        .then_inc(m_sd, 1)
                elif c in (11, 12) and j == 1:
                    t = c - 11
                    act.wait_ge(go_done, t + 1)
                    nc.scalar.activation(xn[:, t, :].rearrange("p (b c) -> p b c", b=2), side(t), ACT.Copy)\
                        .then_inc(go_evac, 1)
                    if t == 1:
                        act.wait_ge(go_evac, TT)
                        nc.scalar.activation(gsq, xn[:, :, :].rearrange("p t (h e) -> p (t h) e", e=GDV), ACT.Square)\
                            .then_inc(go_sq, 1)
                elif (c, j) == (12, 3):
                    act.wait_ge(go_sum, 1)
                    nc.scalar.activation(stat[:, 8:16], stat[:, 0:8], ACT.Sqrt, bias=eps[:, 1:2], scale=1.0 / GDV)\
                        .then_inc(go_sd, 1)
                if c >= 13 and j == 0:
                    mqk_out(c - 13)

            def mqk_out(step):
                for j in (2 * step, 2 * step + 1):
                    g = GROUPS["mqk"] + j
                    act.wait_ge(t_done, g + 1)
                    nc.scalar.activation(mT[:, 2 * j:2 * j + 2, :], tbank(g).rearrange("p (h s) -> p h s", h=2), ACT.Copy,
                                         scale=gcol[:, 33:34] if j < 4 else gcol[:, 32:33]).then_inc(t_lo, 1)

            for c in range(16):
                for j in range(3):
                    adv(n + 4 * c + 4 + j)
                    beside(c, j)
                act.wait_ge(w_used, summed("win", c))
                nc.scalar.activation(u[:, :, c * CW:(c + 1) * CW], pair(un + c),
                                     ACT.Silu if c in (4, 5) else ACT.Sigmoid if c >= 12 else ACT.Copy).then_inc(acc_out, 1)
                adv(n + 4 * c + 7)
                beside(c, 3)
            mqk_out(3)
            gained(3, aH, "oa")

            def mexp(h):
                b = 8 * (h % 4)
                act.wait_ge(m_max, h + 1)
                if h >= 2:
                    act.wait_ge(m_T, h - 1)
                for t in range(TT):
                    ins = nc.scalar.activation(pe_[:, h % 2, t, :], sc[:, h % 2, t, :], ACT.Exp,
                                               bias=stat[:, b + t:b + t + 1],
                                               accum_out=stat[:, b + 2 + t:b + 3 + t])
                ins.then_inc(m_exp, 1)

            mexp(0)
            for h in range(H):
                adv(SUBS["bra"] + 4 + h)
                if h + 1 < H:
                    mexp(h + 1)
                act.wait_ge(m_T, h + 1)
                if h >= 2:
                    act.wait_ge(m_o, h - 1)
                nc.scalar.activation(pT[:, h % 2, :], ps[:, 4, 0:3 * P], ACT.Copy).then_inc(m_Tc, 1)
            for j in range(4):
                hi(GROUPS["ob"] + j, aH[:, 2 * j:2 * j + 2, :])
            for j in range(8):
                adv(SUBS["brb"] + 4 + j)
            for j in range(4):
                hi(GROUPS["y"] + j, aH[:, 2 * j:2 * j + 2, :])
            for j in range(8):
                adv(SUBS["wo2"] + 4 + j)
            rms(1, acc_out, UNITS["wo2"] + 2)
            gained(1, aH, "rms1")
            n, un, g = SUBS["up"], UNITS["up"], GROUPS["up"]

            def up(c, i=0, first=False):
                for j in range(4):
                    adv(n + 4 * c + 4 + j, i)
                if not first:
                    for j in range(2):
                        k0 = 4 * (c - 1) + 2 * j
                        hi(g + 2 * (c - 1) + j, uH[:, k0:k0 + 2, :] if isinstance(i, int)
                           else uH[:, bass.ds(k0 + 8 * i, 2), :], i, step=4)

            up(0, first=True)
            with act.Fori(0, 3) as i:
                up(1, i)
                up(2, i)
            up(7)
            for j in range(2):
                hi(g + 14 + j, uH[:, 28 + 2 * j:30 + 2 * j, :])
            for k in range(F2 // P):
                adv(SUBS["down"] + 4 + k)
            rms(2, acc_out, UNITS["down"] + 2)
            gained(2, aH, "rms2")
            for j in range(8):
                adv(SUBS["pg"] + 4 + j)
            for t in range(TT):
                un = UNITS["pg"] + t
                act.wait_ge(w_used, summed("pg"))
                nc.scalar.activation(gate[:, t, :].rearrange("p (b c) -> p b c", b=2), pair(un), ACT.Sigmoid)\
                    .then_inc(acc_out, 1)
            hi(GROUPS["p"], pH[:, :, :])

        @block.vector
        def _(dve):
            links = [0]

            def link(ins):
                links[0] += 1
                ins.then_inc(dve_self, 1)
                dve.wait_ge(dve_self, links[0])

            V = nc.vector

            def adv(n, i=0):
                if n >= NSUB:
                    return
                dve.wait_ge(w_hi, n + 1 + 8 * i)
                V.tensor_tensor(wL[:, n % WS, :], raw[:, (n // 2) % RAW, (n % 2) * 1024:(n % 2) * 1024 + 1024],
                                wH[:, n % WS, :].bitcast(fp32), ALU.subtract).then_inc(w_lo, 1)

            def lo(g, dst, high, i=0, gain=None, mod=False, step=2, k_hi=None):
                dve.wait_ge(t_hi, k_hi + 1 + step * i)
                src = tbank(g).rearrange("p (k s) -> p k s", k=2)
                if gain is not None:
                    for k in range(2):
                        ins = V.scalar_tensor_tensor(out=dst[:, k, :], in0=src[:, k, :], scalar=gain[:, k:k + 1],
                                                     in1=high[:, k, :].bitcast(fp32), op0=ALU.mult, op1=ALU.subtract)
                elif mod:
                    ins = V.tensor_tensor(dst, tf[:, g % 2, :].rearrange("p (k s) -> p k s", k=2),
                                          high.bitcast(fp32), ALU.subtract)
                else:
                    ins = V.tensor_tensor(dst, src, high.bitcast(fp32), ALU.subtract)
                ins.then_inc(t_lo, 1)

            hcount = [0]

            def lo4(name, L_, H_, **kw):
                gain = kw.pop("gain", None)
                for j in range(4):
                    lo(GROUPS[name] + j, L_[:, 2 * j:2 * j + 2, :], H_[:, 2 * j:2 * j + 2, :],
                       gain=None if gain is None else gain[:, 2 * j:2 * j + 2], k_hi=hcount[0], **kw)
                    hcount[0] += 1

            def mod_put(c):
                layer, m = MODS[c]
                one = 1.0 if m // 2 in (1, 4) else 0.0
                dve.wait_ge(mod_sel, c + 1)
                if mod_is_column(layer, m):
                    b0 = 48 * layer + 4 * m
                    V.scalar_tensor_tensor(
                        out=modcol[:, layer, MOD_WHICH[m // 2], 4 * (m % 2):4 * (m % 2) + 4, :],
                        in0=ps[:, 7, 0:8].rearrange("p (k r) -> p k r", r=2), scalar=one,
                        in1=bcol[:, b0:b0 + 4].unsqueeze(2).to_broadcast([P, 4, 2]),
                        op0=ALU.add, op1=ALU.add).then_inc(mod_out, 1)
                else:
                    dst = {(0, 2): g1b, (0, 5): g2b0, (1, 0): sh1b, (1, 1): sc1b, (1, 2): g1b, (1, 5): g2b1}[layer, m // 2]
                    dst = dst[:, (m % 2) * CW:(m % 2) * CW + CW]
                    if layer == 0:
                        dve.wait_ge(bias0_in, 32)
                    else:
                        dve.wait_ge(bias1_in, 64)
                    V.scalar_tensor_tensor(out=dst, in0=ps[:, 7, :], scalar=one, in1=dst,
                                           op0=ALU.add, op1=ALU.add).then_inc(mod_out, 1)

            for j, value in enumerate((LN_EPS, RMS_EPS)):
                V.memset(eps[:, j:j + 1], value)
            dve.wait_ge(cT_ready, 2)
            for c in range(NMOD0):
                mod_put(c)
            for j in range(4):
                lo(GROUPS["x"] + j, aL[:, 2 * j:2 * j + 2, :], aH[:, 2 * j:2 * j + 2, :], mod=True, k_hi=hcount[0])
                hcount[0] += 1
                adv(j)

            modc = [NMOD0]

            def next_mod():
                mod_put(modc[0])
                modc[0] += 1

            def mod_at(c, sub):
                for kind, m in MODPLAN.get((c, sub), ()):
                    if kind == "select":
                        mod_put(m)
                        modc[0] = m + 1

            rots = [0]

            def rotate(un, done, plain):
                dve.wait_ge(w_used, done)
                rs = ro[:, rots[0] % 2, :, :]
                if rots[0] >= 2:
                    dve.wait_ge(t_done, GROUPS["q"] + 2 * (rots[0] - 1))
                if plain:
                    V.tensor_copy(rs, pair(un)).then_inc(acc_out, 1)
                else:
                    for t in range(TT):
                        src = pair(un)[:, t, :].rearrange("p (m h d) -> p m h d", h=2, d=32)
                        for j, tab in enumerate((C_COS, C_SIN)):
                            cs = cst[:, tab + 32 * t:tab + 32 * t + 32].unsqueeze(1).unsqueeze(1).to_broadcast([P, 8, 2, 32])
                            ins = V.tensor_tensor(rt[:, j, t, :].rearrange("p (m h d) -> p m h d", h=2, d=32), src, cs,
                                                  ALU.mult)
                    link(ins)
                    for t in range(TT):
                        c_, s_ = (rt[:, j, t, :].rearrange("p (m h d) -> p m h d", h=2, d=32) for j in range(2))
                        o_ = rs[:, t, :].rearrange("p (m h d) -> p m h d", h=2, d=32)
                        V.tensor_tensor(o_[:, :, 0, :], c_[:, :, 0, :], s_[:, :, 1, :], ALU.subtract)
                        ins = V.tensor_tensor(o_[:, :, 1, :], s_[:, :, 0, :], c_[:, :, 1, :], ALU.add)
                    ins.then_inc(acc_out, 1)
                rots[0] += 1

            n = SUBS["qkv"]
            for c in range(6):
                for j in range(3):
                    adv(n + 4 * c + 4 + j)
                    mod_at(c, j)
                if c == 0:
                    lo4("ctx", cL, cH, mod=True)
                if c < 2:
                    rotate(UNITS["q"] + c, summed("q", c), False)
                elif c < 4:
                    rotate(UNITS["k"] + 2 * (c - 2), summed("k", 2 * (c - 2)), True)
                    rotate(UNITS["k"] + 2 * (c - 2) + 1, summed("k", 2 * (c - 2)), False)
                adv(n + 4 * c + 7)
                mod_at(c, 3)
                if c == 3:
                    dve.wait_ge(small_in, 16)
                    lv = lamt[:, :].rearrange("p (a b d) -> p a b d", a=2, b=2)
                    link(V.tensor_tensor(lv[:, :, 0, :], lv[:, :, 0, :], lv[:, :, 1, :], ALU.mult))
                    V.tensor_reduce(lam2[:, 0:2], lv[:, :, 0, :], AXX, ALU.add).then_inc(lam_sum, 1)
            dve.wait_ge(lam_exp, 1)
            link(V.tensor_tensor(lam2[:, 4:5], lam2[:, 2:3], lam2[:, 3:4], ALU.subtract))
            link(V.tensor_scalar(lam2[:, 5:6], lam2[:, 4:5], LAM_INIT, None, ALU.add))

            def mix(r):
                b = 8 * (r % 2)
                dve.wait_ge(s_exp, r + 1)
                link(V.reciprocal(stat[:, b + 4:b + 6], stat[:, b + 2:b + 4]))
                link(V.tensor_tensor(stat[:, b + 6:b + 7], stat[:, b + 5:b + 6], lam2[:, 5:6], ALU.mult))
                link(V.tensor_scalar(te, ex[:, r % 2, 1, :], stat[:, b + 6:b + 7], None, ALU.mult))
                if r >= 2:
                    dve.wait_ge(t_done, GROUPS["att"] + r - 1)
                V.scalar_tensor_tensor(out=am[:, r % 2, :], in0=ex[:, r % 2, 0, :], scalar=stat[:, b + 4:b + 5],
                                       in1=te, op0=ALU.mult, op1=ALU.subtract).then_inc(acc_out, 1)

            def put_o(r):
                h, t = r // 2, r % 2
                dve.wait_ge(o_done, r + 1)
                V.tensor_copy(ot[:, t, h * P:(h + 1) * P], ps[:, 6, 0:P]).then_inc(o_out, 1)

            def maxima(r):
                b = 8 * (r % 2)
                dve.wait_ge(acc_done, r + 1)
                link(V.tensor_reduce(stat[:, b + 6:b + 8], pair(UNITS["att"] + r), AXX, ALU.max))
                V.tensor_scalar(stat[:, b:b + 2], stat[:, b + 6:b + 8], -0.125, None, ALU.mult).then_inc(s_max, 1)

            maxima(0)
            maxima(1)
            for r in range(16):
                mix(r)
                if r < 14:
                    maxima(r + 2)
                if r >= 1 and mod_sum_in(r - 1):
                    next_mod()
                if r >= 1:
                    put_o(r - 1)
            put_o(15)
            for t in range(TT):
                o3 = ot[:, t, :].rearrange("p (h d) -> p h d", d=P)
                dve.wait_ge(o_sd, t + 1)
                link(V.reciprocal(stat[:, 16 + 8 * t:24 + 8 * t], stat[:, 32 + 8 * t:40 + 8 * t]))
                V.tensor_tensor(o3, o3, stat[:, 16 + 8 * t:24 + 8 * t].unsqueeze(2).to_broadcast([P, H, P]), ALU.mult)\
                    .then_inc(o_norm, 1)
            for j in range(4):
                lo(GROUPS["o"] + j, aL[:, 2 * j:2 * j + 2, :], aH[:, 2 * j:2 * j + 2, :], gain=subg, k_hi=hcount[0])
                hcount[0] += 1
            for j in range(8):
                adv(SUBS["wo"] + 4 + j)

            def ln(k, stage, gate_):
                tmp = tf[:, :, :].rearrange("p b c -> p (b c)")
                un = UNITS[stage]
                for t in range(TT):
                    dve.wait_ge(w_used, summed(stage))
                    V.tensor_tensor(tf[:, :, :], pair(un + t), gate_[:, :].rearrange("p (b c) -> p b c", b=2), ALU.mult)\
                        .then_inc(acc_out, 1)
                    dve.wait_ge(acc_out, un + t + 1)
                    link(V.scalar_tensor_tensor(out=x[:, t, :], in0=x[:, t, :], scalar=ALPHA, in1=tmp,
                                                op0=ALU.mult, op1=ALU.add))
                    V.bn_stats(bn[:, t, 0:6], x[:, t, 0:512])
                    link(V.bn_stats(bn[:, t, 6:12], x[:, t, 512:1024]))
                    V.bn_aggr(mv[:, t, :], bn[:, t, :]).then_inc(ln_var, 1)
                for t in range(TT):
                    dve.wait_ge(ln_sd, TT * k + t + 1)
                    link(V.reciprocal(stat[:, 54 + t:55 + t], stat[:, 52 + t:53 + t]))
                    link(V.tensor_scalar(x[:, t, :], x[:, t, :], mv[:, t, 0:1], stat[:, 54 + t:55 + t],
                                         ALU.subtract, ALU.mult))
                    dve.wait_ge(ln_in, 32 * (k + 1))
                    link(V.tensor_tensor(x[:, t, :], x[:, t, :], lnp[:, 0, :], ALU.mult))
                    V.tensor_tensor(x[:, t, :], x[:, t, :], lnp[:, 1, :], ALU.add).then_inc(ln_x, 1)

            def swiglu(layer):
                n, un, g = SUBS[f"in{layer}"], UNITS[f"in{layer}"], GROUPS[f"in{layer}"]
                k_hi = hcount[0]
                sbase = 11 * layer

                def low(c, i):
                    k0 = 2 * c + 4 * i
                    d, s = (hL[:, k0:k0 + 2, :], hH[:, k0:k0 + 2, :]) if isinstance(i, int) else \
                           (hL[:, bass.ds(k0, 2), :], hH[:, bass.ds(k0, 2), :])
                    lo(g + c, d, s, i, k_hi=k_hi + c)

                def one(c, i=0, first=False):
                    for j in range(3):
                        adv(n + 4 * c + 4 + j, i)
                    dve.wait_ge(silu_done, sbase + c + 1 + 2 * i)
                    V.tensor_tensor(hid[:, c % 2, :, :], sil[:, c % 2, :, :], pair(un + c)[:, :, 256:512], ALU.mult)\
                        .then_inc(acc_out, 1)
                    adv(n + 4 * c + 7, i)
                    if not first:
                        low(c - 1, i)

                one(0, first=True)
                with dve.Fori(0, 5) as i:
                    one(1, i)
                    one(2, i)
                low(10, 0)
                hcount[0] += 11
                for k in range(F1 // P):
                    adv(SUBS[f"out{layer}"] + 4 + k)
                    if layer == 0 and k % 2 == 1 and k < 16:
                        next_mod()

            ln(0, "wo", g1b)
            lo4("x1", aL, aH, mod=True)
            swiglu(0)
            ln(1, "out0", g2b0)
            dve.wait_ge(ln_x, 2 * TT)
            for t in range(TT):
                V.tensor_tensor(hm[:, t, :], x[:, t, :], sc1b[:, :], ALU.mult)
            dve.wait_ge(pscale_in, 16)
            link(V.tensor_tensor(g1b[:, :], g1b[:, :], psb[:, :], ALU.mult))
            for t in range(TT):
                V.tensor_tensor(hm[:, t, :], hm[:, t, :], sh1b[:, :], ALU.add).then_inc(pool_h, 1)
            lo4("pool", aL, aH)
            for j in range(2):
                adv(SUBS["pool"] + 4 + j)
            ln(2, "pool", g1b)
            lo4("x3", aL, aH, mod=True)
            swiglu(1)
            ln(3, "out1", g2b1)

            def rms(k):
                dve.wait_ge(rms_sq, TT * (k + 1))
                V.tensor_scalar(stat[:, 58:60], stat[:, 56:58], 1.0 / D, RMS_EPS, ALU.mult, ALU.add).then_inc(rms_ms, 1)
                dve.wait_ge(rms_sd, k + 1)
                link(V.reciprocal(stat[:, 62:64], stat[:, 60:62]))
                for t in range(TT):
                    V.tensor_scalar(xn[:, t, :], x[:, t, :], stat[:, 62 + t:63 + t], None, ALU.mult).then_inc(xn_ready, 1)

            rms(0)
            lo4("rms0", aL, aH, gain=gcol[:, 0:8])
            n = SUBS["win"]
            gq, gk = u[:, :, 0:512], u[:, :, 512:1024]
            o4g = xn[:, :, :].rearrange("p t (h e) -> p t h e", e=GDV)
            mqk = u[:, :, 3072:5120].rearrange("p t (g d) -> p t g d", d=P)

            def beside(c, j):
                if (c, j) == (1, 0):
                    dve.wait_ge(lr_hi, 1)
                    V.tensor_tensor(lrL[:, :, :], lrw[:, :, :], lrH[:, :, :].bitcast(fp32), ALU.subtract)\
                        .then_inc(lr_lo, 1)
                elif (c, j) == (4, 0):
                    dve.wait_ge(z_done, 1)
                    dve.wait_ge(vec_in, 32)
                    link(V.tensor_tensor(la, side(0), gbb[:, :].unsqueeze(1).to_broadcast([P, TT, 512]), ALU.add))
                    V.scalar_tensor_tensor(out=lt, in0=la, scalar=-1.0, in1=la,
                                           op0=ALU.mult, op1=ALU.max).then_inc(z_abs, 1)
                elif (c, j) == (4, 2):
                    dve.wait_ge(z_ln, 1)
                    V.scalar_tensor_tensor(out=la, in0=la, scalar=0.0, in1=lt,
                                           op0=ALU.min, op1=ALU.subtract).then_inc(la_ready, 1)
                elif (c, j) == (5, 1):
                    dve.wait_ge(e_ready, 1)
                    V.scalar_tensor_tensor(out=gq, in0=gq, scalar=GDK ** -0.5, in1=lt, op0=ALU.mult, op1=ALU.mult)\
                        .then_inc(g_mul, 1)
                elif (c, j) == (5, 2):
                    dve.wait_ge(e_ready, 2)
                    V.tensor_tensor(ekd[:, :, :], ekd[:, :, :], gk, ALU.mult).then_inc(g_mul, 1)
                elif (c, j) == (5, 3):
                    dve.wait_ge(e_ready, 3)
                    V.tensor_tensor(ekl[:, :, :], ekl[:, :, :], gk, ALU.mult).then_inc(g_mul, 1)
                elif c in (8, 9, 10) and j == 0:
                    k = c - 8
                    dve.wait_ge(kv_done, k + 1)
                    if k == 0:
                        ins = V.tensor_copy(st[:, 0, :, :].rearrange("p (a h) e -> p a (h e)", a=2), side(0))
                    else:
                        dve.wait_ge(dec_exp, 1)
                        dve.wait_ge(kv_out, k)
                        for h in range(GH):
                            ins = V.scalar_tensor_tensor(out=st[:, k, h, :], in0=st[:, k - 1, h, :],
                                                         scalar=dec[:, h, k // 2, k % 2:k % 2 + 1],
                                                         in1=ps[:, 6 + h // 2, (h % 2) * GDV:(h % 2) * GDV + GDV],
                                                         op0=ALU.mult, op1=ALU.add)
                    ins.then_inc(kv_out, 1)
                elif (c, j) in ((10, 1), (10, 3)):
                    t = j // 2
                    dve.wait_ge(m_sq, t + 1)
                    V.tensor_reduce(mst[:, 0, t, :], u[:, t, 6144:8192].rearrange("p (g d) -> p g d", d=P), AXX, ALU.add)\
                        .then_inc(m_sum if t else dve_self, 1)
                    links[0] += 1 - t
                elif (c, j) == (11, 1):
                    dve.wait_ge(m_sd, 1)
                    link(V.reciprocal(mst[:, 0, :, :], mst[:, 1, :, :]))
                if c == 11 and j in (1, 2):
                    t = j - 1
                    V.tensor_tensor(mqk[:, t, :, :], mqk[:, t, :, :], mst[:, 0, t, :].unsqueeze(2)
                                    .to_broadcast([P, 16, P]), ALU.mult).then_inc(m_norm, 1)
                elif (c, j) == (12, 2):
                    dve.wait_ge(go_sq, 1)
                    V.tensor_reduce(stat[:, 0:8], gsq, AXX, ALU.add).then_inc(go_sum, 1)
                elif (c, j) == (13, 0):
                    dve.wait_ge(go_sd, 1)
                    link(V.reciprocal(stat[:, 0:8], stat[:, 8:16]))
                    link(V.tensor_tensor(o4g, o4g, stat[:, 0:8].rearrange("p (t h) -> p t h", t=TT).unsqueeze(3)
                                         .to_broadcast([P, TT, GH, GDV]), ALU.mult))
                elif (c, j) == (13, 2):
                    dve.wait_ge(acc_out, UNITS["win"] + 6)
                    V.tensor_tensor(xn[:, :, :], xn[:, :, :], u[:, :, 2048:3072], ALU.mult).then_inc(oa_ready, 1)

            for c in range(16):
                for j in range(4):
                    adv(n + 4 * c + 4 + j)
                    beside(c, j)
            dist = cst[:, C_DIST:C_TRI].rearrange("p (t k) -> p t k", t=TT)
            ob = xn

            def mmax(h):
                b = 8 * (h % 4)
                dve.wait_ge(m_scores, h + 1)
                if h >= 2:
                    dve.wait_ge(m_exp, h - 1)
                link(V.scalar_tensor_tensor(out=sc[:, h % 2, :, :], in0=dist, scalar=2.0 ** -(h + 1),
                                            in1=ps[:, 6 + h % 2, :].rearrange("p (t k) -> p t k", t=TT),
                                            op0=ALU.mult, op1=ALU.add))
                V.tensor_reduce(stat[:, b:b + 2], sc[:, h % 2, :, :], AXX, ALU.max, negate=True).then_inc(m_max, 1)

            def moba_out(h):
                b = 8 * (h % 4)
                dve.wait_ge(m_exp, h + 1)
                link(V.reciprocal(stat[:, b + 4:b + 6], stat[:, b + 2:b + 4]))
                dve.wait_ge(m_o, h + 1)
                for t in range(TT):
                    ins = V.tensor_scalar(ob[:, t, h * P:(h + 1) * P], ps[:, 5, t * P:(t + 1) * P],
                                          stat[:, b + 4 + t:b + 5 + t], None, ALU.mult)
                ins.then_inc(m_oout, 1)

            lo4("oa", aL, aH, gain=gcol[:, 24:32])
            mmax(0)
            mmax(1)
            for h in range(H):
                adv(SUBS["bra"] + 4 + h)
                if h + 2 < H:
                    mmax(h + 2)
                if h >= 1:
                    moba_out(h - 1)
            ga, gb = u[:, :, 6144:7168], u[:, :, 7168:8192]
            for t in range(TT):
                dve.wait_ge(w_used, summed("bra"))
                V.tensor_tensor(ga[:, t, :].rearrange("p (b c) -> p b c", b=2), pair(UNITS["bra"] + t),
                                ga[:, t, :].rearrange("p (b c) -> p b c", b=2), ALU.mult).then_inc(acc_out, 1)
                if t == 0:
                    moba_out(H - 1)
            lo4("ob", aL, aH)
            for j in range(8):
                adv(SUBS["brb"] + 4 + j)
            for t in range(TT):
                dve.wait_ge(w_used, summed("brb"))
                gbt = gb[:, t, :].rearrange("p (b c) -> p b c", b=2)
                V.tensor_tensor(gbt, pair(UNITS["brb"] + t), gbt, ALU.mult).then_inc(acc_out, 1)
                dve.wait_ge(acc_out, UNITS["brb"] + t + 1)
                V.tensor_tensor(xn[:, t, :], ga[:, t, :], gb[:, t, :], ALU.add).then_inc(oa_ready, 1)
            lo4("y", aL, aH)
            for j in range(8):
                adv(SUBS["wo2"] + 4 + j)

            def residual(stage):
                un = UNITS[stage]
                for t in range(TT):
                    dve.wait_ge(w_used, summed(stage))
                    xt = x[:, t, :].rearrange("p (b c) -> p b c", b=2)
                    V.tensor_tensor(xt, pair(un + t), xt, ALU.add).then_inc(acc_out, 1)

            residual("wo2")
            rms(1)
            lo4("rms1", aL, aH, gain=gcol[:, 8:16])
            n, un, g = SUBS["up"], UNITS["up"], GROUPS["up"]
            k_hi = hcount[0]

            def ulow(c, i):
                for j in range(2):
                    k0 = 4 * c + 2 * j
                    d, s = (uL[:, k0:k0 + 2, :], uH[:, k0:k0 + 2, :]) if isinstance(i, int) else \
                           (uL[:, bass.ds(k0 + 8 * i, 2), :], uH[:, bass.ds(k0 + 8 * i, 2), :])
                    lo(g + 2 * c + j, d, s, i, k_hi=k_hi + 2 * c + j, step=4)

            def up(c, i=0, first=False):
                for j in range(3):
                    adv(n + 4 * c + 4 + j, i)
                dve.wait_ge(w_used, summed("up", c) + 8 * i)
                V.tensor_scalar(hu[:, c % 2, :, :], pair(un + c), 0.0, None, ALU.max).then_inc(acc_out, 1)
                dve.wait_ge(acc_out, un + c + 1 + 2 * i)
                V.tensor_tensor(hu[:, c % 2, :, :], hu[:, c % 2, :, :], hu[:, c % 2, :, :], ALU.mult).then_inc(silu_done, 1)
                adv(n + 4 * c + 7, i)
                if not first:
                    ulow(c - 1, i)

            up(0, first=True)
            with dve.Fori(0, 3) as i:
                up(1, i)
                up(2, i)
            up(7)
            ulow(7, 0)
            hcount[0] += 16
            for k in range(F2 // P):
                adv(SUBS["down"] + 4 + k)
            residual("down")
            rms(2)
            lo4("rms2", aL, aH, gain=gcol[:, 16:24])
            for j in range(8):
                adv(SUBS["pg"] + 4 + j)
            lo(GROUPS["p"], pL[:, :, :], pH[:, :, :], k_hi=hcount[0])
            for t in range(TT):
                dve.wait_ge(w_used, summed("ple"))
                dve.wait_ge(acc_out, UNITS["pg"] + t + 1)
                gt = gate[:, t, :].rearrange("p (b c) -> p b c", b=2)
                link(V.tensor_tensor(gt, pair(UNITS["ple"] + t), gt, ALU.mult))
                V.tensor_tensor(x[:, t, :], x[:, t, :], gate[:, t, :], ALU.add).then_inc(x_done, 1)

        @block.tensor
        def _(pe):
            T = nc.tensor

            def sub_ready(n, i=0):
                pe.wait_ge(w_lo, n + 1 + 8 * i)

            def three(outp, xh, xl, h, l, first, last_):
                T.matmul(outp, xh, h, start=first, stop=False)
                T.matmul(outp, xh, l, start=False, stop=False)
                return T.matmul(outp, xl, h, start=False, stop=last_)

            def chunk_mm(n, i, units, acts, t_need=None, after_sub=None):
                for s in range(4):
                    sub_ready(n + s, i)
                    if t_need is not None:
                        pe.wait_ge(t_lo, t_need + s + 1)
                    for un, (xh, xl) in zip(units, acts):
                        if s == 0:
                            at_least(pe, acc_out, un - 1 + 2 * i)
                        for kk in range(2):
                            k = 2 * s + kk
                            h = wH[:, (n + s) % WS, kk * CW:(kk + 1) * CW]
                            l = wL[:, (n + s) % WS, kk * CW:(kk + 1) * CW]
                            for t in range(TT):
                                ins = three(pair(un)[:, t, :], xh[:, k, t * P:(t + 1) * P], xl[:, k, t * P:(t + 1) * P],
                                            h, l, k == 0, k == KT - 1)
                    ins.then_inc(w_used, 1)
                    if after_sub is not None:
                        after_sub(s)

            def rows_mm(n, un, xh, xl, kn, t_need=None, after_sub=None):
                for k in range(kn):
                    sub_ready(n + k)
                    if t_need is not None and k % 2 == 0:
                        pe.wait_ge(t_lo, t_need + k // 2 + 1)
                    for t in range(TT):
                        if k == 0:
                            at_least(pe, acc_out, un + t - 1)
                        for b in range(2):
                            ins = three(pair(un + t)[:, b, :], xh[:, k, t * P:(t + 1) * P], xl[:, k, t * P:(t + 1) * P],
                                        wH[:, (n + k) % WS, b * CW:(b + 1) * CW], wL[:, (n + k) % WS, b * CW:(b + 1) * CW],
                                        k == 0, k == kn - 1)
                    ins.then_inc(w_used, 1)
                    if after_sub is not None:
                        after_sub(k)

            def group(g, blocks, i=0, step=2):
                at_least(pe, t_lo, g - 1 + step * i if g >= 2 or not isinstance(i, int) else 0)
                for j, b in enumerate(blocks):
                    ins = T.transpose(tbank(g)[:, j * P:(j + 1) * P], b, ident)
                ins.then_inc(t_done, 1)

            def groups(name, src):
                for j in range(4):
                    group(GROUPS[name] + j, [src[:, t, (2 * j + k) * P:(2 * j + k + 1) * P] for k in range(2) for t in range(TT)])

            def mod_mm(c):
                bank = c if c < NMOD0 else 7
                if c > NMOD0:
                    pe.wait_ge(mod_out, c)
                for h in range(2):
                    if c < NMOD0:
                        if h == 0:
                            pe.wait_ge(mod0_in[c], 16)
                        src = mod0[:, 2 * c + h, :]
                    else:
                        pe.wait_ge(mod_in[h], 16 * (c - NMOD0 + 1))
                        src = modraw[:, h, :]
                    for j in range(4):
                        ins = T.matmul(ps[32 * j:32 * j + 32, bank, :], cT[:, 4 * h + j, :], src[:, j * CW:(j + 1) * CW],
                                       start=h == 0, stop=h == 1)
                    if c >= NMOD0:
                        ins.then_inc(mod_used, 1)
                if c < NMOD0:
                    ins.then_inc(mod_acc, 1)

            def mod_select(c):
                layer, m = MODS[c]
                pe.wait_ge(mod_row, c + 1)
                if c and c <= NMOD0:
                    pe.wait_ge(mod_out, c)
                if mod_is_column(layer, m):
                    for k in range(4):
                        ins = T.matmul(ps[:, 7, 2 * k:2 * k + 2], modrow[:, k * P:(k + 1) * P],
                                       cst[:, C_SELC:C_SELC + 2], start=True, stop=True)
                else:
                    ins = T.matmul(ps[:, 7, :], cst[:, C_SELB:C_SELB + P], modrow[:, :], start=True, stop=True)
                ins.then_inc(mod_sel, 1)

            pe.wait_ge(cst_in, 16)
            pe.wait_ge(rows_in, 64)
            T.transpose(ps[:, 6, 0:113], rows[:, :], ident[0:113, 0:113]).then_inc(rows_T, 1)
            pe.wait_ge(cT_ready, 2)
            for c in range(NMOD0):
                mod_mm(c)
            for c in range(NMOD0):
                mod_select(c)
            pe.wait_ge(x_in, 16)
            groups("x", x)

            modc = [NMOD0]

            def mod_at(c, sub):
                for kind, m in MODPLAN.get((c, sub), ()):
                    (mod_mm if kind == "sum" else mod_select)(m)
                    modc[0] = m + 1

            n = SUBS["qkv"]
            X, C = (aH, aL), (cH, cL)

            def heads(unit):
                pe.wait_ge(acc_out, UNITS["q"] + unit + 1)
                g = GROUPS["q"] + 2 * unit
                for j in range(2):
                    group(g + j, [ro[:, unit % 2, t, (2 * j + k) * P:(2 * j + k + 1) * P]
                                  for k in range(2) for t in range(TT)])

            for c in range(6):
                def beside(sub, c=c):
                    mod_at(c, sub)

                if c < 2:
                    chunk_mm(n + 4 * c, 0, [UNITS["q"] + c], [X], GROUPS["x"] if c == 0 else None, beside)
                else:
                    un = UNITS["k"] + 2 * (c - 2)
                    chunk_mm(n + 4 * c, 0, [un, un + 1], [C, X], None, beside)
                if c == 0:
                    pe.wait_ge(ctx_in, 16)
                    groups("ctx", lnp)
                elif c == 1:
                    pe.wait_ge(t_lo, GROUPS["ctx"] + 4)
                    heads(0)
                elif c == 2:
                    heads(1)
                elif c < 5:
                    heads(2 * c - 4)
                    heads(2 * c - 3)

            def scores(r):
                h, t = r // 2, r % 2
                un = UNITS["att"] + r
                if r >= 2:
                    pe.wait_ge(s_exp, r - 1)
                else:
                    pe.wait_ge(acc_out, un - 1)
                for m in range(2):
                    ins = T.matmul(pair(un)[:, m, :], qz[:, h, m, t * P:(t + 1) * P], kT[:, h, :], start=True, stop=True)
                ins.then_inc(acc_done, 1)

            def values(r):
                h = r // 2
                pe.wait_ge(t_lo, GROUPS["att"] + r + 1)
                if r >= 1:
                    pe.wait_ge(o_out, r)
                for k in range(4):
                    ins = T.matmul(ps[:, 6, 0:P], at[:, r % 2, k, :],
                                   v[:, k, h * P:(h + 1) * P], start=k == 0, stop=k == 3)
                ins.then_inc(o_done, 1)

            pe.wait_ge(t_lo, GROUPS["k"] + 8)
            scores(0)
            scores(1)
            for r in range(16):
                if r < 14:
                    scores(r + 2)
                if r >= 1 and mod_sum_in(r - 1):
                    mod_select(modc[0])
                    modc[0] += 1
                pe.wait_ge(acc_out, UNITS["att"] + r + 1)
                group(GROUPS["att"] + r, [am[:, r % 2, k * P:(k + 1) * P] for k in range(4)])
                if r >= 1:
                    values(r - 1)
                if mod_sum_in(r):
                    mod_mm(modc[0])
            values(15)
            pe.wait_ge(o_norm, 2)
            groups("o", ot)
            rows_mm(SUBS["wo"], UNITS["wo"], aH, aL, KT, GROUPS["o"])
            pe.wait_ge(rows2_in, 96)
            pe.wait_ge(o_out, 16)
            T.transpose(ps[:, 6, 0:34], rows2[:, :], ident[0:34, 0:34]).then_inc(rows2_T, 1)
            pe.wait_ge(ln_x, TT)
            groups("x1", x)

            def swiglu(layer, name):
                n, un, g = SUBS[f"in{layer}"], UNITS[f"in{layer}"], GROUPS[f"in{layer}"]

                def mm(c, i=0, need=None):
                    chunk_mm(n + 4 * c, i, [un + c], [X], need)

                def tr(c, i=0):
                    pe.wait_ge(acc_out, un + c + 1 + 2 * i)
                    group(g + c, [hid[:, c % 2, t, k * P:(k + 1) * P] for k in range(2) for t in range(TT)], i)

                mm(0, need=GROUPS[name])
                with pe.Fori(0, 5) as i:
                    mm(1, i)
                    tr(0, i)
                    mm(2, i)
                    tr(1, i)
                tr(10)

                def beside(k):
                    if layer == 0 and k < 16:
                        if k % 2 == 0:
                            mod_mm(modc[0])
                        else:
                            mod_select(modc[0])
                            modc[0] += 1

                rows_mm(SUBS[f"out{layer}"], UNITS[f"out{layer}"], hH, hL, F1 // P, g, beside)

            swiglu(0, "x1")
            pe.wait_ge(pool_in, 16)
            pe.wait_ge(pool_h, 2)
            for j in range(4):
                g = GROUPS["pool"] + j
                at_least(pe, t_lo, g - 1)
                for k in range(2):
                    for t in range(TT):
                        ins = T.matmul(tbank(g)[:, k * S:(k + 1) * S], hm[:, t, (2 * j + k) * P:(2 * j + k + 1) * P],
                                       poolm[:, t, j, :], start=t == 0, stop=t == TT - 1)
                ins.then_inc(t_done, 1)
            n, un = SUBS["pool"], UNITS["pool"]
            for s in range(2):
                sub_ready(n + s)
                for gg in range(2):
                    gr = 2 * s + gg
                    pe.wait_ge(t_lo, GROUPS["pool"] + gr + 1)
                    for t in range(TT):
                        if gr == 0:
                            pe.wait_ge(acc_out, un + t - 1)
                        for k in range(2):
                            w0 = (2 * gg + k) * 256
                            ins = three(pair(un + t)[:, gr // 2, (gr % 2) * 256:(gr % 2) * 256 + 256],
                                        aH[:, 2 * gr + k, t * P:(t + 1) * P], aL[:, 2 * gr + k, t * P:(t + 1) * P],
                                        wH[:, (n + s) % WS, w0:w0 + 256], wL[:, (n + s) % WS, w0:w0 + 256],
                                        k == 0, k == 1)
                ins.then_inc(w_used, 1)
            pe.wait_ge(ln_x, 3 * TT)
            groups("x3", x)
            swiglu(1, "x3")

            pe.wait_ge(xn_ready, TT)
            groups("rms0", xn)
            n, un = SUBS["win"], UNITS["win"]
            pe.wait_ge(t_lo, GROUPS["rms0"] + 4)
            def behind(c):
                if c == 1:
                    pe.wait_ge(lr_lo, 1)
                    for t in range(TT):
                        for k in range(KT):
                            ins = three(ps[:, 6, t * GRANK:(t + 1) * GRANK], aH[:, k, t * P:(t + 1) * P],
                                        aL[:, k, t * P:(t + 1) * P], lrH[:, k, :], lrL[:, k, :], k == 0, k == KT - 1)
                    ins.then_inc(lr_done, 1)
                elif c == 2:
                    pe.wait_ge(lr_t, 1)
                    for t in range(TT):
                        ins = T.transpose(ps[0:GRANK, 6, t * P:(t + 1) * P], lrt[:, t, :], ident)
                    ins.then_inc(lr_T, 1)
                elif c == 3:
                    pe.wait_ge(lr_Tc, 1)
                    pe.wait_ge(vec_in, 32)
                    for t in range(TT):
                        ins = T.matmul(side(0)[:, t, :], lrT[:, t * P:(t + 1) * P], w2[:, :], start=True, stop=True)
                    ins.then_inc(z_done, 1)
                elif c == 4:
                    pe.wait_ge(la_ready, 1)
                    for j, tab in enumerate((C_TRI, C_TRS)):
                        for t in range(TT):
                            ins = T.matmul(side(1 - j)[:, t, :], cst[:, tab:tab + P], la[:, t, :], start=True, stop=True)
                        ins.then_inc(cum_done, 1)
                elif c == 5:
                    pe.wait_ge(e_ready, 3)
                    for h in range(GH):
                        for t in range(TT):
                            ins = T.matmul(ps[:, 6, 4 * h + 2 * t:4 * h + 2 * t + 2], la[:, t, h * GDK:(h + 1) * GDK],
                                           cst[:, C_IND:C_IND + 2], start=True, stop=True)
                    ins.then_inc(dec_sum, 1)
                elif c == 6:
                    pe.wait_ge(g_mul, 2)
                    pe.wait_ge(dec_exp, 1)
                    for j, src in enumerate((u[:, :, 0:512], ekd[:, :, :])):
                        for h in range(GH):
                            for t in range(TT):
                                ins = T.transpose(side(1 - j)[:, h // 2, (h % 2) * S + t * P:(h % 2) * S + (t + 1) * P],
                                                  src[:, t, h * GDK:(h + 1) * GDK], ident)
                        ins.then_inc(gT_done, 1)
                if c == 7:
                    pe.wait_ge(gT_out, 2)
                    for t in range(TT):
                        g = GROUPS["glaA"] + t
                        for h in range(GH):
                            ins = T.matmul(tbank(g)[:, h * P:(h + 1) * P], qkT[:, 1, h, t * P:(t + 1) * P],
                                           qkT[:, 0, h, t * P:(t + 1) * P], start=True, stop=True)
                        ins.then_inc(t_done, 1)
                if c in (7, 8, 9):
                    k = c - 7
                    t, r0 = k // 2, GCH * (k % 2)
                    if k == 0:
                        pe.wait_ge(g_mul, 3)
                    else:
                        pe.wait_ge(kv_out, k)
                    for h in range(GH):
                        ins = T.matmul(ps[:, 6 + h // 2, (h % 2) * GDV:(h % 2) * GDV + GDV],
                                       ekl[r0:r0 + GCH, t, h * GDK:(h + 1) * GDK],
                                       u[r0:r0 + GCH, t, 1024 + h * GDV:1024 + (h + 1) * GDV], start=True, stop=True)
                    ins.then_inc(kv_done, 1)
                elif c in (10, 11):
                    t = c - 10
                    pe.wait_ge(kv_out, 3)
                    pe.wait_ge(t_lo, GROUPS["glaA"] + t + 1)
                    if t == 1:
                        pe.wait_ge(a_evac, TT)
                    for h in range(GH):
                        dst = side(t)[:, h // 2, (h % 2) * GDV:(h % 2) * GDV + GDV]
                        ins = T.matmul(dst, aT[:, t, h, :], u[:, t, 1024 + h * GDV:1024 + (h + 1) * GDV],
                                       start=True, stop=True, skip_group_check=True)
                        for half in range(2):
                            k = 2 * t + half
                            if k == 0:
                                continue
                            ins = T.matmul(dst[GCH * half:GCH * half + GCH, :], qkT[:, 0, h, k * GCH:(k + 1) * GCH],
                                           st[:, k - 1, h, :], start=False, stop=True, skip_group_check=True)
                    ins.then_inc(go_done, 1)
                elif c >= 12:
                    if c == 12:
                        pe.wait_ge(m_norm, TT)
                        pe.wait_ge(go_evac, TT)
                    for j in (2 * (c - 12), 2 * (c - 12) + 1):
                        group(GROUPS["mqk"] + j, [u[:, t, 3072 + (2 * j + k) * P:3072 + (2 * j + k + 1) * P]
                                                  for k in range(2) for t in range(TT)])

            for c in range(16):
                chunk_mm(n + 4 * c, 0, [un + c], [X])
                behind(c)

            def mscores(h):
                pe.wait_ge(t_lo, GROUPS["mqk"] + 5 + h // 2)
                if h >= 2:
                    pe.wait_ge(m_max, h - 1)
                for t in range(TT):
                    ins = T.matmul(ps[:, 6 + h % 2, t * S:(t + 1) * S], mT[:, h, t * P:(t + 1) * P], mT[:, 8 + h, :],
                                   start=True, stop=True)
                ins.then_inc(m_scores, 1)

            def mtranspose(h):
                pe.wait_ge(m_exp, h + 1)
                if h == 0:
                    pe.wait_ge(t_lo, GROUPS["oa"] + 4)
                else:
                    pe.wait_ge(m_Tc, h)
                for j, (t, k) in enumerate(((0, 0), (1, 0), (1, 1))):
                    ins = T.transpose(ps[:, 4, j * P:(j + 1) * P], pe_[:, h % 2, t, k * P:(k + 1) * P], ident)
                ins.then_inc(m_T, 1)

            def mvalues(h):
                pe.wait_ge(m_Tc, h + 1)
                if h >= 1:
                    pe.wait_ge(m_oout, h)
                vh = [u[:, k, 5120 + h * P:5120 + (h + 1) * P] for k in range(2)]
                T.matmul(ps[:, 5, 0:P], pT[:, h % 2, 0:P], vh[0], start=True, stop=True)
                T.matmul(ps[:, 5, P:S], pT[:, h % 2, P:S], vh[0], start=True, stop=False)
                T.matmul(ps[:, 5, P:S], pT[:, h % 2, S:S + P], vh[1], start=False, stop=True).then_inc(m_o, 1)

            def moba(h):
                mtranspose(h)
                if h >= 1:
                    mvalues(h - 1)
                if h + 2 < H:
                    mscores(h + 2)

            mscores(0)
            mscores(1)
            pe.wait_ge(oa_ready, 1)
            groups("oa", xn)
            rows_mm(SUBS["bra"], UNITS["bra"], aH, aL, KT, GROUPS["oa"], moba)
            mvalues(H - 1)
            pe.wait_ge(m_oout, H)
            groups("ob", xn)
            rows_mm(SUBS["brb"], UNITS["brb"], aH, aL, KT, GROUPS["ob"])
            pe.wait_ge(oa_ready, 3)
            groups("y", xn)
            rows_mm(SUBS["wo2"], UNITS["wo2"], aH, aL, KT, GROUPS["y"])
            pe.wait_ge(xn_ready, 2 * TT)
            groups("rms1", xn)
            n, un, g = SUBS["up"], UNITS["up"], GROUPS["up"]

            def um(c, i=0, need=None):
                chunk_mm(n + 4 * c, i, [un + c], [X], need)

            def ut(c, i=0):
                pe.wait_ge(silu_done, 22 + c + 1 + 2 * i)
                for j in range(2):
                    group(g + 2 * c + j, [hu[:, c % 2, t, (2 * j + k) * P:(2 * j + k + 1) * P]
                                          for k in range(2) for t in range(TT)], i, step=4)

            um(0, need=GROUPS["rms1"])
            with pe.Fori(0, 3) as i:
                um(1, i)
                ut(0, i)
                um(2, i)
                ut(1, i)
            um(7)
            ut(6)
            ut(7)
            rows_mm(SUBS["down"], UNITS["down"], uH, uL, F2 // P, g)
            pe.wait_ge(xn_ready, 3 * TT)
            groups("rms2", xn)
            rows_mm(SUBS["pg"], UNITS["pg"], aH, aL, KT, GROUPS["rms2"])
            pe.wait_ge(p_in, 16)
            group(GROUPS["p"], [pt[:, t, k * P:(k + 1) * P] for k in range(2) for t in range(TT)])
            rows_mm(SUBS["ple"], UNITS["ple"], pH, pL, 2, GROUPS["p"])


_INS = ["x", "c", "ctx", "c_ctx", "w_mod", "b_mod", "ln_g", "ln_b", "attn_w_qkv", "attn_lambda", "attn_subln_g",
        "attn_w_o", "pool_w", "pool_scale", "ffn_w_in", "ffn_w_out", "p_2", "norm_mix_2", "w_in_2", "gla_gate_w2_2",
        "gla_gate_b_2", "gla_out_norm_2", "moba_q_norm_2", "moba_k_norm_2", "w_branch_a_2", "w_branch_b_2",
        "w_out_2", "norm_mlp_2", "w_up_2", "w_down_2", "norm_ple_2", "w_ple_gate_2", "w_ple_2"]


def kernel(**inputs):
    import concourse.bacc as bacc
    from concourse.bass_utils import run_bass_kernel_spmd

    nc = bacc.Bacc("TRN2", target_bir_lowering=False, num_devices=1)
    arrays, aps = {}, {}
    for name in _INS:
        arr = np.ascontiguousarray(inputs[name])
        arrays[f"in_{name}"] = arr
        aps[name] = nc.dram_tensor(f"in_{name}", arr.shape, mybir.dt.from_np(arr.dtype), kind="ExternalInput").ap()
    consts = []
    for name, arr in zip(("const_tables", "const_windows"), shape_constants()):
        arrays[name] = arr
        consts.append(nc.dram_tensor(name, arr.shape, fp32, kind="ExternalInput").ap())
    out = nc.dram_tensor("out", (1, S, D), fp32, kind="ExternalOutput").ap()
    build(nc, aps, consts[0], consts[1], out)
    r = run_bass_kernel_spmd(nc, [arrays], core_ids=[0])
    return r.results[0]["out"]
```

```python
import math
from contextlib import ExitStack

import numpy as np

import concourse.bass as bass
from concourse import mybir

fp32 = mybir.dt.float32
f32r = mybir.dt.float32r
ALU = mybir.AluOpType
ACT = mybir.ActivationFunctionType
AXX = mybir.AxisListType.X

P = 128
D = 1024
KT = D // P
S = 256
TT = S // P
F1 = 2816
F2 = 4096
H = 8
GH, GDK, GDV, GCH, GRANK = 4, 128, 256, 64, 16
ALPHA = 4.0 ** 0.25
LN_EPS, RMS_EPS = 1e-5, 1e-6
LAM_INIT = 0.8 - 0.6 * math.exp(0.0)
POOL_WINDOWS = (2, 4, 8, 16)
N_IN = 8208
LR0 = 2 * GH * GDK + GH * GDV
CW = 512

RAW, WS = 4, 4

SUBS = {}
_n = 0
for _name, _count in (("qkv", 24), ("wo", 8), ("in0", 44), ("out0", 22), ("pool", 2), ("in1", 44), ("out1", 22),
                      ("win", 64), ("bra", 8), ("brb", 8), ("wo2", 8), ("up", 32), ("down", 32), ("pg", 8),
                      ("ple", 2)):
    SUBS[_name] = _n
    _n += _count
NSUB = _n

UNITS = {}
_n = 0
for _name, _count in (("q", 2), ("k", 4), ("v", 4), ("att", 16), ("wo", 2), ("in0", 11), ("out0", 2), ("pool", 2),
                      ("in1", 11), ("out1", 2), ("win", 16),
                      ("bra", 2), ("brb", 2), ("wo2", 2), ("up", 8), ("down", 2), ("pg", 2), ("ple", 2)):
    UNITS[_name] = _n
    _n += _count

GROUPS = {}
_n = 0
for _name, _count in (("x", 4), ("ctx", 4), ("q", 4), ("k", 8), ("att", 16), ("o", 4), ("x1", 4), ("in0", 1),
                      ("pool", 4), ("x3", 4), ("in1", 1), ("rms0", 4), ("glaA", 2), ("mqk", 8), ("oa", 4),
                      ("ob", 4), ("y", 4), ("rms1", 4), ("up", 2), ("rms2", 4), ("p", 1)):
    GROUPS[_name] = _n
    _n += _count

MODS = [(0, m) for m in range(12)] + [(1, m) for m in (6, 7, 8, 9)] + [(1, m) for m in (0, 1, 2, 3, 4, 5, 10, 11)]
MOD_WHICH = {0: 0, 1: 1, 3: 2, 4: 3}
NMOD0 = 4


MODPLAN = {}
for _m, _c, _s, _s2 in ((4, 1, 0, 2), (5, 2, 0, 1), (6, 3, 0, 1), (7, 4, 0, 1), (8, 5, 0, 1)):
    MODPLAN.setdefault((_c, _s), []).append(("sum", _m))
    MODPLAN.setdefault((_c, _s2), []).append(("select", _m))


def mod_sum_in(r):
    return r in (-1, 2, 5, 7, 9, 11, 14)


def mod_is_column(layer, m):
    return m // 2 in (3, 4) or (layer == 0 and m // 2 < 2)


C_ID, C_SELC, C_SELB, C_COS, C_SIN, C_DIST, C_TRI, C_TRS, C_IND, C_END = np.cumsum(
    [0, 128, 2, 128, 64, 64, 512, 128, 128, 2]).tolist()


def shape_constants():
    c = np.zeros((P, C_END), np.float32)
    p = np.arange(P)
    c[:, C_ID:C_ID + P] = np.eye(P)
    for r in range(2):
        c[p % 32 == r, C_SELC + r] = 1.0
    c[p % 32 == 0, C_SELB:C_SELB + P] = 1.0
    row = np.repeat(np.arange(S // 64, dtype=np.float32), 64)
    col = np.tile(np.arange(64, dtype=np.float32), S // 64)
    inv = np.power(np.float32(10000.0), -np.arange(16, dtype=np.float32) / np.float32(16))
    ang = np.concatenate([row[:, None] * inv, col[:, None] * inv], axis=-1).astype(np.float32)
    c[:, C_COS:C_SIN] = np.cos(ang).reshape(TT, P, 32).transpose(1, 0, 2).reshape(P, 64)
    c[:, C_SIN:C_DIST] = np.sin(ang).reshape(TT, P, 32).transpose(1, 0, 2).reshape(P, 64)
    q = np.arange(S)[:, None]
    k = np.arange(S)[None, :]
    dist = np.where(k <= q, (k - q).astype(np.float32), np.float32(-1e30))
    c[:, C_DIST:C_TRI] = dist.reshape(TT, P, S).transpose(1, 0, 2).reshape(P, TT * S)
    same = (p[:, None] // GCH) == (p[None, :] // GCH)
    c[:, C_TRI:C_TRS] = np.where(same & (p[:, None] <= p[None, :]), 1.0 / 16.0, 0.0)
    c[:, C_TRS:C_IND] = np.where(same & (p[:, None] > p[None, :]), 1.0 / 16.0, 0.0)
    for j in range(2):
        c[p // GCH == j, C_IND + j] = 1.0 / 16.0
    w = np.zeros((TT, P, 4, S), np.float32)
    t = np.arange(S)
    for g, win in enumerate(POOL_WINDOWS):
        lo = np.clip(t - win // 2, 0, S)
        hi = np.clip(t + win - win // 2, 0, S)
        m = ((t[:, None] >= lo[None, :]) & (t[:, None] < hi[None, :])).astype(np.float32)
        m = m / (hi - lo).astype(np.float32)[None, :] - np.eye(S, dtype=np.float32)
        w[:, :, g, :] = m.reshape(TT, P, S)
    return c, w.transpose(1, 0, 2, 3).reshape(P, TT * 4 * S).copy()


HIDDEN = {"in0": 0, "in1": 10, "up": 20}

TILE0 = {name: i + 1 for i, name in enumerate(("wo", "out0", "pool", "out1", "brb", "wo2", "down", "pg", "ple"))}

SUB_OF = (("q", "qkv", 4, 0), ("k", "qkv", 4, 8), ("v", "qkv", 4, 16), ("wo", "wo", 0, 4), ("in0", "in0", 4, 0),
          ("out0", "out0", 0, 18), ("pool", "pool", 0, -2), ("in1", "in1", 4, 0), ("out1", "out1", 0, 18),
          ("win", "win", 4, 0), ("bra", "bra", 0, 4), ("brb", "brb", 0, 4), ("wo2", "wo2", 0, 4), ("up", "up", 4, 0),
          ("down", "down", 0, 28), ("pg", "pg", 0, 4), ("ple", "ple", 0, -2))


def summed(stage, j=0):
    _, subs, per, off = next(e for e in SUB_OF if e[0] == stage)
    if stage in ("k", "v"):
        j //= 2
    return SUBS[subs] + off + 4 + per * j


def at_least(eng, sem, value):
    if isinstance(value, int) and value <= 0:
        return
    eng.wait_ge(sem, value)


def build(nc, a, cst_d, pool_d, out):
    ctx = ExitStack()
    with ctx:
        def sem(name):
            return ctx.enter_context(nc.semaphore(name))

        def sb(stack, name, shape, dt=fp32):
            return stack.enter_context(nc.sbuf_tensor(name, shape, dt))

        raw = sb(ctx, "raw", [P, RAW, 2048])
        wH = sb(ctx, "wH", [P, WS, 1024], f32r)
        wL = sb(ctx, "wL", [P, WS, 1024], f32r)
        aH = sb(ctx, "aH", [P, KT, S], f32r)
        aL = sb(ctx, "aL", [P, KT, S], f32r)
        x = sb(ctx, "x", [P, TT, D])
        cst = sb(ctx, "cst", [P, C_END])
        stat = sb(ctx, "stat", [P, 64])
        eps = sb(ctx, "eps", [P, 2])
        bn = sb(ctx, "bn", [P, TT, 12])
        mv = sb(ctx, "mv", [P, TT, 2])
        rows = sb(ctx, "rows", [113, P])
        rows2 = rows[0:82, :]
        gcol = sb(ctx, "gcol", [P, 82])
        lncol = sb(ctx, "lncol", [P, 3, 2, KT])
        lrw = sb(ctx, "lrw", [P, KT, GRANK])
        ps = ctx.enter_context(nc.psum_tensor("ps", [P, 8, 512], fp32))
        ident = cst[:, C_ID:C_ID + P]

        sA = ExitStack()
        modraw = sb(sA, "modraw", [P, 2, 2048])
        lnp = sb(sA, "lnp", [P, 2, D])
        tf = sb(sA, "tf", [P, 2, 512])
        ro = lnp[:, :, :].rearrange("p u (t c) -> p u t c", t=TT)
        te = tf[:, 0, :]
        modrow = sb(sA, "modrow", [P, 512])
        modcol = sb(sA, "modcol", [P, 2, 4, KT, 2])
        bcol = sb(sA, "bcol", [P, 96])
        cT = sb(sA, "cT", [P, KT, 32])
        lamt = sb(sA, "lamt", [P, 256])
        lam2 = sb(sA, "lam2", [P, 8])
        subg = sb(sA, "subg", [P, 2])
        g1b = sb(sA, "g1b", [P, D])
        g2b0 = sb(sA, "g2b0", [P, D])
        sAtt = ExitStack()
        v = sb(sAtt, "v", [P, 4, D])
        qz = sb(sAtt, "qz", [P, H, 2, S])
        kT = sb(sAtt, "kT", [P, H, 512])
        sPrj = ExitStack()
        cH = sb(sPrj, "cH", [P, KT, S], f32r)
        cL = sb(sPrj, "cL", [P, KT, S], f32r)
        rt = sb(sPrj, "rt", [P, 2, TT, 512])
        sPrj.close()
        sCore = ExitStack()
        ex = sb(sCore, "ex", [P, 2, 2, 512])
        am = sb(sCore, "am", [P, 2, 512])
        at = sb(sCore, "at", [P, 2, 4, P])
        ot = sb(sCore, "ot", [P, TT, D])
        sCore.close()
        sAtt.close()
        sIni = ExitStack()
        mod0 = sb(sIni, "mod0", [P, 2 * NMOD0, 2048])
        sIni.close()
        sL1 = ExitStack()
        g2b1 = sb(sL1, "g2b1", [P, D])
        sh1b = sb(sL1, "sh1b", [P, D])
        sc1b = sb(sL1, "sc1b", [P, D])
        psb = sb(sL1, "psb", [P, D])
        sF = ExitStack()
        hH = sb(sF, "hH", [P, F1 // P, S], f32r)
        hL = sb(sF, "hL", [P, F1 // P, S], f32r)
        sil = sb(sF, "sil", [P, 2, TT, 256])
        hid = sb(sF, "hid", [P, 2, TT, 256])
        lnt = sil[:, :, :, :].rearrange("p a t c -> p a (t c)")
        sF.close()
        poolm = modraw[:, 0, :].rearrange("p (t g s) -> p t g s", t=TT, g=4)
        hm = modraw[:, 1, :].rearrange("p (t d) -> p t d", t=TT)
        sL1.close()
        sA.close()

        sB = ExitStack()
        xn = sb(sB, "xn", [P, TT, D])
        sM = ExitStack()
        u = sb(sM, "u", [P, TT, 8192])
        lrH = sb(sM, "lrH", [P, KT, GRANK], f32r)
        lrL = sb(sM, "lrL", [P, KT, GRANK], f32r)
        lrt = sb(sM, "lrt", [P, TT, GRANK])
        lrT = sb(sM, "lrT", [GRANK, S])
        w2 = sb(sM, "w2", [GRANK, 512])
        gbb = sb(sM, "gbb", [P, 512])
        mst = sb(sM, "mst", [P, 2, TT, 16])
        sG = ExitStack()
        la, lt = xn[:, :, 0:512], xn[:, :, 512:D]
        ekd = sb(sG, "ekd", [P, TT, 512])
        ekl = sb(sG, "ekl", [P, TT, 512])
        qkT = sb(sG, "qkT", [P, 2, GH, S])
        aT = ekd[:, :, :].rearrange("p t (h c) -> p t h c", h=GH)
        st = sb(sG, "st", [P, 3, GH, GDV])
        dec = sb(sG, "dec", [P, GH, TT, 2])
        sG.close()
        sQ = ExitStack()
        mT = sb(sQ, "mT", [P, 16, S])
        sc = sb(sQ, "sc", [P, 2, TT, S])
        pe_ = sb(sQ, "pe_", [P, 2, TT, S])
        pT = sb(sQ, "pT", [P, 2, 3 * P])
        sQ.close()
        sM.close()
        sU = ExitStack()
        uH = sb(sU, "uH", [P, F2 // P, S], f32r)
        uL = sb(sU, "uL", [P, F2 // P, S], f32r)
        hu = sb(sU, "hu", [P, 2, TT, 512])
        sU.close()
        sE = ExitStack()
        pt = sb(sE, "pt", [P, TT, 256])
        pH = sb(sE, "pH", [P, 2, S], f32r)
        pL = sb(sE, "pL", [P, 2, S], f32r)
        gate = sb(sE, "gate", [P, TT, D])
        sE.close()
        sB.close()

        gsq = st[:, 0:2, :, :].rearrange("p t h e -> p (t h) e")
        w_raw = [sem(f"w_raw{i}") for i in range(RAW)]
        w_hi, w_lo, w_used = sem("w_hi"), sem("w_lo"), sem("w_used")
        acc_done, acc_out = sem("acc_done"), sem("acc_out")
        t_done, t_f, t_hi, t_lo = sem("t_done"), sem("t_f"), sem("t_hi"), sem("t_lo")
        x_in, ctx_in, rows_in, cst_in = sem("x_in"), sem("ctx_in"), sem("rows_in"), sem("cst_in")
        small_in = sem("small_in")
        mod0_in = [sem(f"mod0_in{i}") for i in range(NMOD0)]
        mod_in = [sem(f"mod_in{i}") for i in range(2)]
        mod_used, mod_acc, mod_row, mod_sel, mod_out = (sem(n) for n in
                                                        ("mod_used", "mod_acc", "mod_row", "mod_sel", "mod_out"))
        bias0_in, bias1_in, pscale_in = sem("bias0_in"), sem("bias1_in"), sem("pscale_in")
        rows_T, cT_zero, cT_ready, qz_zero = sem("rows_T"), sem("cT_zero"), sem("cT_ready"), sem("qz_zero")
        lam_sum, lam_exp = sem("lam_sum"), sem("lam_exp")
        s_max, s_exp, o_done, o_out = (sem(n) for n in ("s_max", "s_exp", "o_done", "o_out"))
        o_sq, o_sd, o_norm = sem("o_sq"), sem("o_sd"), sem("o_norm")
        ln_in, ln_var, ln_sd, ln_x = sem("ln_in"), sem("ln_var"), sem("ln_sd"), sem("ln_x")
        ln_hat, lncol_ready, lnrow_ready, tile0_done = (sem(n) for n in ("ln_hat", "lncol_ready", "lnrow_ready", "tile0_done"))
        silu_done = sem("silu_done")
        h_hi, h_lo = sem("h_hi"), sem("h_lo")
        pool_in, pool_h = sem("pool_in"), sem("pool_h")
        act_self, dve_self, pool_self = sem("act_self"), sem("dve_self"), sem("pool_self")
        rms_sd, xn_ready = sem("rms_sd"), sem("xn_ready")
        rows2_in, rows2_T, gcol_ready = sem("rows2_in"), sem("rows2_T"), sem("gcol_ready")
        lrw_in, lr_hi, lr_lo, lr_done, lr_t, lr_T, lr_Tc = (sem(n) for n in
                                                           ("lrw_in", "lr_hi", "lr_lo", "lr_done", "lr_t", "lr_T", "lr_Tc"))
        vec_in = sem("vec_in")
        z_abs, z_ln, la_ready, dec_sum, dec_exp, e_ready, g_mul = (sem(n) for n in
                                                                  ("z_abs", "z_ln", "la_ready", "dec_sum", "dec_exp", "e_ready", "g_mul"))
        z_done, cum_done, gT_done, gT_out = sem("z_done"), sem("cum_done"), sem("gT_done"), sem("gT_out")
        a_evac, kv_done, kv_out = sem("a_evac"), sem("kv_done"), sem("kv_out")
        go_done, go_evac, go_sq, go_sum, go_sd = (sem(n) for n in ("go_done", "go_evac", "go_sq", "go_sum", "go_sd"))
        oa_ready = sem("oa_ready")
        m_sq, m_sum, m_sd, m_norm = sem("m_sq"), sem("m_sum"), sem("m_sd"), sem("m_norm")
        m_scores, m_max, m_exp, m_T, m_Tc = (sem(n) for n in ("m_scores", "m_max", "m_exp", "m_T", "m_Tc"))
        m_o, m_oout = sem("m_o"), sem("m_oout")
        p_in, x_done, out_done = sem("p_in"), sem("x_done"), sem("out_done")

        def pair(un):
            b = 2 * (un % 2)
            return ps[:, b:b + 2, :]

        def side(j):
            return ps[:, 6:8, :] if j == 0 else ps[:, 4:6, :]

        def tbank(g):
            return ps[:, 4 + g % 2, :]

        block = ctx.enter_context(nc.Block())

        @block.sync
        def _(sp):
            def piece(n, i, parts):
                slot = (n // 2) % RAW
                at_least(sp, w_lo, n - 2 * RAW + 2 + 8 * i if n >= 2 * RAW or not isinstance(i, int) else 0)
                for (lo, hi), src in parts:
                    shape = src.shape
                    dst = raw[:, slot, :].rearrange("p (k c) -> p k c", k=shape[1])[:, :, lo:hi]
                    sp.dma_start(dst, src).then_inc(w_raw[slot], 32 // len(parts))

            def by_k(w):
                return w.rearrange("(k p) n -> p k n", p=P)

            def chunk(n, i, w, c0):
                for h in range(2):
                    piece(n + 4 * 0 + 2 * h, i, [((0, CW), by_k(w)[:, 4 * h:4 * h + 4, bass.ds(c0, CW)])])

            def rows_of(n, w, k0, kn):
                for k in range(k0, k0 + kn, 2):
                    piece(n + k - k0, 0, [((0, D), by_k(w)[:, k:k + 2, :])])

            sp.dma_start(rows[96:104, :], a["c"].rearrange("b (r p) -> (b r) p", p=P)).then_inc(rows_in, 16)
            sp.dma_start(rows[104:112, :], a["c_ctx"].rearrange("(r p) -> r p", p=P)).then_inc(rows_in, 16)
            sp.dma_start(rows[0:96, :], a["b_mod"].rearrange("l (r p) -> (l r) p", p=P)).then_inc(rows_in, 16)
            sp.dma_start(rows[112:113, :], a["attn_subln_g"]).then_inc(rows_in, 16)
            sp.dma_start(cst[:, :], cst_d).then_inc(cst_in, 16)
            for m in range(NMOD0):
                sp.dma_start(mod0[:, 2 * m:2 * m + 2, :].rearrange("p h (k c) -> p (h k) c", k=4),
                             by_k(a["w_mod"][0])[:, :, m * CW:(m + 1) * CW]).then_inc(mod0_in[m], 16)
            sp.dma_start(x[:, :, :], a["x"].rearrange("b (t p) d -> p (b t) d", p=P)).then_inc(x_in, 16)
            for c in range(6):
                chunk(SUBS["qkv"] + 4 * c, 0, a["attn_w_qkv"][0], c * CW)
                if c == 0:
                    sp.dma_start(lnp[:, :, :], a["ctx"].rearrange("b (t p) d -> p (b t) d", p=P)).then_inc(ctx_in, 16)
            rows_of(SUBS["wo"], a["attn_w_o"][0], 0, KT)

            def swiglu_chunk(n, i, w, c0):
                for h in range(2):
                    wk = by_k(w)[:, 4 * h:4 * h + 4, :]
                    piece(n + 2 * h, i, [((256 * s, 256 * s + 256), wk[:, :, bass.ds(c0 + s * F1, 256)])
                                         for s in range(2)])

            def swiglu(layer):
                n = SUBS[f"in{layer}"]
                swiglu_chunk(n, 0, a["ffn_w_in"][layer], 0)
                with sp.Fori(0, 5) as i:
                    for j in range(2):
                        swiglu_chunk(n + 4 + 4 * j, i, a["ffn_w_in"][layer], i * 512 + (256 + 256 * j))
                rows_of(SUBS[f"out{layer}"], a["ffn_w_out"][layer], 0, F1 // P)

            swiglu(0)
            slot = (SUBS["pool"] // 2) % RAW
            sp.wait_ge(w_lo, SUBS["pool"] - 2 * RAW + 2)
            sp.dma_start(raw[:, slot, :].rearrange("p (g c) -> p g c", g=8),
                         a["pool_w"][0].rearrange("g (k p) o -> p (g k) o", p=P)).then_inc(w_raw[slot], 32)
            swiglu(1)
            n = SUBS["win"]
            with sp.Fori(0, 2) as i:
                for j in range(2):
                    chunk(n + 4 * j, i, a["w_in_2"][0], i * (2 * CW) + j * CW)
            with sp.Fori(0, 6) as i:
                for j in range(2):
                    chunk(n + 16 + 4 * j, i, a["w_in_2"][0], i * (2 * CW) + (LR0 + GRANK + j * CW))
            rows_of(SUBS["bra"], a["w_branch_a_2"][0], 0, KT)
            rows_of(SUBS["brb"], a["w_branch_b_2"][0], 0, KT)
            rows_of(SUBS["wo2"], a["w_out_2"][0], 0, KT)
            n = SUBS["up"]
            with sp.Fori(0, 4) as i:
                for j in range(2):
                    chunk(n + 4 * j, i, a["w_up_2"][0], i * (2 * CW) + j * CW)
            rows_of(SUBS["down"], a["w_down_2"][0], 0, F2 // P)
            rows_of(SUBS["pg"], a["w_ple_gate_2"][0], 0, KT)
            rows_of(SUBS["ple"], a["w_ple_2"][0], 0, 2)
            for t in range(TT):
                sp.wait_ge(x_done, t + 1)
                sp.dma_start(out[0, t * P:(t + 1) * P, :], x[:, t, :]).then_inc(out_done, 16)
            sp.wait_ge(out_done, 16 * TT)

        @block.gpsimd
        def _(pool):
            nc.gpsimd.memset(cT[:, :, :], 0.0).then_inc(cT_zero, 1)
            pool.wait_ge(mod0_in[2], 16)
            pool.dma_start(lamt[:, :], a["attn_lambda"].rearrange("a l d -> a (l d)").to_broadcast([P, 256]))\
                .then_inc(small_in, 16)
            pool.dma_start(g1b[:, :], a["b_mod"][0:1, 2 * D:3 * D].to_broadcast([P, D])).then_inc(bias0_in, 16)
            pool.dma_start(g2b0[:, :], a["b_mod"][0:1, 5 * D:6 * D].to_broadcast([P, D])).then_inc(bias0_in, 16)

            pool.wait_ge(rows_T, 1)
            for j, nm in enumerate(("norm_mix_2", "norm_mlp_2", "norm_ple_2")):
                pool.dma_start(rows2[8 * j:8 * j + 8, :], a[nm].rearrange("l (r p) -> (l r) p", p=P))\
                    .then_inc(rows2_in, 16)
            pool.dma_start(rows2[24:32, :], a["gla_out_norm_2"].rearrange("l h (r p) -> (l h r) p", p=P)).then_inc(rows2_in, 16)
            pool.dma_start(rows2[32:33, :], a["moba_k_norm_2"]).then_inc(rows2_in, 16)
            pool.dma_start(rows2[33:34, :], a["moba_q_norm_2"]).then_inc(rows2_in, 16)
            for j in range(6):
                w = (a["ln_g"], a["ln_b"])[j % 2]
                k = (0, 2, 3)[j // 2]
                pool.dma_start(rows2[34 + 8 * j:42 + 8 * j, :],
                               w[k // 2, k % 2:k % 2 + 1, :].rearrange("l (r p) -> (l r) p", p=P)).then_inc(rows2_in, 16)
            with nc.allow_non_contiguous_dma(reason="16 columns of w_in"):
                pool.dma_start(lrw[:, :, :], a["w_in_2"][0].rearrange("(k p) n -> p k n", p=P)[:, :, LR0:LR0 + GRANK])\
                    .then_inc(lrw_in, 16)

            def mod_load(c):
                layer, m = MODS[c]
                wk = a["w_mod"][layer].rearrange("(k p) n -> p k n", p=P)
                for h in range(2):
                    if c > NMOD0:
                        pool.wait_ge(mod_used, 2 * (c - NMOD0 - 1) + h + 1)
                    pool.dma_start(modraw[:, h, :].rearrange("p (k c) -> p k c", k=4),
                                   wk[:, 4 * h:4 * h + 4, m * CW:(m + 1) * CW]).then_inc(mod_in[h], 16)

            def ln_load(k):
                if k == 0:
                    pool.wait_ge(t_done, GROUPS["k"] + 8)
                else:
                    pool.wait_ge(ln_x, TT * k)
                for j, w in enumerate((a["ln_g"], a["ln_b"])):
                    pool.dma_start(lnp[:, j, :], w[k // 2, k % 2:k % 2 + 1, :].to_broadcast([P, D])).then_inc(ln_in, 16)

            mod_load(NMOD0)
            pool.wait_ge(mod_acc, NMOD0)
            nc.gpsimd.memset(qz[:, :, :, :], 0.0).then_inc(qz_zero, 1)
            for c in range(NMOD0 + 1, 16):
                mod_load(c)
                if c == 10:
                    ln_load(0)
            G = nc.gpsimd
            links = [0]

            def link(ins):
                links[0] += 1
                ins.then_inc(pool_self, 1)
                pool.wait_ge(pool_self, links[0])

            def low(n):
                pool.wait_ge(w_hi, n + 1)
                G.tensor_tensor(wL[:, n % WS, :], raw[:, (n // 2) % RAW, (n % 2) * 1024:(n % 2) * 1024 + 1024],
                                wH[:, n % WS, :].bitcast(fp32), ALU.subtract).then_inc(w_lo, 1)

            def finish(k, tiles=range(TT)):
                pool.wait_ge(ln_in, 32 * (k + 1))
                for t in tiles:
                    link(G.tensor_tensor(x[:, t, :], x[:, t, :], lnp[:, 0, :], ALU.mult))
                    G.tensor_tensor(x[:, t, :], x[:, t, :], lnp[:, 1, :], ALU.add).then_inc(ln_x, 1)

            for j in range(4):
                low(SUBS["in0"] + j)
            pool.wait_ge(t_done, GROUPS["x1"] + 4)
            finish(0)
            ln_load(1)
            for dst, j in ((sh1b, 0), (sc1b, 1), (g1b, 2), (g2b1, 5)):
                pool.dma_start(dst[:, :], a["b_mod"][1:2, j * D:(j + 1) * D].to_broadcast([P, D])).then_inc(bias1_in, 16)
            pool.dma_start(psb[:, :], a["pool_scale"].to_broadcast([P, D])).then_inc(pscale_in, 16)
            for c in range(16, 24):
                mod_load(c)
            pool.wait_ge(mod_used, 2 * (len(MODS) - NMOD0))
            pool.dma_start(poolm[:, :, :, :].rearrange("p t g s -> p (t g s)"), pool_d).then_inc(pool_in, 16)
            pool.wait_ge(mod_out, len(MODS))
            pool.wait_ge(pscale_in, 16)
            pool.wait_ge(ln_in, 64)
            link(G.tensor_tensor(g1b[:, :], g1b[:, :], psb[:, :], ALU.mult))
            link(G.tensor_tensor(psb[:, :], lnp[:, 1, :], sc1b[:, :], ALU.mult))
            link(G.tensor_tensor(sh1b[:, :], sh1b[:, :], psb[:, :], ALU.add))
            G.tensor_tensor(sc1b[:, :], sc1b[:, :], lnp[:, 0, :], ALU.mult).then_inc(lnrow_ready, 1)
            pool.wait_ge(lnrow_ready, 1)
            for j in range(2):
                low(SUBS["pool"] + j)
            pool.wait_ge(ln_hat, TT + 1)
            link(G.tensor_tensor(hm[:, 0, :], x[:, 0, :], sc1b[:, :], ALU.mult))
            G.tensor_tensor(hm[:, 0, :], hm[:, 0, :], sh1b[:, :], ALU.add).then_inc(pool_h, 1)
            for j in range(2):
                low(SUBS["in1"] + j)
            pool.wait_ge(ln_hat, 2 * TT)
            finish(1)
            for j in range(2):
                low(SUBS["in1"] + 2 + j)
            ln_load(2)
            pool.wait_ge(t_done, GROUPS["x3"] + 4)
            finish(2)
            ln_load(3)
            for j in range(4):
                low(SUBS["win"] + j)
            pool.wait_ge(t_done, GROUPS["rms0"] + 4)
            finish(3, (1,))
            pool.wait_ge(ln_x, TT * 4)
            pool.dma_start(w2[:, :], a["gla_gate_w2_2"][0]).then_inc(vec_in, 16)
            pool.dma_start(gbb[:, :], a["gla_gate_b_2"].to_broadcast([P, 512])).then_inc(vec_in, 16)
            for t in range(TT):
                pool.wait_ge(a_evac, t + 1)
                nc.gpsimd.affine_select(out=aT[:, t, :, :], in_=aT[:, t, :, :], compare_op=ALU.is_ge, fill=0.0,
                                        base=0, pattern=[[0, GH], [1, P]], channel_multiplier=-1).then_inc(pool_self, 1)
                links[0] += 1
                pool.wait_ge(pool_self, links[0])
                nc.gpsimd.memset(aT[0:GCH, t, :, GCH:P], 0.0).then_inc(t_lo, 1)
            for j in range(4):
                low(SUBS["wo2"] + j)
            for j in range(4):
                low(SUBS["up"] + j)
            for j in range(4):
                low(SUBS["pg"] + j)
            pool.wait_ge(w_used, summed("down"))
            pool.dma_start(pt[:, :, :], a["p_2"][0, 0].rearrange("(t p) d -> p t d", p=P)).then_inc(p_in, 16)

        @block.scalar
        def _(act):
            links = [0]

            def link(ins):
                links[0] += 1
                ins.then_inc(act_self, 1)
                act.wait_ge(act_self, links[0])

            def adv(n, i=0):
                if n >= NSUB:
                    return
                if n % 2 == 0:
                    act.wait_ge(w_raw[(n // 2) % RAW], 32 * (n // 8 + 1) + 32 * i)
                at_least(act, w_used, n - WS + 1 + 8 * i)
                nc.scalar.activation(wH[:, n % WS, :], raw[:, (n // 2) % RAW, (n % 2) * 1024:(n % 2) * 1024 + 1024],
                                     ACT.Copy).then_inc(w_hi, 1)

            def hi(g, dst, i=0, gain=None, mod=None, step=2):
                act.wait_ge(t_done, g + 1 + step * i)
                src = tbank(g).rearrange("p (k s) -> p k s", k=2)
                if gain is not None:
                    for k in range(2):
                        ins = nc.scalar.activation(dst[:, k, :], src[:, k, :], ACT.Copy, scale=gain[:, k:k + 1])
                elif mod is not None:
                    shift, scale = mod
                    tmp = tf[:, g % 2, :].rearrange("p (k s) -> p k s", k=2)
                    for k in range(2):
                        ins = nc.scalar.activation(tmp[:, k, :], src[:, k, :], ACT.Identity,
                                                   bias=shift[:, k:k + 1], scale=scale[:, k:k + 1])
                    link(ins)
                    ins = nc.scalar.activation(dst, tmp, ACT.Copy)
                else:
                    ins = nc.scalar.activation(dst, src, ACT.Copy)
                ins.then_inc(t_hi, 1)

            def hi_t(name, j, gain=None, norm=None):
                g, t, k0 = GROUPS[name] + j, j // 2, 4 * (j % 2)
                act.wait_ge(t_done, g + 1)
                dst = aH[:, k0:k0 + 4, t * P:(t + 1) * P]
                src = tbank(g).rearrange("p (k s) -> p k s", k=4)
                if norm is not None:
                    tmp = tf[:, g % 2, :].rearrange("p (k s) -> p k s", k=4)
                    if j < 3:
                        for k in range(4):
                            ins = nc.scalar.activation(tmp[:, k, :], src[:, k, :], ACT.Identity,
                                                       bias=lncol[:, norm, 1, k0 + k:k0 + k + 1],
                                                       scale=lncol[:, norm, 0, k0 + k:k0 + k + 1])
                        link(ins)
                    else:
                        act.wait_ge(t_f, norm + 1)
                    ins = nc.scalar.activation(dst, tmp, ACT.Copy)
                elif gain is not None and gain is not subg:
                    for k in range(4):
                        ins = nc.scalar.activation(dst[:, k, :], src[:, k, :], ACT.Copy, scale=gain[:, k0 + k:k0 + k + 1])
                else:
                    ins = nc.scalar.activation(dst, src, ACT.Copy, scale=1.0 if gain is None else gain[:, 0:1])
                ins.then_inc(t_hi, 1)

            def modulated(layer, which, stream):
                c = modcol[:, layer, :, :, :]
                return lambda j: (c[:, which, 2 * j:2 * j + 2, stream], c[:, which + 1, 2 * j:2 * j + 2, stream])

            def mod_copy(c):
                if c < NMOD0:
                    act.wait_ge(mod_acc, c + 1)
                else:
                    act.wait_ge(mod_used, 2 * (c - NMOD0) + 2)
                nc.scalar.activation(modrow[:, :], ps[:, c if c < NMOD0 else 7, :], ACT.Copy).then_inc(mod_row, 1)

            act.wait_ge(rows_T, 1)
            act.wait_ge(cT_zero, 1)
            nc.scalar.activation(cT[:, :, 0:2].rearrange("p k r -> p r k"),
                                 ps[:, 6, 96:112].rearrange("p (r k) -> p r k", r=2), ACT.Silu).then_inc(cT_ready, 1)
            nc.scalar.activation(subg[:, :], ps[:, 6, 112:113].to_broadcast([P, 2]), ACT.Copy, scale=1.0 - LAM_INIT)
            nc.scalar.activation(bcol[:, :], ps[:, 6, 0:96], ACT.Copy).then_inc(cT_ready, 1)
            for c in range(NMOD0):
                if c:
                    act.wait_ge(mod_sel, c)
                mod_copy(c)
            act.wait_ge(mod_out, NMOD0)
            mc = modulated(0, 0, 0)
            for j in range(4):
                hi(GROUPS["x"] + j, aH[:, 2 * j:2 * j + 2, :], mod=mc(j))
                adv(j)

            n = SUBS["qkv"]
            modc = [NMOD0]

            def next_mod():
                act.wait_ge(mod_sel, modc[0])
                mod_copy(modc[0])
                modc[0] += 1

            def mod_at(c, sub):
                for kind, m in MODPLAN.get((c, sub), ()):
                    if kind == "sum":
                        act.wait_ge(mod_sel, m)
                        mod_copy(m)
                        modc[0] = m + 1

            def heads_out(c, groups_=range(4)):
                if c < 2:
                    for j in range(2):
                        g = GROUPS["q"] + 2 * c + j
                        act.wait_ge(t_done, g + 1)
                        if c == 0 and j == 0:
                            act.wait_ge(qz_zero, 1)
                        src = tbank(g).rearrange("p (h s) -> p h s", h=2)
                        for m in range(2):
                            ins = nc.scalar.activation(qz[64 * m:64 * m + 64, 4 * c + 2 * j:4 * c + 2 * j + 2, m, :],
                                                       src[64 * m:64 * m + 64, :, :], ACT.Copy)
                        ins.then_inc(t_lo, 1)
                else:
                    for j in groups_:
                        g = GROUPS["k"] + 4 * (c - 2) + j
                        act.wait_ge(t_done, g + 1)
                        h0 = 4 * (c - 2) + 2 * (j % 2)
                        nc.scalar.activation(kT[:, h0:h0 + 2, (j // 2) * 256:(j // 2) * 256 + 256],
                                             tbank(g).rearrange("p (h s) -> p h s", h=2), ACT.Copy).then_inc(t_lo, 1)

            for c in range(6):
                for j in range(3):
                    adv(n + 4 * c + 4 + j)
                    mod_at(c, j)
                if c == 0:
                    mc = modulated(0, 0, 1)
                    for j in range(4):
                        hi(GROUPS["ctx"] + j, cH[:, 2 * j:2 * j + 2, :], mod=mc(j))
                if c == 4:
                    act.wait_ge(lam_sum, 1)
                    nc.scalar.activation(lam2[:, 2:4], lam2[:, 0:2], ACT.Exp).then_inc(lam_exp, 1)
                if c >= 4:
                    un = UNITS["k"] + 2 * (c - 2)
                    for j in range(2):
                        act.wait_ge(w_used, summed("v", 2 * (c - 4)))
                        nc.scalar.activation(v[:, 2 * j:2 * j + 2, (c - 4) * CW:(c - 3) * CW], pair(un + j),
                                             ACT.Copy).then_inc(acc_out, 1)
                        if c == 4:
                            heads_out(c - 1, (2 * j, 2 * j + 1))
                adv(n + 4 * c + 7)
                mod_at(c, 3)
                if 1 <= c <= 3:
                    heads_out(c - 1)

            def exps(r):
                un = UNITS["att"] + r
                act.wait_ge(s_max, r + 1)
                if r >= 2:
                    act.wait_ge(acc_out, UNITS["att"] + r - 1)
                for m in range(2):
                    ins = nc.scalar.activation(ex[:, r % 2, m, :], pair(un)[:, m, :], ACT.Exp,
                                               bias=stat[:, 8 * (r % 2) + m:8 * (r % 2) + m + 1], scale=0.125,
                                               accum_out=stat[:, 8 * (r % 2) + 2 + m:8 * (r % 2) + 3 + m])
                ins.then_inc(s_exp, 1)

            def square(r):
                h, t = r // 2, r % 2
                act.wait_ge(o_out, r + 1)
                at_least(act, o_sq, r)
                nc.scalar.activation(tf[:, 1, 0:P], ot[:, t, h * P:(h + 1) * P], ACT.Square,
                                     accum_out=stat[:, 16 + 8 * t + h:17 + 8 * t + h]).then_inc(o_sq, 1)

            exps(0)
            next_mod()
            for r in range(16):
                if r < 15:
                    exps(r + 1)
                g = GROUPS["att"] + r
                act.wait_ge(t_done, g + 1)
                if r >= 2:
                    act.wait_ge(o_done, r - 1)
                nc.scalar.activation(at[:, r % 2, :, :], tbank(g).rearrange("p (k q) -> p k q", k=4),
                                     ACT.Copy).then_inc(t_lo, 1)
                if r >= 2:
                    square(r - 2)
                if mod_sum_in(r):
                    next_mod()
            for t in range(TT):
                square(14 + t)
                act.wait_ge(o_sq, 15 + t)
                nc.scalar.activation(stat[:, 32 + 8 * t:40 + 8 * t], stat[:, 16 + 8 * t:24 + 8 * t], ACT.Sqrt,
                                     bias=eps[:, 0:1], scale=1.0 / P).then_inc(o_sd, 1)
            for j in range(4):
                hi_t("o", j, gain=subg)
            act.wait_ge(rows2_T, 1)
            nc.scalar.activation(gcol[:, 0:33], ps[:, 6, 0:33], ACT.Copy)
            nc.scalar.activation(gcol[:, 34:82], ps[:, 6, 34:82], ACT.Copy)
            nc.scalar.activation(gcol[:, 33:34], ps[:, 6, 33:34], ACT.Copy, scale=P ** -0.5).then_inc(gcol_ready, 1)
            for j in range(6):
                adv(SUBS["wo"] + 4 + j)

            def sd(k, t):
                act.wait_ge(ln_var, TT * k + t + 1)
                nc.scalar.activation(stat[:, 52 + t:53 + t], mv[:, t, 1:2], ACT.Sqrt, bias=eps[:, 0:1]).then_inc(ln_sd, 1)

            def ln(k, n, name=None):
                sd(k, 0)
                adv(n)
                adv(n + 1)
                if name is None:
                    sd(k, 1)
                    return
                act.wait_ge(lncol_ready, 1)
                norm = (k + 1) // 2
                hi_t(name, 0, norm=norm)
                sd(k, 1)
                for j in range(1, 4):
                    hi_t(name, j, norm=norm)

            def swiglu(layer):
                n, un, g = SUBS[f"in{layer}"], UNITS[f"in{layer}"], GROUPS[f"in{layer}"]

                def one(c, i=0, first=False):
                    for j in range(3):
                        adv(n + 4 * c + 4 + j, i)
                    act.wait_ge(w_used, summed(f"in{layer}", c) + 8 * i)
                    if first:
                        src = pair(un)[:, :, 0:256]
                    else:
                        src = pair(un + c)[:, 0, :].rearrange("p (t c) -> p t c", t=2)
                    nc.scalar.activation(sil[:, c % 2, :, :], src, ACT.Silu).then_inc(silu_done, 1)
                    adv(n + 4 * c + 7, i)

                def high(c, i=0):
                    act.wait_ge(acc_out, un + c + 1 + 2 * i)
                    k0 = 2 * c + 4 * i
                    dst = hH[:, bass.ds(k0, 2), :] if not isinstance(i, int) else hH[:, k0:k0 + 2, :]
                    nc.scalar.activation(dst, hid[:, c % 2, :, :], ACT.Copy).then_inc(h_hi, 1)

                one(0, first=True)
                one(1)
                hi(g, hH[:, 0:2, :])
                one(2)
                high(1)
                with act.Fori(0, 4) as i:
                    one(3, i)
                    high(2, i)
                    one(4, i)
                    high(3, i)
                high(10)
                for k in range(F1 // P - 2):
                    adv(SUBS[f"out{layer}"] + 4 + k)
                    if layer == 0 and k % 2 == 0 and k < 16:
                        next_mod()

            ln(0, SUBS["in0"] + 2, "x1")
            swiglu(0)
            ln(1, SUBS["in1"])
            for j in range(4):
                hi(GROUPS["pool"] + j, aH[:, 2 * j:2 * j + 2, :])
            ln(2, SUBS["in1"] + 2, "x3")
            swiglu(1)
            ln(3, SUBS["win"] + 2, "rms0")

            def rms_tile(t, after, value):
                act.wait_ge(after, value)
                link(nc.scalar.activation(xn[:, t, :], x[:, t, :], ACT.Square, accum_out=stat[:, 56 + t:57 + t]))
                nc.scalar.activation(stat[:, 60 + t:61 + t], stat[:, 56 + t:57 + t], ACT.Sqrt, bias=eps[:, 1:2],
                                     scale=1.0 / D).then_inc(rms_sd, 1)

            def rms(k, after, value, name):
                gain = gcol[:, 8 * k:8 * k + 8]
                rms_tile(0, after, value)
                for j in range(3):
                    adv(SUBS[("up", "pg")[k - 1]] + j)
                hi_t(name, 0, gain=gain)
                adv(SUBS[("up", "pg")[k - 1]] + 3)
                rms_tile(1, after, value + 1)
                for j in range(1, 4):
                    hi_t(name, j, gain=gain)

            act.wait_ge(lrw_in, 16)
            nc.scalar.activation(lrH[:, :, :], lrw[:, :, :], ACT.Copy).then_inc(lr_hi, 1)
            n, un = SUBS["win"], UNITS["win"]

            def beside(c, j):
                if (c, j) == (1, 0):
                    act.wait_ge(lr_done, 1)
                    act.wait_ge(xn_ready, TT)
                    for t in range(TT):
                        ins = nc.scalar.activation(lrt[:, t, :], ps[:, 6, t * GRANK:(t + 1) * GRANK], ACT.Copy,
                                                   scale=stat[:, 62 + t:63 + t])
                    ins.then_inc(lr_t, 1)
                elif (c, j) == (2, 0):
                    act.wait_ge(lr_T, 1)
                    nc.scalar.activation(lrT[:, :], ps[0:GRANK, 6, 0:S], ACT.Copy).then_inc(lr_Tc, 1)
                elif (c, j) == (3, 1):
                    act.wait_ge(z_abs, 1)
                    link(nc.scalar.activation(lt, lt, ACT.Exp, scale=-1.0))
                    nc.scalar.activation(lt, lt, ACT.Ln, bias=1.0).then_inc(z_ln, 1)
                elif (c, j) == (5, 0):
                    act.wait_ge(cum_done, 1)
                    nc.scalar.activation(lt, side(1), ACT.Exp).then_inc(e_ready, 1)
                    nc.scalar.activation(ekd[:, :, :], side(1), ACT.Exp, scale=-1.0).then_inc(e_ready, 1)
                elif (c, j) == (5, 1):
                    act.wait_ge(cum_done, 2)
                    nc.scalar.activation(ekl[:, :, :], side(0), ACT.Exp).then_inc(e_ready, 1)
                elif (c, j) == (6, 0):
                    act.wait_ge(dec_sum, 1)
                    nc.scalar.activation(dec[:, :, :, :].rearrange("p h t j -> p (h t j)"), ps[:, 6, 0:16], ACT.Exp)\
                        .then_inc(dec_exp, 1)
                elif c == 7 and j < 2:
                    act.wait_ge(gT_done, j + 1)
                    nc.scalar.activation(qkT[:, j, :, :].rearrange("p (a h) s -> p a (h s)", a=2), side(1 - j), ACT.Copy)\
                        .then_inc(gT_out, 1)
                elif c == 8 and j < 2:
                    g = GROUPS["glaA"] + j
                    act.wait_ge(t_done, g + 1)
                    nc.scalar.activation(ekd[:, j, :], tbank(g), ACT.Copy).then_inc(a_evac, 1)
                elif c == 10 and j < 2:
                    act.wait_ge(acc_out, un + 10)
                    nc.scalar.activation(u[:, j, 6144:8192], u[:, j, 3072:5120], ACT.Square).then_inc(m_sq, 1)
                elif (c, j) == (11, 0):
                    act.wait_ge(m_sum, 1)
                    nc.scalar.activation(mst[:, 1, :, :], mst[:, 0, :, :], ACT.Sqrt, bias=eps[:, 1:2], scale=1.0 / P)\
                        .then_inc(m_sd, 1)
                elif c in (11, 12) and j == 1:
                    t = c - 11
                    act.wait_ge(go_done, t + 1)
                    nc.scalar.activation(xn[:, t, :].rearrange("p (b c) -> p b c", b=2), side(t), ACT.Copy)\
                        .then_inc(go_evac, 1)
                    if t == 1:
                        act.wait_ge(go_evac, TT)
                        nc.scalar.activation(gsq, xn[:, :, :].rearrange("p t (h e) -> p (t h) e", e=GDV), ACT.Square)\
                            .then_inc(go_sq, 1)
                elif (c, j) == (12, 3):
                    act.wait_ge(go_sum, 1)
                    nc.scalar.activation(stat[:, 8:16], stat[:, 0:8], ACT.Sqrt, bias=eps[:, 1:2], scale=1.0 / GDV)\
                        .then_inc(go_sd, 1)
                if c >= 13 and j == 0:
                    mqk_out(c - 13)

            def mqk_out(step):
                for j in (2 * step, 2 * step + 1):
                    g = GROUPS["mqk"] + j
                    act.wait_ge(t_done, g + 1)
                    nc.scalar.activation(mT[:, 2 * j:2 * j + 2, :], tbank(g).rearrange("p (h s) -> p h s", h=2), ACT.Copy,
                                         scale=gcol[:, 33:34] if j < 4 else gcol[:, 32:33]).then_inc(t_lo, 1)

            for c in range(16):
                for j in range(3):
                    adv(n + 4 * c + 4 + j)
                    beside(c, j)
                if c == 0:
                    for t in range(TT):
                        rms_tile(t, ln_x, 8)
                    act.wait_ge(xn_ready, TT)
                act.wait_ge(w_used, summed("win", c))
                for t in range(TT):
                    ins = nc.scalar.activation(u[:, t, c * CW:(c + 1) * CW], pair(un + c)[:, t, :],
                                               ACT.Silu if c in (4, 5) else ACT.Sigmoid if c >= 12 else ACT.Copy,
                                               scale=stat[:, 62 + t:63 + t])
                ins.then_inc(acc_out, 1)
                adv(n + 4 * c + 7)
                beside(c, 3)
            mqk_out(3)
            for j in range(4):
                hi(GROUPS["oa"] + j, aH[:, 2 * j:2 * j + 2, :], gain=gcol[:, 24 + 2 * j:26 + 2 * j])

            def mexp(h):
                b = 8 * (h % 4)
                act.wait_ge(m_max, h + 1)
                if h >= 2:
                    act.wait_ge(m_T, h - 1)
                for t in range(TT):
                    ins = nc.scalar.activation(pe_[:, h % 2, t, :], sc[:, h % 2, t, :], ACT.Exp,
                                               bias=stat[:, b + t:b + t + 1],
                                               accum_out=stat[:, b + 2 + t:b + 3 + t])
                ins.then_inc(m_exp, 1)

            mexp(0)
            for h in range(H):
                adv(SUBS["bra"] + 4 + h)
                if h + 1 < H:
                    mexp(h + 1)
                act.wait_ge(m_T, h + 1)
                if h >= 2:
                    act.wait_ge(m_o, h - 1)
                nc.scalar.activation(pT[:, h % 2, :], ps[:, 4, 0:3 * P], ACT.Copy).then_inc(m_Tc, 1)
            for j in range(4):
                hi_t("ob", j)
            for j in range(7):
                adv(SUBS["brb"] + 4 + j)
            hi_t("y", 0)
            adv(SUBS["brb"] + 11)
            for j in range(1, 4):
                hi_t("y", j)
            for j in range(4):
                adv(SUBS["wo2"] + 4 + j)
            rms(1, acc_out, UNITS["wo2"] + 1, "rms1")
            n, un, g = SUBS["up"], UNITS["up"], GROUPS["up"]

            def up(c, i=0):
                for j in range(4):
                    adv(n + 4 * c + 4 + j, i)
                if isinstance(i, int) and c == 1:
                    return
                high(c - 1, i)

            def square_up(c, i=0):
                act.wait_ge(acc_out, un + c + 1 + 2 * i)
                return nc.scalar.activation(hu[:, c % 2, :, :], hu[:, c % 2, :, :], ACT.Square)

            def high(c, i=0):
                square_up(c, i).then_inc(silu_done, 1)
                act.wait_ge(silu_done, 22 + c + 1 + 2 * i)
                k0 = 4 * c + 8 * i
                dst = uH[:, k0:k0 + 4, :] if isinstance(i, int) else uH[:, bass.ds(k0, 4), :]
                nc.scalar.activation(dst, hu[:, c % 2, :, :].rearrange("p t (k s) -> p (t k) s", s=S), ACT.Copy)\
                    .then_inc(h_hi, 1)

            for j in range(4):
                adv(n + 4 + j)
            square_up(0).then_inc(silu_done, 1)
            up(1)
            for j in range(2):
                hi(g + j, uH[:, 2 * j:2 * j + 2, :])
            with act.Fori(0, 3) as i:
                up(2, i)
                up(3, i)
            high(7)
            for k in range(F2 // P - 4):
                adv(SUBS["down"] + 4 + k)
            rms(2, acc_out, UNITS["down"] + 1, "rms2")
            for j in range(4):
                adv(SUBS["pg"] + 4 + j)
            hi(GROUPS["p"], pH[:, :, :])
            for j in range(4, 8):
                adv(SUBS["pg"] + 4 + j)
            for t in range(TT):
                un = UNITS["pg"] + t
                if t == 0:
                    act.wait_ge(tile0_done, TILE0["pg"])
                else:
                    act.wait_ge(w_used, summed("pg"))
                nc.scalar.activation(gate[:, t, :].rearrange("p (b c) -> p b c", b=2), pair(un), ACT.Sigmoid)\
                    .then_inc(acc_out, 1)

        @block.vector
        def _(dve):
            links = [0]

            def link(ins):
                links[0] += 1
                ins.then_inc(dve_self, 1)
                dve.wait_ge(dve_self, links[0])

            V = nc.vector

            def adv(n, i=0):
                if n >= NSUB:
                    return
                dve.wait_ge(w_hi, n + 1 + 8 * i)
                V.tensor_tensor(wL[:, n % WS, :], raw[:, (n // 2) % RAW, (n % 2) * 1024:(n % 2) * 1024 + 1024],
                                wH[:, n % WS, :].bitcast(fp32), ALU.subtract).then_inc(w_lo, 1)

            def lo(g, dst, high, i=0, gain=None, mod=False, step=2, k_hi=None):
                dve.wait_ge(t_hi, k_hi + 1 + step * i)
                src = tbank(g).rearrange("p (k s) -> p k s", k=2)
                if gain is not None:
                    for k in range(2):
                        ins = V.scalar_tensor_tensor(out=dst[:, k, :], in0=src[:, k, :], scalar=gain[:, k:k + 1],
                                                     in1=high[:, k, :].bitcast(fp32), op0=ALU.mult, op1=ALU.subtract)
                elif mod:
                    ins = V.tensor_tensor(dst, tf[:, g % 2, :].rearrange("p (k s) -> p k s", k=2),
                                          high.bitcast(fp32), ALU.subtract)
                else:
                    ins = V.tensor_tensor(dst, src, high.bitcast(fp32), ALU.subtract)
                ins.then_inc(t_lo, 1)

            hcount = [0]

            def lo_t(name, j, gain=None, norm=None):
                g, t, k0 = GROUPS[name] + j, j // 2, 4 * (j % 2)
                hcount[0] += 1
                dve.wait_ge(t_hi, hcount[0])
                dst, high = aL[:, k0:k0 + 4, t * P:(t + 1) * P], aH[:, k0:k0 + 4, t * P:(t + 1) * P]
                src = tbank(g).rearrange("p (k s) -> p k s", k=4)
                if norm is not None:
                    ins = V.tensor_tensor(dst, tf[:, g % 2, :].rearrange("p (k s) -> p k s", k=4), high.bitcast(fp32),
                                          ALU.subtract)
                elif gain is subg:
                    ins = V.scalar_tensor_tensor(out=dst, in0=src, scalar=gain[:, 0:1], in1=high.bitcast(fp32),
                                                 op0=ALU.mult, op1=ALU.subtract)
                elif gain is not None:
                    for k in range(4):
                        ins = V.scalar_tensor_tensor(out=dst[:, k, :], in0=src[:, k, :], scalar=gain[:, k0 + k:k0 + k + 1],
                                                     in1=high[:, k, :].bitcast(fp32), op0=ALU.mult, op1=ALU.subtract)
                else:
                    ins = V.tensor_tensor(dst, src, high.bitcast(fp32), ALU.subtract)
                ins.then_inc(t_lo, 1)

            def product_done(stage, t):
                if t == 0:
                    dve.wait_ge(tile0_done, TILE0[stage])
                else:
                    dve.wait_ge(w_used, summed(stage))

            def lo4(name, L_, H_, **kw):
                gain = kw.pop("gain", None)
                for j in range(4):
                    lo(GROUPS[name] + j, L_[:, 2 * j:2 * j + 2, :], H_[:, 2 * j:2 * j + 2, :],
                       gain=None if gain is None else gain[:, 2 * j:2 * j + 2], k_hi=hcount[0], **kw)
                    hcount[0] += 1

            def mod_put(c):
                layer, m = MODS[c]
                one = 1.0 if m // 2 in (1, 4) else 0.0
                dve.wait_ge(mod_sel, c + 1)
                if mod_is_column(layer, m):
                    b0 = 48 * layer + 4 * m
                    V.scalar_tensor_tensor(
                        out=modcol[:, layer, MOD_WHICH[m // 2], 4 * (m % 2):4 * (m % 2) + 4, :],
                        in0=ps[:, 7, 0:8].rearrange("p (k r) -> p k r", r=2), scalar=one,
                        in1=bcol[:, b0:b0 + 4].unsqueeze(2).to_broadcast([P, 4, 2]),
                        op0=ALU.add, op1=ALU.add).then_inc(mod_out, 1)
                else:
                    dst = {(0, 2): g1b, (0, 5): g2b0, (1, 0): sh1b, (1, 1): sc1b, (1, 2): g1b, (1, 5): g2b1}[layer, m // 2]
                    dst = dst[:, (m % 2) * CW:(m % 2) * CW + CW]
                    if layer == 0:
                        dve.wait_ge(bias0_in, 32)
                    else:
                        dve.wait_ge(bias1_in, 64)
                    V.scalar_tensor_tensor(out=dst, in0=ps[:, 7, :], scalar=one, in1=dst,
                                           op0=ALU.add, op1=ALU.add).then_inc(mod_out, 1)

            for j, value in enumerate((LN_EPS, RMS_EPS)):
                V.memset(eps[:, j:j + 1], value)
            dve.wait_ge(cT_ready, 2)
            for c in range(NMOD0):
                mod_put(c)
            for j in range(4):
                lo(GROUPS["x"] + j, aL[:, 2 * j:2 * j + 2, :], aH[:, 2 * j:2 * j + 2, :], mod=True, k_hi=hcount[0])
                hcount[0] += 1
                adv(j)

            modc = [NMOD0]

            def next_mod():
                mod_put(modc[0])
                modc[0] += 1

            def mod_at(c, sub):
                for kind, m in MODPLAN.get((c, sub), ()):
                    if kind == "select":
                        mod_put(m)
                        modc[0] = m + 1

            rots = [0]

            def rotate(un, done, plain):
                dve.wait_ge(w_used, done)
                rs = ro[:, rots[0] % 2, :, :]
                if rots[0] >= 2:
                    dve.wait_ge(t_done, GROUPS["q"] + 2 * (rots[0] - 1))
                if plain:
                    V.tensor_copy(rs, pair(un)).then_inc(acc_out, 1)
                else:
                    for t in range(TT):
                        src = pair(un)[:, t, :].rearrange("p (m h d) -> p m h d", h=2, d=32)
                        for j, tab in enumerate((C_COS, C_SIN)):
                            cs = cst[:, tab + 32 * t:tab + 32 * t + 32].unsqueeze(1).unsqueeze(1).to_broadcast([P, 8, 2, 32])
                            ins = V.tensor_tensor(rt[:, j, t, :].rearrange("p (m h d) -> p m h d", h=2, d=32), src, cs,
                                                  ALU.mult)
                    link(ins)
                    for t in range(TT):
                        c_, s_ = (rt[:, j, t, :].rearrange("p (m h d) -> p m h d", h=2, d=32) for j in range(2))
                        o_ = rs[:, t, :].rearrange("p (m h d) -> p m h d", h=2, d=32)
                        V.tensor_tensor(o_[:, :, 0, :], c_[:, :, 0, :], s_[:, :, 1, :], ALU.subtract)
                        ins = V.tensor_tensor(o_[:, :, 1, :], s_[:, :, 0, :], c_[:, :, 1, :], ALU.add)
                    ins.then_inc(acc_out, 1)
                rots[0] += 1

            n = SUBS["qkv"]
            for c in range(6):
                for j in range(3):
                    adv(n + 4 * c + 4 + j)
                    mod_at(c, j)
                if c == 0:
                    lo4("ctx", cL, cH, mod=True)
                if c < 2:
                    rotate(UNITS["q"] + c, summed("q", c), False)
                elif c < 4:
                    rotate(UNITS["k"] + 2 * (c - 2), summed("k", 2 * (c - 2)), True)
                    rotate(UNITS["k"] + 2 * (c - 2) + 1, summed("k", 2 * (c - 2)), False)
                adv(n + 4 * c + 7)
                mod_at(c, 3)
                if c == 3:
                    dve.wait_ge(small_in, 16)
                    lv = lamt[:, :].rearrange("p (a b d) -> p a b d", a=2, b=2)
                    link(V.tensor_tensor(lv[:, :, 0, :], lv[:, :, 0, :], lv[:, :, 1, :], ALU.mult))
                    V.tensor_reduce(lam2[:, 0:2], lv[:, :, 0, :], AXX, ALU.add).then_inc(lam_sum, 1)
            dve.wait_ge(lam_exp, 1)
            link(V.tensor_tensor(lam2[:, 4:5], lam2[:, 2:3], lam2[:, 3:4], ALU.subtract))
            link(V.tensor_scalar(lam2[:, 5:6], lam2[:, 4:5], LAM_INIT, None, ALU.add))

            def mix(r):
                b = 8 * (r % 2)
                dve.wait_ge(s_exp, r + 1)
                link(V.reciprocal(stat[:, b + 4:b + 6], stat[:, b + 2:b + 4]))
                link(V.tensor_tensor(stat[:, b + 6:b + 7], stat[:, b + 5:b + 6], lam2[:, 5:6], ALU.mult))
                link(V.tensor_scalar(te, ex[:, r % 2, 1, :], stat[:, b + 6:b + 7], None, ALU.mult))
                if r >= 2:
                    dve.wait_ge(t_done, GROUPS["att"] + r - 1)
                V.scalar_tensor_tensor(out=am[:, r % 2, :], in0=ex[:, r % 2, 0, :], scalar=stat[:, b + 4:b + 5],
                                       in1=te, op0=ALU.mult, op1=ALU.subtract).then_inc(acc_out, 1)

            def put_o(r):
                h, t = r // 2, r % 2
                dve.wait_ge(o_done, r + 1)
                V.tensor_copy(ot[:, t, h * P:(h + 1) * P], ps[:, 6, 0:P]).then_inc(o_out, 1)

            def maxima(r):
                b = 8 * (r % 2)
                dve.wait_ge(acc_done, r + 1)
                link(V.tensor_reduce(stat[:, b + 6:b + 8], pair(UNITS["att"] + r), AXX, ALU.max))
                V.tensor_scalar(stat[:, b:b + 2], stat[:, b + 6:b + 8], -0.125, None, ALU.mult).then_inc(s_max, 1)

            maxima(0)
            maxima(1)
            for r in range(16):
                mix(r)
                if r < 14:
                    maxima(r + 2)
                if mod_sum_in(r - 1):
                    next_mod()
                if r >= 1:
                    put_o(r - 1)
            put_o(15)
            for t in range(TT):
                o3 = ot[:, t, :].rearrange("p (h d) -> p h d", d=P)
                dve.wait_ge(o_sd, t + 1)
                link(V.reciprocal(stat[:, 16 + 8 * t:24 + 8 * t], stat[:, 32 + 8 * t:40 + 8 * t]))
                V.tensor_tensor(o3, o3, stat[:, 16 + 8 * t:24 + 8 * t].unsqueeze(2).to_broadcast([P, H, P]), ALU.mult)\
                    .then_inc(o_norm, 1)
            for j in range(4):
                lo_t("o", j, gain=subg)
            for j in range(4):
                adv(SUBS["wo"] + 4 + j)
            dve.wait_ge(gcol_ready, 1)
            for k in range(2):
                gc = [gcol[:, 34 + 16 * k + 8 * j:42 + 16 * k + 8 * j] for j in range(2)]
                shift, scale = (modcol[:, k, which, :, 0:1].rearrange("p k r -> p (k r)") for which in (2, 3))
                V.tensor_tensor(lncol[:, k, 0, :], gc[0], scale, ALU.mult)
                link(V.tensor_tensor(lncol[:, k, 1, :], gc[1], scale, ALU.mult))
                V.tensor_tensor(lncol[:, k, 1, :], lncol[:, k, 1, :], shift, ALU.add)
            for j in range(2):
                ins = V.tensor_tensor(lncol[:, 2, j, :], gcol[:, 66 + 8 * j:74 + 8 * j], gcol[:, 0:8], ALU.mult)
            ins.then_inc(lncol_ready, 1)

            def ln(k, stage, gate_, name=None):
                un = UNITS[stage]
                norm = (k + 1) // 2
                for t in range(TT):
                    product_done(stage, t)
                    V.tensor_tensor(lnt, pair(un + t), gate_[:, :].rearrange("p (b c) -> p b c", b=2), ALU.mult)\
                        .then_inc(acc_out, 1)
                    dve.wait_ge(acc_out, un + t + 1)
                    if k and t == 0:
                        dve.wait_ge(ln_x, TT * k)
                    link(V.scalar_tensor_tensor(out=x[:, t, :], in0=x[:, t, :], scalar=ALPHA,
                                                in1=lnt.rearrange("p b c -> p (b c)"), op0=ALU.mult, op1=ALU.add))
                    if t == 1 and name is not None:
                        lo_t(name, 0, norm=norm)
                    V.bn_stats(bn[:, t, 0:6], x[:, t, 0:512])
                    link(V.bn_stats(bn[:, t, 6:12], x[:, t, 512:1024]))
                    V.bn_aggr(mv[:, t, :], bn[:, t, :]).then_inc(ln_var, 1)
                    if k == 1 and t == 1:
                        dve.wait_ge(lnrow_ready, 1)
                        dve.wait_ge(ln_var, TT * k + t + 1)
                        V.scalar_tensor_tensor(out=hm[:, 1, :], in0=x[:, 1, :], scalar=mv[:, 1, 0:1], in1=sc1b[:, :],
                                               op0=ALU.subtract, op1=ALU.mult)
                    dve.wait_ge(ln_sd, TT * k + t + 1)
                    link(V.reciprocal(stat[:, 54 + t:55 + t], stat[:, 52 + t:53 + t]))
                    if k == 1 and t == 1:
                        V.scalar_tensor_tensor(out=hm[:, 1, :], in0=hm[:, 1, :], scalar=stat[:, 55:56], in1=sh1b[:, :],
                                               op0=ALU.mult, op1=ALU.add).then_inc(pool_h, 1)
                    V.tensor_scalar(x[:, t, :], x[:, t, :], mv[:, t, 0:1], stat[:, 54 + t:55 + t],
                                    ALU.subtract, ALU.mult).then_inc(ln_hat, 1)
                if name is not None:
                    lo_t(name, 1, norm=norm)
                    g = GROUPS[name] + 3
                    dve.wait_ge(t_done, g + 1)
                    f = tf[:, g % 2, :].rearrange("p (k s) -> p k s", k=4)
                    cols = [lncol[:, norm, j, 4:8].unsqueeze(2).to_broadcast([P, 4, P]) for j in range(2)]
                    link(V.tensor_tensor(f, tbank(g).rearrange("p (k s) -> p k s", k=4), cols[0], ALU.mult))
                    V.tensor_tensor(f, f, cols[1], ALU.add).then_inc(t_f, 1)
                    lo_t(name, 2, norm=norm)
                    lo_t(name, 3, norm=norm)

            def swiglu(layer):
                n, un, g = SUBS[f"in{layer}"], UNITS[f"in{layer}"], GROUPS[f"in{layer}"]
                k_hi = hcount[0]
                sbase = 11 * layer

                def low(c, i=0):
                    k0 = 2 * c + 4 * i
                    d, h = (hL[:, k0:k0 + 2, :], hH[:, k0:k0 + 2, :]) if isinstance(i, int) else \
                           (hL[:, bass.ds(k0, 2), :], hH[:, bass.ds(k0, 2), :])
                    dve.wait_ge(h_hi, HIDDEN[f"in{layer}"] + c + 2 * i)
                    V.tensor_tensor(d, hid[:, c % 2, :, :], h.bitcast(fp32), ALU.subtract).then_inc(h_lo, 1)

                def one(c, i=0, first=False):
                    for j in range(3):
                        adv(n + 4 * c + 4 + j, i)
                    dve.wait_ge(silu_done, sbase + c + 1 + 2 * i)
                    if first:
                        other = pair(un)[:, :, 256:512]
                    else:
                        other = pair(un + c)[:, 1, :].rearrange("p (t c) -> p t c", t=2)
                    if c >= 3:
                        dve.wait_ge(h_lo, HIDDEN[f"in{layer}"] + c - 2 + 2 * i)
                    V.tensor_tensor(hid[:, c % 2, :, :], sil[:, c % 2, :, :], other, ALU.mult).then_inc(acc_out, 1)
                    adv(n + 4 * c + 7, i)

                one(0, first=True)
                one(1)
                lo(g, hL[:, 0:2, :], hH[:, 0:2, :], k_hi=k_hi)
                one(2)
                low(1)
                with dve.Fori(0, 4) as i:
                    one(3, i)
                    low(2, i)
                    one(4, i)
                    low(3, i)
                low(10)
                hcount[0] += 1
                for k in range(F1 // P - 4):
                    adv(SUBS[f"out{layer}"] + 4 + k)
                    if layer == 0 and k % 2 == 1 and k < 16:
                        next_mod()

            ln(0, "wo", g1b, "x1")
            swiglu(0)
            ln(1, "out0", g2b0)
            lo4("pool", aL, aH)
            ln(2, "pool", g1b, "x3")
            swiglu(1)
            ln(3, "out1", g2b1, "rms0")
            dve.wait_ge(ln_in, 128)
            dve.wait_ge(t_done, GROUPS["rms0"] + 2)
            link(V.tensor_tensor(x[:, 0, :], x[:, 0, :], lnp[:, 0, :], ALU.mult))
            V.tensor_tensor(x[:, 0, :], x[:, 0, :], lnp[:, 1, :], ALU.add).then_inc(ln_x, 1)

            def rms(k, name, stage):
                gain = gcol[:, 8 * k:8 * k + 8]
                for t in range(TT):
                    if t == 1:
                        lo_t(name, 0, gain=gain)
                    product_done(stage, t)
                    xt = x[:, t, :].rearrange("p (b c) -> p b c", b=2)
                    V.tensor_tensor(xt, pair(UNITS[stage] + t), xt, ALU.add).then_inc(acc_out, 1)
                    dve.wait_ge(rms_sd, TT * k + t + 1)
                    link(V.reciprocal(stat[:, 62 + t:63 + t], stat[:, 60 + t:61 + t]))
                    V.tensor_scalar(xn[:, t, :], x[:, t, :], stat[:, 62 + t:63 + t], None, ALU.mult).then_inc(xn_ready, 1)
                for j in range(1, 4):
                    lo_t(name, j, gain=gain)

            dve.wait_ge(lr_hi, 1)
            V.tensor_tensor(lrL[:, :, :], lrw[:, :, :], lrH[:, :, :].bitcast(fp32), ALU.subtract).then_inc(lr_lo, 1)
            n = SUBS["win"]
            gq, gk = u[:, :, 0:512], u[:, :, 512:1024]
            o4g = xn[:, :, :].rearrange("p t (h e) -> p t h e", e=GDV)
            mqk = u[:, :, 3072:5120].rearrange("p t (g d) -> p t g d", d=P)

            def beside(c, j):
                if (c, j) == (3, 0):
                    dve.wait_ge(z_done, 1)
                    dve.wait_ge(vec_in, 32)
                    link(V.tensor_tensor(la, side(0), gbb[:, :].unsqueeze(1).to_broadcast([P, TT, 512]), ALU.add))
                    V.scalar_tensor_tensor(out=lt, in0=la, scalar=-1.0, in1=la,
                                           op0=ALU.mult, op1=ALU.max).then_inc(z_abs, 1)
                elif (c, j) == (3, 2):
                    dve.wait_ge(z_ln, 1)
                    V.scalar_tensor_tensor(out=la, in0=la, scalar=0.0, in1=lt,
                                           op0=ALU.min, op1=ALU.subtract).then_inc(la_ready, 1)
                elif (c, j) == (5, 1):
                    dve.wait_ge(e_ready, 1)
                    V.scalar_tensor_tensor(out=gq, in0=gq, scalar=GDK ** -0.5, in1=lt, op0=ALU.mult, op1=ALU.mult)\
                        .then_inc(g_mul, 1)
                elif (c, j) == (5, 2):
                    dve.wait_ge(e_ready, 2)
                    V.tensor_tensor(ekd[:, :, :], ekd[:, :, :], gk, ALU.mult).then_inc(g_mul, 1)
                elif (c, j) == (5, 3):
                    dve.wait_ge(e_ready, 3)
                    V.tensor_tensor(ekl[:, :, :], ekl[:, :, :], gk, ALU.mult).then_inc(g_mul, 1)
                elif c in (8, 9, 10) and j == 0:
                    k = c - 8
                    dve.wait_ge(kv_done, k + 1)
                    if k == 0:
                        ins = V.tensor_copy(st[:, 0, :, :].rearrange("p (a h) e -> p a (h e)", a=2), side(0))
                    else:
                        dve.wait_ge(dec_exp, 1)
                        dve.wait_ge(kv_out, k)
                        for h in range(GH):
                            ins = V.scalar_tensor_tensor(out=st[:, k, h, :], in0=st[:, k - 1, h, :],
                                                         scalar=dec[:, h, k // 2, k % 2:k % 2 + 1],
                                                         in1=ps[:, 6 + h // 2, (h % 2) * GDV:(h % 2) * GDV + GDV],
                                                         op0=ALU.mult, op1=ALU.add)
                    ins.then_inc(kv_out, 1)
                elif (c, j) in ((10, 1), (10, 3)):
                    t = j // 2
                    dve.wait_ge(m_sq, t + 1)
                    V.tensor_reduce(mst[:, 0, t, :], u[:, t, 6144:8192].rearrange("p (g d) -> p g d", d=P), AXX, ALU.add)\
                        .then_inc(m_sum if t else dve_self, 1)
                    links[0] += 1 - t
                elif (c, j) == (11, 1):
                    dve.wait_ge(m_sd, 1)
                    link(V.reciprocal(mst[:, 0, :, :], mst[:, 1, :, :]))
                if c == 11 and j in (1, 2):
                    t = j - 1
                    V.tensor_tensor(mqk[:, t, :, :], mqk[:, t, :, :], mst[:, 0, t, :].unsqueeze(2)
                                    .to_broadcast([P, 16, P]), ALU.mult).then_inc(m_norm, 1)
                elif (c, j) == (12, 2):
                    dve.wait_ge(go_sq, 1)
                    V.tensor_reduce(stat[:, 0:8], gsq, AXX, ALU.add).then_inc(go_sum, 1)
                elif (c, j) == (13, 0):
                    dve.wait_ge(go_sd, 1)
                    link(V.reciprocal(stat[:, 0:8], stat[:, 8:16]))
                    link(V.tensor_tensor(o4g, o4g, stat[:, 0:8].rearrange("p (t h) -> p t h", t=TT).unsqueeze(3)
                                         .to_broadcast([P, TT, GH, GDV]), ALU.mult))
                elif (c, j) == (13, 2):
                    dve.wait_ge(acc_out, UNITS["win"] + 6)
                    V.tensor_tensor(xn[:, :, :], xn[:, :, :], u[:, :, 2048:3072], ALU.mult).then_inc(oa_ready, 1)

            for c in range(16):
                for j in range(4):
                    adv(n + 4 * c + 4 + j)
                    beside(c, j)
                    if (c, j) == (0, 2):
                        for t in range(TT):
                            dve.wait_ge(rms_sd, t + 1)
                            V.reciprocal(stat[:, 62 + t:63 + t], stat[:, 60 + t:61 + t]).then_inc(xn_ready, 1)
            dist = cst[:, C_DIST:C_TRI].rearrange("p (t k) -> p t k", t=TT)
            ob = xn

            def mmax(h):
                b = 8 * (h % 4)
                dve.wait_ge(m_scores, h + 1)
                if h >= 2:
                    dve.wait_ge(m_exp, h - 1)
                link(V.scalar_tensor_tensor(out=sc[:, h % 2, :, :], in0=dist, scalar=2.0 ** -(h + 1),
                                            in1=ps[:, 6 + h % 2, :].rearrange("p (t k) -> p t k", t=TT),
                                            op0=ALU.mult, op1=ALU.add))
                V.tensor_reduce(stat[:, b:b + 2], sc[:, h % 2, :, :], AXX, ALU.max, negate=True).then_inc(m_max, 1)

            def moba_out(h):
                b = 8 * (h % 4)
                dve.wait_ge(m_exp, h + 1)
                link(V.reciprocal(stat[:, b + 4:b + 6], stat[:, b + 2:b + 4]))
                dve.wait_ge(m_o, h + 1)
                for t in range(TT):
                    ins = V.tensor_scalar(ob[:, t, h * P:(h + 1) * P], ps[:, 5, t * P:(t + 1) * P],
                                          stat[:, b + 4 + t:b + 5 + t], None, ALU.mult)
                ins.then_inc(m_oout, 1)

            lo4("oa", aL, aH, gain=gcol[:, 24:32])
            mmax(0)
            mmax(1)
            for h in range(H):
                adv(SUBS["bra"] + 4 + h)
                if h + 2 < H:
                    mmax(h + 2)
                if h >= 1:
                    moba_out(h - 1)
            ga, gb = u[:, :, 6144:7168], u[:, :, 7168:8192]
            for t in range(TT):
                dve.wait_ge(w_used, summed("bra"))
                V.tensor_tensor(ga[:, t, :].rearrange("p (b c) -> p b c", b=2), pair(UNITS["bra"] + t),
                                ga[:, t, :].rearrange("p (b c) -> p b c", b=2), ALU.mult).then_inc(acc_out, 1)
                if t == 0:
                    moba_out(H - 1)
            for j in range(4):
                lo_t("ob", j)
            for j in range(4):
                adv(SUBS["brb"] + 4 + j)
            for t in range(TT):
                if t == 1:
                    lo_t("y", 0)
                product_done("brb", t)
                gbt = gb[:, t, :].rearrange("p (b c) -> p b c", b=2)
                V.tensor_tensor(gbt, pair(UNITS["brb"] + t), gbt, ALU.mult).then_inc(acc_out, 1)
                dve.wait_ge(acc_out, UNITS["brb"] + t + 1)
                V.tensor_tensor(xn[:, t, :], ga[:, t, :], gb[:, t, :], ALU.add).then_inc(oa_ready, 1)
            for j in range(1, 4):
                lo_t("y", j)
            for j in range(4):
                adv(SUBS["wo2"] + 4 + j)
            rms(1, "rms1", "wo2")
            n, un, g = SUBS["up"], UNITS["up"], GROUPS["up"]
            k_hi = hcount[0]

            def ulow(c, i=0):
                k0 = 4 * c + 8 * i
                d, h = (uL[:, k0:k0 + 4, :], uH[:, k0:k0 + 4, :]) if isinstance(i, int) else \
                       (uL[:, bass.ds(k0, 4), :], uH[:, bass.ds(k0, 4), :])
                dve.wait_ge(h_hi, HIDDEN["up"] + c + 2 * i)
                V.tensor_tensor(d, hu[:, c % 2, :, :].rearrange("p t (k s) -> p (t k) s", s=S), h.bitcast(fp32),
                                ALU.subtract).then_inc(h_lo, 1)

            def up(c, i=0):
                for j in range(3):
                    adv(n + 4 * c + 4 + j, i)
                dve.wait_ge(w_used, summed("up", c) + 8 * i)
                if c >= 3:
                    dve.wait_ge(h_lo, HIDDEN["up"] + c - 2 + 2 * i)
                elif not isinstance(i, int):
                    dve.wait_ge(h_lo, HIDDEN["up"] + 2 * i)
                V.tensor_scalar(hu[:, c % 2, :, :], pair(un + c), 0.0, None, ALU.max).then_inc(acc_out, 1)
                adv(n + 4 * c + 7, i)

            up(0)
            up(1)
            for j in range(2):
                lo(g + j, uL[:, 2 * j:2 * j + 2, :], uH[:, 2 * j:2 * j + 2, :], k_hi=k_hi + j)
            with dve.Fori(0, 3) as i:
                up(2, i)
                ulow(1, i)
                up(3, i)
                ulow(2, i)
            ulow(7)
            hcount[0] += 2
            for k in range(F2 // P - 4):
                adv(SUBS["down"] + 4 + k)
            rms(2, "rms2", "down")
            for j in range(4):
                adv(SUBS["pg"] + 4 + j)
            lo(GROUPS["p"], pL[:, :, :], pH[:, :, :], k_hi=hcount[0])
            for j in range(4, 8):
                adv(SUBS["pg"] + 4 + j)
            for t in range(TT):
                product_done("ple", t)
                dve.wait_ge(acc_out, UNITS["pg"] + t + 1)
                gt = gate[:, t, :].rearrange("p (b c) -> p b c", b=2)
                link(V.tensor_tensor(gt, pair(UNITS["ple"] + t), gt, ALU.mult))
                V.tensor_tensor(x[:, t, :], x[:, t, :], gate[:, t, :], ALU.add).then_inc(x_done, 1)

        @block.tensor
        def _(pe):
            T = nc.tensor

            def sub_ready(n, i=0):
                pe.wait_ge(w_lo, n + 1 + 8 * i)

            def three(outp, xh, xl, h, l, first, last_):
                T.matmul(outp, xh, h, start=first, stop=False)
                T.matmul(outp, xh, l, start=False, stop=False)
                return T.matmul(outp, xl, h, start=False, stop=last_)

            def chunk_mm(n, i, units, acts, t_need=None, after_sub=None):
                for s in range(4):
                    sub_ready(n + s, i)
                    if t_need is not None:
                        pe.wait_ge(t_lo, t_need + s + 1)
                    for un, (xh, xl) in zip(units, acts):
                        if s == 0:
                            at_least(pe, acc_out, un - 1 + 2 * i)
                        for kk in range(2):
                            k = 2 * s + kk
                            h = wH[:, (n + s) % WS, kk * CW:(kk + 1) * CW]
                            l = wL[:, (n + s) % WS, kk * CW:(kk + 1) * CW]
                            for t in range(TT):
                                ins = three(pair(un)[:, t, :], xh[:, k, t * P:(t + 1) * P], xl[:, k, t * P:(t + 1) * P],
                                            h, l, k == 0, k == KT - 1)
                    ins.then_inc(w_used, 1)
                    if after_sub is not None:
                        after_sub(s)

            def chunk_mm_T(n, i, un, x_h, x_l):
                for s in range(4):
                    sub_ready(n + s, i)
                    if s == 0:
                        at_least(pe, acc_out, un - 1 + 2 * i)
                    for kk in range(2):
                        k = 2 * s + kk
                        for b in range(4):
                            dst = pair(un)[:, b // 2, (b % 2) * S:(b % 2) * S + S]
                            c0 = kk * CW + b * P
                            h, l = wH[:, (n + s) % WS, c0:c0 + P], wL[:, (n + s) % WS, c0:c0 + P]
                            T.matmul(dst, h, x_h[:, k, :], start=k == 0 and b % 2 == 0, stop=False, skip_group_check=True)
                            T.matmul(dst, h, x_l[:, k, :], start=False, stop=False, skip_group_check=True)
                            ins = T.matmul(dst, l, x_h[:, k, :], start=False, stop=k == KT - 1, skip_group_check=True)
                    ins.then_inc(w_used, 1)

            def hidden_ready(name, k):
                per = 4 if name == "up" else 2
                if k < per:
                    pe.wait_ge(t_lo, GROUPS[name] + k // 2 + 1)
                else:
                    pe.wait_ge(h_lo, HIDDEN[name] + k // per)

            def rows_mm(n, un, xh, xl, kn, t_need=None, after_sub=None, tiled=True, between=None,
                        hidden=None, late=None, early=None):
                def part(k, t):
                    if k == 0:
                        at_least(pe, acc_out, un + t - 1)
                    for b in range(2):
                        ins = three(pair(un + t)[:, b, :], xh[:, k, t * P:(t + 1) * P], xl[:, k, t * P:(t + 1) * P],
                                    wH[:, (n + k) % WS, b * CW:(b + 1) * CW], wL[:, (n + k) % WS, b * CW:(b + 1) * CW],
                                    k == 0, k == kn - 1)
                    return ins

                single = 0 if tiled and kn <= KT else kn - 4 if tiled else kn
                for k in range(single):
                    sub_ready(n + k)
                    if hidden is not None:
                        hidden_ready(hidden, k)
                    elif t_need is not None and k % 2 == 0:
                        pe.wait_ge(t_lo, t_need + k // 2 + 1)
                    for t in range(TT):
                        ins = part(k, t)
                    ins.then_inc(w_used, 1)
                    if after_sub is not None:
                        after_sub(k)
                for k0 in range(single, kn, 4):
                    for t in range(TT):
                        for k in range(k0, min(k0 + 4, kn)):
                            if t == 0:
                                sub_ready(n + k)
                            if t_need is not None and k % 4 == 0 and kn == KT:
                                pe.wait_ge(t_lo, t_need + 2 * t + k // 4 + 1)
                            elif hidden is not None:
                                hidden_ready(hidden, k)
                            elif t_need is not None:
                                pe.wait_ge(t_lo, t_need + 1)
                            if early is not None and (k, t) == (kn - 1, 1):
                                early()
                            ins = part(k, t)
                            if t == 1:
                                ins.then_inc(w_used, 1)
                            elif k == kn - 1:
                                ins.then_inc(tile0_done, 1)
                            if between is not None and (k, t) == (1, 0):
                                between()
                            if late is not None and (k, t) == (5, 0):
                                late()

            def first_mm(n, un, name, between):
                for t in range(TT):
                    for s in range(4):
                        if t == 0:
                            sub_ready(n + s)
                            if s == 0:
                                at_least(pe, acc_out, un - 1)
                        if s % 2 == 0:
                            pe.wait_ge(t_lo, GROUPS[name] + 2 * t + s // 2 + 1)
                        for kk in range(2):
                            k = 2 * s + kk
                            ins = three(pair(un)[:, t, :], aH[:, k, t * P:(t + 1) * P], aL[:, k, t * P:(t + 1) * P],
                                        wH[:, (n + s) % WS, kk * CW:(kk + 1) * CW], wL[:, (n + s) % WS, kk * CW:(kk + 1) * CW],
                                        k == 0, k == KT - 1)
                        if t == 1:
                            ins.then_inc(w_used, 1)
                        elif s == 1:
                            between()

            def group(g, blocks, i=0, step=2):
                at_least(pe, t_lo, g - 1 + step * i if g >= 2 or not isinstance(i, int) else 0)
                for j, b in enumerate(blocks):
                    ins = T.transpose(tbank(g)[:, j * P:(j + 1) * P], b, ident)
                ins.then_inc(t_done, 1)

            def groups(name, src):
                for j in range(4):
                    group(GROUPS[name] + j, [src[:, t, (2 * j + k) * P:(2 * j + k + 1) * P] for k in range(2) for t in range(TT)])

            def tile_groups(name, src, t):
                for j in range(2):
                    group(GROUPS[name] + 2 * t + j, [src[:, t, (4 * j + k) * P:(4 * j + k + 1) * P] for k in range(4)])

            def tile_ready(name, src, cond, value, t=1):
                def go():
                    pe.wait_ge(cond, value)
                    tile_groups(name, src, t)
                return go

            def keep_warm(count):
                for _ in range(count):
                    T.transpose(ps[:, 7, 0:P], ident, ident)

            def mod_mm(c):
                bank = c if c < NMOD0 else 7
                if c > NMOD0:
                    pe.wait_ge(mod_out, c)
                for h in range(2):
                    if c < NMOD0:
                        if h == 0:
                            pe.wait_ge(mod0_in[c], 16)
                        src = mod0[:, 2 * c + h, :]
                    else:
                        pe.wait_ge(mod_in[h], 16 * (c - NMOD0 + 1))
                        src = modraw[:, h, :]
                    for j in range(4):
                        ins = T.matmul(ps[32 * j:32 * j + 32, bank, :], cT[:, 4 * h + j, :], src[:, j * CW:(j + 1) * CW],
                                       start=h == 0, stop=h == 1)
                    if c >= NMOD0:
                        ins.then_inc(mod_used, 1)
                if c < NMOD0:
                    ins.then_inc(mod_acc, 1)

            def mod_select(c):
                layer, m = MODS[c]
                pe.wait_ge(mod_row, c + 1)
                if c and c <= NMOD0:
                    pe.wait_ge(mod_out, c)
                if mod_is_column(layer, m):
                    for k in range(4):
                        ins = T.matmul(ps[:, 7, 2 * k:2 * k + 2], modrow[:, k * P:(k + 1) * P],
                                       cst[:, C_SELC:C_SELC + 2], start=True, stop=True)
                else:
                    ins = T.matmul(ps[:, 7, :], cst[:, C_SELB:C_SELB + P], modrow[:, :], start=True, stop=True)
                ins.then_inc(mod_sel, 1)

            pe.wait_ge(cst_in, 16)
            pe.wait_ge(rows_in, 64)
            T.transpose(ps[:, 6, 0:113], rows[:, :], ident[0:113, 0:113]).then_inc(rows_T, 1)
            pe.wait_ge(cT_ready, 2)
            for c in range(NMOD0):
                mod_mm(c)
                if c:
                    mod_select(c - 1)
            mod_select(NMOD0 - 1)
            pe.wait_ge(x_in, 16)
            groups("x", x)

            modc = [NMOD0]

            def mod_at(c, sub):
                for kind, m in MODPLAN.get((c, sub), ()):
                    (mod_mm if kind == "sum" else mod_select)(m)
                    modc[0] = m + 1

            n = SUBS["qkv"]
            X, C = (aH, aL), (cH, cL)

            def heads(unit):
                pe.wait_ge(acc_out, UNITS["q"] + unit + 1)
                g = GROUPS["q"] + 2 * unit
                for j in range(2):
                    group(g + j, [ro[:, unit % 2, t, (2 * j + k) * P:(2 * j + k + 1) * P]
                                  for k in range(2) for t in range(TT)])

            for c in range(6):
                def beside(sub, c=c):
                    mod_at(c, sub)

                if c < 2:
                    chunk_mm(n + 4 * c, 0, [UNITS["q"] + c], [X], GROUPS["x"] if c == 0 else None, beside)
                else:
                    un = UNITS["k"] + 2 * (c - 2)
                    chunk_mm(n + 4 * c, 0, [un, un + 1], [C, X], None, beside)
                if c == 0:
                    pe.wait_ge(ctx_in, 16)
                    groups("ctx", lnp)
                elif c == 1:
                    pe.wait_ge(t_lo, GROUPS["ctx"] + 4)
                    heads(0)
                elif c == 2:
                    heads(1)
                elif c < 5:
                    heads(2 * c - 4)
                    heads(2 * c - 3)

            def scores(r):
                h, t = r // 2, r % 2
                un = UNITS["att"] + r
                if r >= 2:
                    pe.wait_ge(s_exp, r - 1)
                else:
                    pe.wait_ge(acc_out, un - 1)
                for m in range(2):
                    ins = T.matmul(pair(un)[:, m, :], qz[:, h, m, t * P:(t + 1) * P], kT[:, h, :], start=True, stop=True)
                ins.then_inc(acc_done, 1)

            def values(r):
                h = r // 2
                pe.wait_ge(t_lo, GROUPS["att"] + r + 1)
                if r >= 1:
                    pe.wait_ge(o_out, r)
                for k in range(4):
                    ins = T.matmul(ps[:, 6, 0:P], at[:, r % 2, k, :],
                                   v[:, k, h * P:(h + 1) * P], start=k == 0, stop=k == 3)
                ins.then_inc(o_done, 1)

            pe.wait_ge(t_lo, GROUPS["k"] + 8)
            scores(0)
            scores(1)
            mod_mm(modc[0])
            for r in range(16):
                if r < 14:
                    scores(r + 2)
                if mod_sum_in(r - 1):
                    mod_select(modc[0])
                    modc[0] += 1
                pe.wait_ge(acc_out, UNITS["att"] + r + 1)
                group(GROUPS["att"] + r, [am[:, r % 2, k * P:(k + 1) * P] for k in range(4)])
                if r >= 1:
                    values(r - 1)
                if mod_sum_in(r):
                    mod_mm(modc[0])
            values(15)
            pe.wait_ge(rows2_in, 192)
            pe.wait_ge(o_out, 16)
            T.transpose(ps[:, 6, 0:82], rows2[:, :], ident[0:82, 0:82]).then_inc(rows2_T, 1)
            pe.wait_ge(o_norm, 1)
            tile_groups("o", ot, 0)
            rows_mm(SUBS["wo"], UNITS["wo"], aH, aL, KT, GROUPS["o"], between=tile_ready("o", ot, o_norm, 2))
            pe.wait_ge(ln_hat, 1)
            tile_groups("x1", x, 0)
            pe.wait_ge(mod_out, 16)
            keep_warm(12)

            def swiglu(layer, name):
                n, un, g = SUBS[f"in{layer}"], UNITS[f"in{layer}"], GROUPS[f"in{layer}"]

                first_mm(n, un, name, tile_ready(name, x, ln_hat, 4 * layer + 2))
                chunk_mm_T(n + 4, 0, un + 1, aH, aL)
                pe.wait_ge(acc_out, un + 1)
                group(g, [hid[:, 0, t, k * P:(k + 1) * P] for k in range(2) for t in range(TT)])
                with pe.Fori(0, 4) as i:
                    chunk_mm_T(n + 8, i, un + 2, aH, aL)
                    chunk_mm_T(n + 12, i, un + 3, aH, aL)
                chunk_mm_T(n + 40, 0, un + 10, aH, aL)

                def beside(k):
                    if layer == 0 and k < 16:
                        if k % 2 == 0:
                            mod_mm(modc[0])
                        else:
                            mod_select(modc[0])
                            modc[0] += 1

                rows_mm(SUBS[f"out{layer}"], UNITS[f"out{layer}"], hH, hL, F1 // P, None, beside,
                        hidden=f"in{layer}")

            swiglu(0, "x1")
            pe.wait_ge(mod_out, len(MODS))
            keep_warm(30)
            pe.wait_ge(pool_in, 16)
            pe.wait_ge(pool_h, 2)
            for j in range(4):
                g = GROUPS["pool"] + j
                at_least(pe, t_lo, g - 1)
                for k in range(2):
                    for t in range(TT):
                        ins = T.matmul(tbank(g)[:, k * S:(k + 1) * S], hm[:, t, (2 * j + k) * P:(2 * j + k + 1) * P],
                                       poolm[:, t, j, :], start=t == 0, stop=t == TT - 1)
                ins.then_inc(t_done, 1)
            n, un = SUBS["pool"], UNITS["pool"]
            for t in range(TT):
                for s in range(2):
                    if t == 0:
                        sub_ready(n + s)
                    for gg in range(2):
                        gr = 2 * s + gg
                        pe.wait_ge(t_lo, GROUPS["pool"] + gr + 1)
                        if gr == 0:
                            pe.wait_ge(acc_out, un + t - 1)
                        for k in range(2):
                            w0 = (2 * gg + k) * 256
                            ins = three(pair(un + t)[:, gr // 2, (gr % 2) * 256:(gr % 2) * 256 + 256],
                                        aH[:, 2 * gr + k, t * P:(t + 1) * P], aL[:, 2 * gr + k, t * P:(t + 1) * P],
                                        wH[:, (n + s) % WS, w0:w0 + 256], wL[:, (n + s) % WS, w0:w0 + 256],
                                        k == 0, k == 1)
                    if t == 1:
                        ins.then_inc(w_used, 1)
                if t == 0:
                    ins.then_inc(tile0_done, 1)
            keep_warm(12)
            pe.wait_ge(ln_hat, 2 * TT + 1)
            tile_groups("x3", x, 0)
            keep_warm(11)
            swiglu(1, "x3")

            keep_warm(4)
            pe.wait_ge(ln_hat, 3 * TT + 1)
            tile_groups("rms0", x, 0)
            keep_warm(12)
            n, un = SUBS["win"], UNITS["win"]
            def behind(c):
                if c == 0:
                    pe.wait_ge(lr_lo, 1)
                    for t in range(TT):
                        for k in range(KT):
                            ins = three(ps[:, 6, t * GRANK:(t + 1) * GRANK], aH[:, k, t * P:(t + 1) * P],
                                        aL[:, k, t * P:(t + 1) * P], lrH[:, k, :], lrL[:, k, :], k == 0, k == KT - 1)
                    ins.then_inc(lr_done, 1)
                elif c == 1:
                    pe.wait_ge(lr_t, 1)
                    for t in range(TT):
                        ins = T.transpose(ps[0:GRANK, 6, t * P:(t + 1) * P], lrt[:, t, :], ident)
                    ins.then_inc(lr_T, 1)
                elif c == 2:
                    pe.wait_ge(lr_Tc, 1)
                    pe.wait_ge(vec_in, 32)
                    for t in range(TT):
                        ins = T.matmul(side(0)[:, t, :], lrT[:, t * P:(t + 1) * P], w2[:, :], start=True, stop=True)
                    ins.then_inc(z_done, 1)
                elif c == 4:
                    pe.wait_ge(la_ready, 1)
                    for j, tab in enumerate((C_TRI, C_TRS)):
                        for t in range(TT):
                            ins = T.matmul(side(1 - j)[:, t, :], cst[:, tab:tab + P], la[:, t, :], start=True, stop=True)
                        ins.then_inc(cum_done, 1)
                elif c == 5:
                    pe.wait_ge(e_ready, 3)
                    for h in range(GH):
                        for t in range(TT):
                            ins = T.matmul(ps[:, 6, 4 * h + 2 * t:4 * h + 2 * t + 2], la[:, t, h * GDK:(h + 1) * GDK],
                                           cst[:, C_IND:C_IND + 2], start=True, stop=True)
                    ins.then_inc(dec_sum, 1)
                elif c == 6:
                    pe.wait_ge(g_mul, 2)
                    pe.wait_ge(dec_exp, 1)
                    for j, src in enumerate((u[:, :, 0:512], ekd[:, :, :])):
                        for h in range(GH):
                            for t in range(TT):
                                ins = T.transpose(side(1 - j)[:, h // 2, (h % 2) * S + t * P:(h % 2) * S + (t + 1) * P],
                                                  src[:, t, h * GDK:(h + 1) * GDK], ident)
                        ins.then_inc(gT_done, 1)
                if c == 7:
                    pe.wait_ge(gT_out, 2)
                    for t in range(TT):
                        g = GROUPS["glaA"] + t
                        for h in range(GH):
                            ins = T.matmul(tbank(g)[:, h * P:(h + 1) * P], qkT[:, 1, h, t * P:(t + 1) * P],
                                           qkT[:, 0, h, t * P:(t + 1) * P], start=True, stop=True)
                        ins.then_inc(t_done, 1)
                if c in (7, 8, 9):
                    k = c - 7
                    t, r0 = k // 2, GCH * (k % 2)
                    if k == 0:
                        pe.wait_ge(g_mul, 3)
                    else:
                        pe.wait_ge(kv_out, k)
                    for h in range(GH):
                        ins = T.matmul(ps[:, 6 + h // 2, (h % 2) * GDV:(h % 2) * GDV + GDV],
                                       ekl[r0:r0 + GCH, t, h * GDK:(h + 1) * GDK],
                                       u[r0:r0 + GCH, t, 1024 + h * GDV:1024 + (h + 1) * GDV], start=True, stop=True)
                    ins.then_inc(kv_done, 1)
                elif c in (10, 11):
                    t = c - 10
                    pe.wait_ge(kv_out, 3)
                    pe.wait_ge(t_lo, GROUPS["glaA"] + t + 1)
                    if t == 1:
                        pe.wait_ge(a_evac, TT)
                    for h in range(GH):
                        dst = side(t)[:, h // 2, (h % 2) * GDV:(h % 2) * GDV + GDV]
                        ins = T.matmul(dst, aT[:, t, h, :], u[:, t, 1024 + h * GDV:1024 + (h + 1) * GDV],
                                       start=True, stop=True, skip_group_check=True)
                        for half in range(2):
                            k = 2 * t + half
                            if k == 0:
                                continue
                            ins = T.matmul(dst[GCH * half:GCH * half + GCH, :], qkT[:, 0, h, k * GCH:(k + 1) * GCH],
                                           st[:, k - 1, h, :], start=False, stop=True, skip_group_check=True)
                    ins.then_inc(go_done, 1)
                elif c >= 12:
                    if c == 12:
                        pe.wait_ge(m_norm, TT)
                        pe.wait_ge(go_evac, TT)
                    for j in (2 * (c - 12), 2 * (c - 12) + 1):
                        group(GROUPS["mqk"] + j, [u[:, t, 3072 + (2 * j + k) * P:3072 + (2 * j + k + 1) * P]
                                                  for k in range(2) for t in range(TT)])

            first_mm(n, un, "rms0", tile_ready("rms0", x, ln_hat, 4 * TT))
            behind(0)
            for c in range(1, 16):
                chunk_mm(n + 4 * c, 0, [un + c], [X])
                behind(c)

            def mscores(h):
                pe.wait_ge(t_lo, GROUPS["mqk"] + 5 + h // 2)
                if h >= 2:
                    pe.wait_ge(m_max, h - 1)
                for t in range(TT):
                    ins = T.matmul(ps[:, 6 + h % 2, t * S:(t + 1) * S], mT[:, h, t * P:(t + 1) * P], mT[:, 8 + h, :],
                                   start=True, stop=True)
                ins.then_inc(m_scores, 1)

            def mtranspose(h):
                pe.wait_ge(m_exp, h + 1)
                if h == 0:
                    pe.wait_ge(t_lo, GROUPS["oa"] + 4)
                else:
                    pe.wait_ge(m_Tc, h)
                for j, (t, k) in enumerate(((0, 0), (1, 0), (1, 1))):
                    ins = T.transpose(ps[:, 4, j * P:(j + 1) * P], pe_[:, h % 2, t, k * P:(k + 1) * P], ident)
                ins.then_inc(m_T, 1)

            def mvalues(h):
                pe.wait_ge(m_Tc, h + 1)
                if h >= 1:
                    pe.wait_ge(m_oout, h)
                vh = [u[:, k, 5120 + h * P:5120 + (h + 1) * P] for k in range(2)]
                T.matmul(ps[:, 5, 0:P], pT[:, h % 2, 0:P], vh[0], start=True, stop=True)
                T.matmul(ps[:, 5, P:S], pT[:, h % 2, P:S], vh[0], start=True, stop=False)
                T.matmul(ps[:, 5, P:S], pT[:, h % 2, S:S + P], vh[1], start=False, stop=True).then_inc(m_o, 1)

            def moba(h):
                mtranspose(h)
                if h >= 1:
                    mvalues(h - 1)
                if h + 2 < H:
                    mscores(h + 2)

            mscores(0)
            mscores(1)
            pe.wait_ge(oa_ready, 1)
            groups("oa", xn)
            rows_mm(SUBS["bra"], UNITS["bra"], aH, aL, KT, GROUPS["oa"], moba, tiled=False)
            keep_warm(9)
            mvalues(H - 1)
            keep_warm(3)
            pe.wait_ge(m_oout, H)
            tile_groups("ob", xn, 0)
            rows_mm(SUBS["brb"], UNITS["brb"], aH, aL, KT, GROUPS["ob"], between=tile_ready("ob", xn, m_oout, H),
                    early=tile_ready("y", xn, oa_ready, 2, 0))
            rows_mm(SUBS["wo2"], UNITS["wo2"], aH, aL, KT, GROUPS["y"], between=tile_ready("y", xn, oa_ready, 3),
                    early=tile_ready("rms1", xn, xn_ready, TT + 1, 0))
            n, un, g = SUBS["up"], UNITS["up"], GROUPS["up"]

            first_mm(n, un, "rms1", tile_ready("rms1", xn, xn_ready, 2 * TT))
            chunk_mm_T(n + 4, 0, un + 1, aH, aL)
            pe.wait_ge(silu_done, 23)
            for j in range(2):
                group(g + j, [hu[:, 0, t, (2 * j + k) * P:(2 * j + k + 1) * P] for k in range(2) for t in range(TT)])
            with pe.Fori(0, 3) as i:
                chunk_mm_T(n + 8, i, un + 2, aH, aL)
                chunk_mm_T(n + 12, i, un + 3, aH, aL)
            rows_mm(SUBS["down"], UNITS["down"], uH, uL, F2 // P, hidden="up",
                    early=tile_ready("rms2", xn, xn_ready, 2 * TT + 1, 0))

            def p_group():
                pe.wait_ge(p_in, 16)
                group(GROUPS["p"], [pt[:, t, k * P:(k + 1) * P] for k in range(2) for t in range(TT)])

            rows_mm(SUBS["pg"], UNITS["pg"], aH, aL, KT, GROUPS["rms2"], between=tile_ready("rms2", xn, xn_ready, 3 * TT),
                    late=p_group)
            rows_mm(SUBS["ple"], UNITS["ple"], pH, pL, 2, GROUPS["p"])


_INS = ["x", "c", "ctx", "c_ctx", "w_mod", "b_mod", "ln_g", "ln_b", "attn_w_qkv", "attn_lambda", "attn_subln_g",
        "attn_w_o", "pool_w", "pool_scale", "ffn_w_in", "ffn_w_out", "p_2", "norm_mix_2", "w_in_2", "gla_gate_w2_2",
        "gla_gate_b_2", "gla_out_norm_2", "moba_q_norm_2", "moba_k_norm_2", "w_branch_a_2", "w_branch_b_2",
        "w_out_2", "norm_mlp_2", "w_up_2", "w_down_2", "norm_ple_2", "w_ple_gate_2", "w_ple_2"]


def kernel(**inputs):
    import concourse.bacc as bacc
    from concourse.bass_utils import run_bass_kernel_spmd

    nc = bacc.Bacc("TRN2", target_bir_lowering=False, num_devices=1)
    arrays, aps = {}, {}
    for name in _INS:
        arr = np.ascontiguousarray(inputs[name])
        arrays[f"in_{name}"] = arr
        aps[name] = nc.dram_tensor(f"in_{name}", arr.shape, mybir.dt.from_np(arr.dtype), kind="ExternalInput").ap()
    consts = []
    for name, arr in zip(("const_tables", "const_windows"), shape_constants()):
        arrays[name] = arr
        consts.append(nc.dram_tensor(name, arr.shape, fp32, kind="ExternalInput").ap())
    out = nc.dram_tensor("out", (1, S, D), fp32, kind="ExternalOutput").ap()
    build(nc, aps, consts[0], consts[1], out)
    r = run_bass_kernel_spmd(nc, [arrays], core_ids=[0])
    return r.results[0]["out"]
```
